# Optimizing a Trainium2 kernel written in Bass

```python
import jax
import jax.numpy as jnp
from jax import lax
import numpy as np

D_MODEL = 1024
BATCH = 1
SEQ = 128
DEPTH = 1
DEC_BATCH = 1
DEC_SEQ = 512
PAST_LEN = 128

GRID_W = 64
HEAD_DIM = 64
N_HEADS_A = D_MODEL // 2 // HEAD_DIM
N_KV_A = N_HEADS_A // 4
N_HEADS_B = D_MODEL // 2 // HEAD_DIM
N_KV_B = N_HEADS_B // 4
Q_A_W = N_HEADS_A * HEAD_DIM
KV_A_W = N_KV_A * HEAD_DIM
Q_B_W = N_HEADS_B * HEAD_DIM
KV_B_W = N_KV_B * HEAD_DIM
IN_W = Q_A_W + 2 * KV_A_W + Q_B_W + 2 * KV_B_W
MIX_W = Q_A_W + Q_B_W
BLOCK = 128
WINDOW = 128
ROPE_THETA = 10000.0
N_EXPERTS = 16
CAPACITY_FACTOR = 2
D_FF_EXPERT = D_MODEL
N_MOD = 6
EPS = 1e-6
NEG_INF = -1e30

kernel_name = 'hybrid_dit_prefix_gqa_swa_ec_moe_step'

def rms_norm(x, g):
    xf = x.astype(jnp.float32)
    y = xf * lax.rsqrt(jnp.mean(xf * xf, axis=-1, keepdims=True) + EPS)
    return y.astype(x.dtype) * g

def _rope_1d(x, pos):
    half = x.shape[-1] // 2
    freqs = ROPE_THETA ** (-jnp.arange(half, dtype=jnp.float32) / half)
    ang = pos[:, None] * freqs[None, :]
    cos = jnp.cos(ang)[:, None, :].astype(x.dtype)
    sin = jnp.sin(ang)[:, None, :].astype(x.dtype)
    x1, x2 = x[..., :half], x[..., half:]
    return jnp.concatenate([x1 * cos - x2 * sin, x2 * cos + x1 * sin], axis=-1)

def rope_2d(x, rows, cols):
    half = x.shape[-1] // 2
    return jnp.concatenate([_rope_1d(x[..., :half], rows), _rope_1d(x[..., half:], cols)], axis=-1)

def grid_positions(n_tokens):
    rows_n = n_tokens // GRID_W
    rows = jnp.repeat(jnp.arange(rows_n, dtype=jnp.float32), GRID_W)
    cols = jnp.tile(jnp.arange(GRID_W, dtype=jnp.float32), rows_n)
    return rows, cols

def softmax_with_sink(s, sink):
    m = jnp.maximum(jnp.max(s, axis=-1, keepdims=True), sink)
    e = jnp.exp(s - m)
    return e / (jnp.sum(e, axis=-1, keepdims=True) + jnp.exp(sink - m))

def modulation(cond, w_ada, b_ada):
    m = jnp.einsum('btd,dk->btk', jax.nn.silu(cond), w_ada) + b_ada
    return jnp.split(m, N_MOD, axis=-1)

def modulate(x, g, shift, scale):
    return rms_norm(x, g) * (1.0 + scale) + shift

def attn_projections(h, w_in, g_qa, g_ka):
    B, T, _ = h.shape
    p = jnp.einsum('btd,dk->btk', h, w_in)
    c1 = Q_A_W
    c2 = c1 + KV_A_W
    c3 = c2 + KV_A_W
    c4 = c3 + Q_B_W
    c5 = c4 + KV_B_W
    qa, ka, va, qb, kb, vb = jnp.split(p, [c1, c2, c3, c4, c5], axis=-1)
    heads = lambda t: t.reshape(B, T, -1, HEAD_DIM)
    qa = rms_norm(heads(qa), g_qa)
    ka = rms_norm(heads(ka), g_ka)
    return qa, ka, heads(va), heads(qb), heads(kb), heads(vb)

def blocked_gqa(q, k, v, sink=None):
    B, T, H, d = q.shape
    KV = k.shape[2]
    G = H // KV
    nb = T // BLOCK
    scale = d ** -0.5
    qb = q.reshape(B, nb, BLOCK, KV, G, d).transpose(1, 0, 2, 3, 4, 5)
    sink_f = None if sink is None else sink.astype(jnp.float32).reshape(1, KV, G, 1, 1)

    def one_block(q_blk):
        s = jnp.einsum('bqkgd,bskd->bkgqs', q_blk, k, preferred_element_type=jnp.float32) * scale
        p = jax.nn.softmax(s, axis=-1) if sink_f is None else softmax_with_sink(s, sink_f)
        return jnp.einsum('bkgqs,bskd->bqkgd', p.astype(v.dtype), v)

    o = lax.map(one_block, qb)
    return o.transpose(1, 0, 2, 3, 4, 5).reshape(B, T, H * d)

def windowed_gqa_with_ctx(q, k, v, k_ctx, v_ctx, sink):
    B, T, H, d = q.shape
    KV = k.shape[2]
    G = H // KV
    P = k_ctx.shape[1]
    nb = T // BLOCK
    scale = d ** -0.5
    pad = ((0, 0), (BLOCK, BLOCK), (0, 0), (0, 0))
    kp = jnp.pad(k, pad).reshape(B, nb + 2, BLOCK, KV, d)
    vp = jnp.pad(v, pad).reshape(B, nb + 2, BLOCK, KV, d)
    kb = jnp.concatenate([kp[:, :nb], kp[:, 1:nb + 1], kp[:, 2:]], axis=2)
    vb = jnp.concatenate([vp[:, :nb], vp[:, 1:nb + 1], vp[:, 2:]], axis=2)
    qb = q.reshape(B, nb, BLOCK, KV, G, d)
    s_loc = jnp.einsum('bnqkgd,bnskd->bnkgqs', qb, kb, preferred_element_type=jnp.float32) * scale
    blk = jnp.arange(nb)[:, None] * BLOCK
    qpos = blk + jnp.arange(BLOCK)[None, :]
    kpos = blk - BLOCK + jnp.arange(3 * BLOCK)[None, :]
    diff = kpos[:, None, :] - qpos[:, :, None]
    valid = (jnp.abs(diff) <= WINDOW) & (kpos[:, None, :] >= 0) & (kpos[:, None, :] < T)
    s_loc = jnp.where(valid[None, :, None, None, :, :], s_loc, NEG_INF)
    s_ctx = jnp.einsum('bnqkgd,bskd->bnkgqs', qb, k_ctx, preferred_element_type=jnp.float32) * scale
    s = jnp.concatenate([s_ctx, s_loc], axis=-1)
    p = softmax_with_sink(s, sink.astype(jnp.float32).reshape(1, 1, KV, G, 1, 1)).astype(v.dtype)
    o = (jnp.einsum('bnkgqs,bskd->bnqkgd', p[..., :P], v_ctx)
         + jnp.einsum('bnkgqs,bnskd->bnqkgd', p[..., P:], vb))
    return o.reshape(B, T, H * d)

def expert_choice_moe(h, w_router, w_gate, w_up, w_down):
    B, T, D = h.shape
    cap = CAPACITY_FACTOR * T // N_EXPERTS
    logits = jnp.einsum('btd,de->bte', h, w_router, preferred_element_type=jnp.float32)
    aff = jax.nn.softmax(logits, axis=-1)
    g, idx = lax.top_k(jnp.swapaxes(aff, 1, 2), cap)
    xg = jax.vmap(lambda hb, ib: hb[ib])(h, idx)
    a = jnp.einsum('becd,edf->becf', xg, w_gate)
    u = jnp.einsum('becd,edf->becf', xg, w_up)
    y = jnp.einsum('becf,efd->becd', jax.nn.silu(a) * u, w_down) * g[..., None].astype(h.dtype)
    return jax.vmap(lambda yb, ib: jnp.zeros((T, D), yb.dtype).at[ib.reshape(-1)].add(yb.reshape(-1, D)))(y, idx)

def ffn_sublayer(x, shift, scale, gate, g_pre_ffn, w_router, w_gate, w_up, w_down, g_post_ffn):
    h = modulate(x, g_pre_ffn, shift, scale)
    return x + gate * rms_norm(expert_choice_moe(h, w_router, w_gate, w_up, w_down), g_post_ffn)

def context_layer(x, c_ctx, w_ada, b_ada, g_pre_attn, w_in, g_qa, g_ka, sink_b, w_out,
                  g_post_attn, g_pre_ffn, w_router, w_gate, w_up, w_down, g_post_ffn):
    sh1, sc1, gt1, sh2, sc2, gt2 = modulation(c_ctx[None, None, :], w_ada, b_ada)
    h = modulate(x, g_pre_attn, sh1, sc1)
    qa, ka, va, qb, kb, vb = attn_projections(h, w_in, g_qa, g_ka)
    oa = blocked_gqa(qa, ka, va)
    ob = blocked_gqa(qb, kb, vb, sink_b)
    o = jnp.einsum('btk,kd->btd', jnp.concatenate([oa, ob], axis=-1), w_out)
    x = x + gt1 * rms_norm(o, g_post_attn)
    x = ffn_sublayer(x, sh2, sc2, gt2, g_pre_ffn, w_router, w_gate, w_up, w_down, g_post_ffn)
    return x, ka, va, kb, vb

def latent_layer(x, c, k_a_ctx, v_a_ctx, k_b_ctx, v_b_ctx, rows, cols, w_ada, b_ada, g_pre_attn,
                 w_in, g_qa, g_ka, sink_b, w_out, g_post_attn, g_pre_ffn, w_router, w_gate,
                 w_up, w_down, g_post_ffn):
    sh1, sc1, gt1, sh2, sc2, gt2 = modulation(c[:, None, :], w_ada, b_ada)
    h = modulate(x, g_pre_attn, sh1, sc1)
    qa, ka, va, qb, kb, vb = attn_projections(h, w_in, g_qa, g_ka)
    qa, ka = rope_2d(qa, rows, cols), rope_2d(ka, rows, cols)
    qb, kb = rope_2d(qb, rows, cols), rope_2d(kb, rows, cols)
    oa = blocked_gqa(qa, jnp.concatenate([k_a_ctx, ka], axis=1), jnp.concatenate([v_a_ctx, va], axis=1))
    ob = windowed_gqa_with_ctx(qb, kb, vb, k_b_ctx, v_b_ctx, sink_b)
    o = jnp.einsum('btk,kd->btd', jnp.concatenate([oa, ob], axis=-1), w_out)
    x = x + gt1 * rms_norm(o, g_post_attn)
    return ffn_sublayer(x, sh2, sc2, gt2, g_pre_ffn, w_router, w_gate, w_up, w_down, g_post_ffn)

def setup_inputs(seed: int = 0) -> dict:
    key = jax.random.key(seed)
    ks = jax.random.split(key, 24)
    f32 = jnp.float32

    def nrm(k, shape, scale=1.0):
        return jax.random.normal(k, shape, f32) * scale

    def gain(k, shape):
        return 1.0 + 0.05 * jax.random.normal(k, shape, f32)

    return {
        'x_prompt': nrm(ks[0], (BATCH, SEQ, D_MODEL)),
        'x_sample': nrm(ks[1], (DEC_BATCH, DEC_SEQ, D_MODEL)),
        'cache_a_k': nrm(ks[2], (DEC_BATCH, DEPTH, PAST_LEN, N_KV_A, HEAD_DIM)),
        'cache_a_v': nrm(ks[3], (DEC_BATCH, DEPTH, PAST_LEN, N_KV_A, HEAD_DIM)),
        'cache_b_k': nrm(ks[4], (DEC_BATCH, DEPTH, PAST_LEN, N_KV_B, HEAD_DIM)),
        'cache_b_v': nrm(ks[5], (DEC_BATCH, DEPTH, PAST_LEN, N_KV_B, HEAD_DIM)),
        'c': nrm(ks[6], (DEC_BATCH, D_MODEL)),
        'c_ctx': nrm(ks[7], (D_MODEL,)),
        'w_ada': nrm(ks[8], (DEPTH, D_MODEL, N_MOD * D_MODEL), 0.5 * D_MODEL ** -0.5),
        'b_ada': nrm(ks[9], (DEPTH, N_MOD * D_MODEL), 0.02),
        'g_pre_attn': gain(ks[10], (DEPTH, D_MODEL)),
        'w_in': nrm(ks[11], (DEPTH, D_MODEL, IN_W), D_MODEL ** -0.5),
        'g_qa': gain(ks[12], (DEPTH, HEAD_DIM)),
        'g_ka': gain(ks[13], (DEPTH, HEAD_DIM)),
        'sink_b': nrm(ks[14], (DEPTH, N_HEADS_B), 0.5),
        'w_out': nrm(ks[15], (DEPTH, MIX_W, D_MODEL), MIX_W ** -0.5),
        'g_post_attn': gain(ks[16], (DEPTH, D_MODEL)),
        'g_pre_ffn': gain(ks[17], (DEPTH, D_MODEL)),
        'w_router': nrm(ks[18], (DEPTH, D_MODEL, N_EXPERTS), D_MODEL ** -0.5),
        'w_gate': nrm(ks[19], (DEPTH, N_EXPERTS, D_MODEL, D_FF_EXPERT), D_MODEL ** -0.5),
        'w_up': nrm(ks[20], (DEPTH, N_EXPERTS, D_MODEL, D_FF_EXPERT), D_MODEL ** -0.5),
        'w_down': nrm(ks[21], (DEPTH, N_EXPERTS, D_FF_EXPERT, D_MODEL), D_FF_EXPERT ** -0.5),
        'g_post_ffn': gain(ks[22], (DEPTH, D_MODEL)),
    }

def reference(x_prompt, x_sample, cache_a_k, cache_a_v, cache_b_k, cache_b_v, c, c_ctx,
              w_ada, b_ada, g_pre_attn, w_in, g_qa, g_ka, sink_b, w_out, g_post_attn,
              g_pre_ffn, w_router, w_gate, w_up, w_down, g_post_ffn):
    rows, cols = grid_positions(x_sample.shape[1])
    y_prompt = x_prompt
    y_sample = x_sample
    ak_list, av_list, bk_list, bv_list = [], [], [], []
    for l in range(DEPTH):
        y_prompt, ka, va, kb, vb = context_layer(
            y_prompt, c_ctx, w_ada[l], b_ada[l], g_pre_attn[l], w_in[l], g_qa[l], g_ka[l],
            sink_b[l], w_out[l], g_post_attn[l], g_pre_ffn[l], w_router[l], w_gate[l],
            w_up[l], w_down[l], g_post_ffn[l])
        ak_list.append(ka)
        av_list.append(va)
        bk_list.append(kb)
        bv_list.append(vb)
        y_sample = latent_layer(
            y_sample, c, cache_a_k[:, l], cache_a_v[:, l], cache_b_k[:, l], cache_b_v[:, l],
            rows, cols, w_ada[l], b_ada[l], g_pre_attn[l], w_in[l], g_qa[l], g_ka[l],
            sink_b[l], w_out[l], g_post_attn[l], g_pre_ffn[l], w_router[l], w_gate[l],
            w_up[l], w_down[l], g_post_ffn[l])
    new_a_k = jnp.stack(ak_list, axis=1)
    new_a_v = jnp.stack(av_list, axis=1)
    new_b_k = jnp.stack(bk_list, axis=1)
    new_b_v = jnp.stack(bv_list, axis=1)
    return (y_prompt, y_sample, new_a_k, new_a_v, new_b_k, new_b_v)


_drawn_inputs = setup_inputs


def setup_inputs(seed=0):
    import zlib

    import numpy as np

    out = dict(_drawn_inputs(seed))
    spreads = {}
    factors = {'g_qa': 3.173, 'sink_b': 8.0, 'g_post_ffn': 4.092}
    for name, (base, spread) in spreads.items():
        noise = np.random.default_rng([zlib.crc32(name.encode()), seed]).standard_normal(out[name].shape)
        drawn = base * np.exp(spread * noise) if base else spread * noise
        out[name] = jnp.asarray(drawn.astype(out[name].dtype))
    for name, factor in factors.items():
        out[name] = (out[name] * factor).astype(out[name].dtype)
    return out
```

```python
from contextlib import ExitStack

import numpy as np

import concourse.bass as bass
from concourse import mybir

F32 = mybir.dt.float32
I32 = mybir.dt.int32
U32 = mybir.dt.uint32
ALU = mybir.AluOpType
ACT = mybir.ActivationFunctionType
AX = mybir.AxisListType

P = 128
D = 1024
KC = D // P
CTX = 128
LAT = 512
TILES = (CTX + LAT) // P
LT = LAT // P
TOK = CTX + LAT
DH = 64
HEADS = 8
PAIRS = HEADS // 2
E = 16
CAP_L = 2 * LAT // E
CAP_C = 2 * CTX // E
CPAD = 32
HALF = D // 2
QUART = D // 4
N_MOD = 6
EPS = 1e-6
SLOTS = 6
UNIT = 4096
NEG = -1e30
CTX_ROWS = 4 * CTX + 4 * (CPAD - CAP_C)

UNITS = ([("ada", m, h) for m in (0, 1) for h in (0, 1)] + [("win", s, 0) for s in range(3)]
         + [("ada", m, h) for m in (2, 3, 4, 5) for h in (0, 1)] + [("wout", 0, h) for h in (0, 1)])
FIRST_SLOT = SLOTS - len(UNITS) % SLOTS
MODS = (0, 1, 2, 3, 4, 5)
COLS = {0: 0, 1: 1, 3: 2, 4: 3}
HEAD_UNITS = [(g, h, t) for g in (0, 1) for t in range(TILES) for h in range(HEADS)]


def slot_of(u):
    return (u + FIRST_SLOT) % SLOTS


def key_parts(g, t):
    if t == 0:
        return [(0, TOK, CTX)]
    if g == 0:
        return [(0, 0, 512), (512, 512, TOK - 512)]
    lo, hi = max(0, t - 2), min(LT - 1, t)
    return [(0, 0, CTX), (CTX, CTX + lo * P, (hi + 1 - lo) * P)]


def key_count(g, t):
    return sum(n for _, _, n in key_parts(g, t))


def value_blocks(g, t):
    if t == 0:
        return [4]
    if g == 0:
        return [-1, 0, 1, 2, 3]
    return [-1] + list(range(max(0, t - 2), min(LT - 1, t) + 1))


def build(nc, A, out):
    ctx = ExitStack()
    with ctx:
        def sb(name, n, dt=F32):
            return ctx.enter_context(nc.sbuf_tensor(name, [P, n], dt))

        def sem(name):
            return ctx.enter_context(nc.semaphore(name))

        def dram(name, shape):
            return nc.dram_tensor(name, shape, F32, kind="Internal").ap()

        ring = sb("ring", SLOTS * UNIT)
        reg1 = sb("reg1", KC * TOK)
        reg2 = sb("reg2", KC * TOK)
        reg3 = sb("reg3", KC * TOK)
        qt = sb("qt", 2 * PAIRS * TOK)
        kt = sb("kt", 2 * 2 * (TOK + CTX))
        v_lat = sb("v_lat", LT * 256)
        kv_ctx = sb("kv_ctx", 512)
        cache = sb("cache", 4 * P)
        ident = sb("ident", P)
        mod = sb("mod", N_MOD * QUART)
        gpost = sb("gpost", 2 * QUART)
        gpre = sb("gpre", 2 * KC)
        colmod = sb("colmod", 4 * 2 * KC)
        wr = sb("wr", KC * E)
        cvec = sb("cvec", 2 * KC)
        gqk = sb("gqk", 2 * DH)
        sink = sb("sink", HEADS)
        nsink = sb("nsink", HEADS)
        small = sb("small", 160)
        mhalf = sb("mhalf", 16)
        held = small[:, 110:111]

        def ring_slot(s):
            return ring[:, s * UNIT:(s + 1) * UNIT]

        x_in = reg1[:, :].rearrange("p (t d) -> p t d", t=TILES)
        hT = reg2[:, :].rearrange("p (c n) -> p c n", c=KC)
        attnT = reg1[:, :].rearrange("p (c n) -> p c n", c=KC)
        h2T = attnT
        xn = reg2[:, :].rearrange("p (t d) -> p t d", t=TILES)
        xr = reg3[:, :].rearrange("p (t d) -> p t d", t=TILES)
        total = xn
        nat = reg3[:, 0:1024].rearrange("p (b n) -> p b n", b=2)
        sq = reg3[:, 1024:1536]
        rot = reg3[:, 1536:2560].rearrange("p (b n) -> p b n", b=2)
        rot2 = reg3[:, 2560:3072]
        rope = reg3[:, 3072:3584].rearrange("p (a t d) -> p a t d", a=2, t=LT)
        ropeq = reg3[:, 3584:4096].rearrange("p (a t d) -> p a t d", a=2, t=LT)
        masks = reg3[:, 4096:4352].rearrange("p (a j) -> p a j", a=2)
        silu = reg3[:, 4352:4608].rearrange("p (c m) -> p c m", c=KC)
        rot3 = reg3[:, 4608:5120]
        probs = reg3[:, 0:1280].rearrange("p (b n) -> p b n", b=2)
        pT = reg3[:, 1280:3840].rearrange("p (b h n) -> p b h n", b=2, h=2)
        qT = qt[:, :].rearrange("p (g i n) -> p g i n", g=2, i=PAIRS)
        kT = kt[:, :].rearrange("p (g v n) -> p g v n", g=2, v=2)
        vl = v_lat[:, :].rearrange("p (t n) -> p t n", t=LT)
        gate_rows = qt[:, 0:2 * D].rearrange("p (c n) -> p c n", c=2)
        cmod = colmod[:, :].rearrange("p (m c k) -> p m c k", m=4, c=2)
        modq = mod[:, :].rearrange("p (m n) -> p m n", m=N_MOD)
        ss1, ms1, rs1 = small[:, 0:5], small[:, 5:10], small[:, 10:15]
        sso, mso, rso = small[:, 15:20], small[:, 20:25], small[:, 25:30]
        ss2, ms2, rs2 = small[:, 30:35], small[:, 35:40], small[:, 40:45]
        ssh, msh, rsh = small[:, 45:53], small[:, 53:61], small[:, 61:69]
        mx, negm, den, rden, esink = (small[:, 69 + 2 * i:71 + 2 * i] for i in range(5))
        lmax, lsum, lrec = small[:, 80:85], small[:, 85:90], small[:, 90:95]
        ssf, msf, rsf = small[:, 95:100], small[:, 100:105], small[:, 105:110]
        logit = kt[:, 0:80].rearrange("p (t e) -> p t e", t=TILES)
        expl = kt[:, 80:160].rearrange("p (t e) -> p t e", t=TILES)
        aff = kt[0:E, 256:256 + TOK]
        vals_l, vals_c = kt[0:E, 1024:1024 + CAP_L], kt[0:E, 1088:1088 + CAP_C]
        idxu_l = kt[0:E, 1104:1104 + CAP_L].bitcast(U32)
        idxu_c = kt[0:E, 1168:1168 + CAP_C].bitcast(U32)
        idxf_l, idxf_c = kt[0:E, 1184:1184 + CAP_L], kt[0:E, 1248:1248 + CAP_C]
        lists = kt[0:E, 1280:1280 + 4 * P].rearrange("e (a r) -> e a r", a=4)
        row_l = kt[:, 1800:1800 + E + 1].bitcast(I32)
        row_c = kt[:, 1820:1820 + E + 1].bitcast(I32)
        g_l, g_c = kt[:, 1840:1840 + E], kt[:, 1856:1856 + E]
        get_l, get_c = kt[:, 1872:1873].bitcast(I32), kt[:, 1873:1874].bitcast(I32)
        put_l, put_c = kt[:, 1874:1875].bitcast(I32), kt[:, 1875:1876].bitcast(I32)
        xg_l, xg_c = reg1[:, 0:512], reg1[:, 512:768]
        xT_l = reg1[:, 768:1280].rearrange("p (j h s) -> p j h s", j=4, h=2)
        xT_c = reg1[:, 1280:1536].rearrange("p (j q s) -> p j q s", j=2, q=4)
        s_l, s_c = reg1[:, 1536:2048], reg1[:, 2048:2304]
        a_l, a_c = reg1[:, 2304:2816], reg1[:, 2816:3072]
        aT_l = reg1[:, 3072:3584].rearrange("p (j h s) -> p j h s", j=4, h=2)
        aT_c = reg1[:, 3584:3840].rearrange("p (j q s) -> p j q s", j=2, q=4)
        y_l, y_c = reg1[:, 3840:4352], reg1[:, 4352:4608]
        squares = x_in
        zeros = qt[:, 0:QUART]

        rows_l, rows_c = dram("rows_l", [2 * LAT, HALF]), dram("rows_c", [CTX_ROWS, QUART])
        sum_l, sum_c = dram("sum_l", [2 * LAT, HALF]), dram("sum_c", [CTX_ROWS, QUART])

        ps = ctx.enter_context(nc.psum_tensor("ps", [P, 8, 512], F32))
        flat = ps[:, :, :].rearrange("p b n -> p (b n)")
        two = [flat[:, 0:1024], flat[:, 1024:2048], flat[:, 2048:3072]]

        early_in, consts_in = sem("early_in"), sem("consts_in")
        x_loaded = [sem(f"x_loaded{t}") for t in range(TILES)]
        slot_in = [sem(f"slot_in{s}") for s in range(SLOTS)]
        zeros_set, pad_cleared = sem("zeros_set"), sem("pad_cleared")
        kt_cleared, mhalf_set = sem("kt_cleared"), sem("mhalf_set")
        silu_cleared, silu_ready = sem("silu_cleared"), sem("silu_ready")
        x_squared, x_mean, x_rstd, x_normed = sem("x_squared"), sem("x_mean"), sem("x_rstd"), sem("x_normed")
        ada_half, ada_done, mod_ready = sem("ada_half"), sem("ada_done"), sem("mod_ready")
        modcol_done, modcol_ready = sem("modcol_done"), sem("modcol_ready")
        xt_done, ht_ready, htc_ready = sem("xt_done"), sem("ht_ready"), sem("htc_ready")
        proj_done, nat_ready, sq_ready = sem("proj_done"), sem("nat_ready"), sem("sq_ready")
        head_mean, head_rstd, rot_ready = sem("head_mean"), sem("head_rstd"), sem("rot_ready")
        qk_turned, qkT_ready = sem("qk_turned"), sem("qkT_ready")
        scores_done, negmax_ready, exp_done = sem("scores_done"), sem("negmax_ready"), sem("exp_done")
        sink_exp, probs_ready = sem("sink_exp"), sem("probs_ready")
        probs_turned, pT_ready, pv_done, attn_ready = (sem("probs_turned"), sem("pT_ready"), sem("pv_done"),
                                                      sem("attn_ready"))
        gate_gained, gate_cast, gate_ready = sem("gate_gained"), sem("gate_cast"), sem("gate_ready")
        x_again = sem("x_again")
        wout_half, wout_done = sem("wout_half"), sem("wout_done")
        o_squared, o_mean, o_rstd, o_scaled = sem("o_squared"), sem("o_mean"), sem("o_rstd"), sem("o_scaled")
        x1_ready, x1_squared, x1_mean, x1_rstd = sem("x1_ready"), sem("x1_squared"), sem("x1_mean"), sem("x1_rstd")
        xn_ready, xn_turned, h2_ready, router_done = (sem("xn_ready"), sem("xn_turned"), sem("h2_ready"),
                                                      sem("router_done"))
        rows_stored = sem("rows_stored")
        logits_ready, logits_exp, aff_ready, aff_turned = (sem("logits_ready"), sem("logits_exp"),
                                                           sem("aff_ready"), sem("aff_turned"))
        lists_ready, lists_turned, rows_ready = sem("lists_ready"), sem("lists_turned"), sem("rows_ready")
        pad_set = sem("pad_set")
        get_copied, gathered_l, gathered_c = sem("get_copied"), sem("gathered_l"), sem("gathered_c")
        put_copied, added_l, added_c = sem("put_copied"), sem("added_l"), sem("added_c")
        xe_turned, xe_scaled, xe_ready = sem("xe_turned"), sem("xe_scaled"), sem("xe_ready")
        gate_a, gate_b, up_a, up_b, down_a, down_b = (sem(n) for n in (
            "gate_a", "gate_b", "up_a", "up_b", "down_a", "down_b"))
        up_c, silu_done = sem("up_c"), sem("silu_done")
        act_l_ready, act_l_turned = sem("act_l_ready"), sem("act_l_turned")
        act_c_ready, act_c_turned = sem("act_c_ready"), sem("act_c_turned")
        actT_l_ready, actT_c_ready, y_ready = sem("actT_l_ready"), sem("actT_c_ready"), sem("y_ready")
        sum_in = [sem(f"sum_in{t}") for t in range(TILES)]
        f_squared, f_mean, f_rstd = sem("f_squared"), sem("f_mean"), sem("f_rstd")
        f_gated, f_ready = sem("f_gated"), sem("f_ready")
        stored = sem("stored")
        dve_step, held_ops = sem("dve_step"), sem("held_ops")

        N_EARLY = 7
        N_CONSTS = 18
        LOADS = [sum((2 if UNITS[v][:2] == ("win", 0) else 1) for v in range(len(UNITS)) if slot_of(v) == s)
                 for s in range(SLOTS)]
        block = ctx.enter_context(nc.Block())

        @block.sync
        def _(sp):
            sp.dma_start(cvec[:, :], A["c_columns"]).then_inc(early_in, 16)
            sp.dma_start(ident[:, :], A["identity"]).then_inc(early_in, 16)
            sp.dma_start(gpre[:, :], A["g_pre_columns"]).then_inc(early_in, 16)
            b_rows = A["b_ada"][0].rearrange("(m q n) -> q m n", m=N_MOD, q=4)
            for q in range(4):
                sp.dma_start(modq[32 * q:32 * q + 32, :, :], b_rows[q:q + 1].to_broadcast([32, N_MOD, QUART]))\
                    .then_inc(early_in, 16)
            for t in range(TILES):
                src = A["x_prompt"][0] if t == 0 else A["x_sample"][0, (t - 1) * P:t * P]
                sp.dma_start(x_in[:, t, :], src).then_inc(x_loaded[t], 16)

            freed = []
            n_half = n_ada = 0
            for kind, m, h in UNITS:
                if kind == "ada" and h == 0:
                    n_half += 1
                    freed.append((ada_half, n_half))
                elif kind == "ada":
                    n_ada += 1
                    freed.append((ada_done, n_ada))
                elif kind == "win":
                    freed.append((proj_done, TILES * (m + 1)))
                else:
                    freed.append((wout_half, TILES) if h == 0 else (wout_done, TILES))
            for u, (kind, m, h) in enumerate(UNITS):
                dst = ring_slot(slot_of(u))
                if u >= SLOTS:
                    sp.wait_ge(*freed[u - SLOTS])
                if kind == "ada":
                    src = A["w_ada"][0].rearrange("(p c) n -> p c n", c=KC)[:, 4 * h:4 * h + 4, m * D:(m + 1) * D]
                    sp.dma_start(dst.rearrange("p (c n) -> p c n", c=4), src).then_inc(slot_in[slot_of(u)], 16)
                elif kind == "win":
                    w = A["w_in"][0].rearrange("(c p) n -> p c n", p=P)
                    d = dst.rearrange("p (c n) -> p c n", c=KC)
                    if m == 0:
                        sp.dma_start(d[:, :, 0:256], w[:, :, 512:768]).then_inc(slot_in[slot_of(u)], 16)
                        sp.dma_start(d[:, :, 256:512], w[:, :, 1280:1536]).then_inc(slot_in[slot_of(u)], 16)
                    else:
                        first = 0 if m == 1 else 768
                        sp.dma_start(d, w[:, :, first:first + 512]).then_inc(slot_in[slot_of(u)], 16)
                else:
                    src = A["w_out"][0].rearrange("(c p) n -> p c n", p=P)[:, 4 * h:4 * h + 4, :]
                    sp.dma_start(dst.rearrange("p (c n) -> p c n", c=4), src).then_inc(slot_in[slot_of(u)], 16)

            def expert_weight(e, s):
                w = (A["w_gate"], A["w_up"], A["w_down"])[s // 2]
                src = w[0].rearrange("e (c p) n -> e p c n", p=P)[e][:, 4 * (s % 2):4 * (s % 2) + 4, :]
                sp.dma_start(ring_slot(s).rearrange("p (c n) -> p c n", c=4), src).then_inc(slot_in[s], 16)

            for s in range(SLOTS):
                sp.wait_ge(*freed[len(UNITS) - SLOTS + s])
                expert_weight(0, s)
            with sp.Fori(1, E) as e:
                for s, used in enumerate((gate_a, gate_b, up_a, up_b, down_a, down_b)):
                    sp.wait_ge(used, e)
                    expert_weight(e, s)

            sp.wait_ge(rows_stored, 16 * TILES)
            sp.wait_ge(added_l, 16 * (E + 1))
            sp.wait_ge(added_c, 16 * (E + 1))
            for t in range(TILES):
                src = (sum_c[0:4 * CTX].rearrange("(p q) n -> p (q n)", q=4) if t == 0 else
                       sum_l[2 * (t - 1) * P:2 * t * P].rearrange("(p q) n -> p (q n)", q=2))
                sp.dma_start(total[:, t, :], src).then_inc(sum_in[t], 16)

        @block.tensor
        def _(pe):
            def landed(u):
                loads = sum((2 if UNITS[v][:2] == ("win", 0) else 1) for v in range(u + 1) if slot_of(v) == slot_of(u))
                pe.wait_ge(slot_in[slot_of(u)], 16 * loads)

            def unit_at(u, c):
                return ring_slot(slot_of(u)).rearrange("p (c n) -> p c n", c=c)

            ada_units = [u for u, x in enumerate(UNITS) if x[0] == "ada"]
            win_units = [u for u, x in enumerate(UNITS) if x[0] == "win"]
            wout_units = [u for u, x in enumerate(UNITS) if x[0] == "wout"]

            def ada(m):
                if m:
                    pe.wait_ge(mod_ready, m)
                for h in (0, 1):
                    u = ada_units[2 * m + h]
                    landed(u)
                    w = unit_at(u, 4)
                    for c in range(4):
                        for q in range(4):
                            last = pe.matmul(ps[32 * q:32 * q + 32, 4, 0:QUART], silu[:, 4 * h + c, :],
                                             w[:, c, q * QUART:(q + 1) * QUART],
                                             start=(h == 0 and c == 0), stop=(h == 1 and c == 3))
                    last.then_inc(ada_done if h else ada_half, 1)

            def mod_columns(n, m):
                pe.wait_ge(mod_ready, m + 1)
                if n:
                    pe.wait_ge(modcol_ready, n)
                for j in range(2):
                    last = pe.transpose(ps[:, 7, j * P:(j + 1) * P], modq[:, m, j * P:(j + 1) * P], ident[:, :])
                last.then_inc(modcol_done, 1)

            pe.wait_ge(early_in, 16 * N_EARLY)
            pe.wait_ge(silu_ready, 1)
            ada(0)
            mod_columns(0, 0)
            def turn_x(c):
                if c >= 2:
                    pe.wait_ge(ht_ready, c - 1)
                    pe.wait_ge(htc_ready, c - 1)
                for t in range(TILES):
                    if c == 0:
                        pe.wait_ge(x_normed, t + 1)
                    o = ps[:, 5 + c % 2, 0:P] if t == 0 else ps[:, 2 + c % 2, (t - 1) * P:t * P]
                    last = pe.transpose(o, x_in[:, t, c * P:(c + 1) * P], ident[:, :])
                last.then_inc(xt_done, 1)
            turn_x(0)
            turn_x(1)
            ada(1)
            mod_columns(1, 1)
            for c in range(2, KC):
                turn_x(c)

            def project(i):
                s, t = divmod(i, TILES)
                if i == 0:
                    pe.wait_ge(ht_ready, KC)
                    pe.wait_ge(htc_ready, KC)
                if t == 0:
                    landed(win_units[s])
                if i >= 2:
                    pe.wait_ge(nat_ready, i - 1)
                w = unit_at(win_units[s], KC)
                for c in range(KC):
                    last = pe.matmul(ps[:, i % 2, :], hT[:, c, t * P:(t + 1) * P], w[:, c, :],
                                     start=(c == 0), stop=(c == KC - 1))
                last.then_inc(proj_done, 1)

            def turn_qk(k):
                if k >= 2:
                    pe.wait_ge(qkT_ready, k - 1)
                bank = ps[:, 2 + k % 2, :]
                if k == 0:
                    for g in (0, 1):
                        last = pe.transpose(bank[:, g * P:(g + 1) * P], cache[:, 2 * g * P:(2 * g + 1) * P], ident[:, :])
                else:
                    pe.wait_ge(rot_ready, k)
                    s, t = divmod(k - 1, TILES)
                    if s == 0:
                        for g in (0, 1):
                            src = kv_ctx[:, 256 * g:256 * g + P] if t == 0 else rot[:, (k - 1) % 2, g * P:(g + 1) * P]
                            last = pe.transpose(bank[:, g * P:(g + 1) * P], src, ident[:, :])
                    else:
                        for i in range(PAIRS):
                            last = pe.transpose(bank[:, i * P:(i + 1) * P], rot[:, (k - 1) % 2, i * P:(i + 1) * P],
                                                ident[:, :])
                last.then_inc(qk_turned, 1)

            for i in range(3 * TILES):
                project(i)
                if i == 0:
                    pe.wait_ge(consts_in, 16 * N_CONSTS)
                    turn_qk(0)
                if i >= 2:
                    turn_qk(i - 1)
            for m in (2, 3, 4, 5):
                ada(m)
                if m == 2:
                    turn_qk(3 * TILES - 1)
                    turn_qk(3 * TILES)
                if m in COLS:
                    mod_columns(COLS[m], m)

            def scores(u):
                g, h, t = HEAD_UNITS[u]
                if u == 0:
                    pe.wait_ge(qkT_ready, 3 * TILES + 1)
                if u >= 2:
                    pe.wait_ge(exp_done, u - 1)
                for at, k0, n in key_parts(g, t):
                    last = pe.matmul(two[u % 2][:, at:at + n], qT[:, g, h % 4, t * P:(t + 1) * P],
                                     kT[:, g, h // 4, k0:k0 + n], start=True, stop=True)
                last.then_inc(scores_done, 1)

            def turn_probs(u):
                g, h, t = HEAD_UNITS[u]
                pe.wait_ge(probs_ready, u + 1)
                if u == 0:
                    pe.wait_ge(mod_ready, N_MOD)
                if u:
                    pe.wait_ge(pT_ready, u)
                for b in range(key_count(g, t) // P):
                    last = pe.transpose(two[2][:, b * P:(b + 1) * P], probs[:, u % 2, b * P:(b + 1) * P], ident[:, :])
                last.then_inc(probs_turned, 1)

            def values(k):
                g, h, t = HEAD_UNITS[2 * k]
                pe.wait_ge(pT_ready, 2 * k + 2)
                if k >= 2:
                    pe.wait_ge(attn_ready, k - 1)
                blocks = value_blocks(g, t)
                for n, b in enumerate(blocks):
                    for hh in (0, 1):
                        kv = (h + hh) // 4
                        if b == -1:
                            v = cache[:, (2 * g + 1) * P + kv * DH:(2 * g + 1) * P + (kv + 1) * DH]
                        elif b == 4:
                            v = kv_ctx[:, 256 * g + P + kv * DH:256 * g + P + (kv + 1) * DH]
                        else:
                            v = vl[:, b, g * P + kv * DH:g * P + (kv + 1) * DH]
                        last = pe.matmul(ps[64 * hh:64 * hh + 64, 6 + k % 2, 0:P], v,
                                         pT[:, k % 2, hh, n * P:(n + 1) * P], start=(n == 0),
                                         stop=(n == len(blocks) - 1))
                last.then_inc(pv_done, 1)

            n_units = len(HEAD_UNITS)
            scores(0)
            scores(1)
            for u in range(n_units):
                if u + 2 < n_units:
                    scores(u + 2)
                turn_probs(u)
                if u % 2 == 0 and u:
                    values(u // 2 - 1)
            values(n_units // 2 - 1)

            def cast_gate(n, m):
                for r in range(4):
                    cond, half = divmod(r, 2)
                    k = 4 * n + r
                    if r >= 2:
                        pe.wait_ge(gate_ready, k - 1)
                    elif r == 0 and n == 0:
                        pe.wait_ge(gate_gained, 1)
                        pe.wait_ge(pT_ready, n_units)
                    elif r == 0:
                        pe.wait_ge(gate_gained, 2)
                        pe.wait_ge(h2_ready, TILES)
                    for q in (0, 1):
                        row = 32 * (2 * half + q) + cond
                        last = pe.matmul(ps[:, 4 + r % 2, q * QUART:(q + 1) * QUART],
                                         ident[:, row:row + 1].to_broadcast([P, P]), modq[:, m, :],
                                         start=True, stop=True)
                    last.then_inc(gate_cast, 1)

            cast_gate(0, 2)

            def project_out(t):
                if t == 0:
                    pe.wait_ge(attn_ready, n_units // 2)
                    pe.wait_ge(exp_done, n_units)
                if t >= 2:
                    pe.wait_ge(o_scaled, t - 1)
                for h in (0, 1):
                    if t == 0:
                        landed(wout_units[h])
                    w = unit_at(wout_units[h], 4)
                    for n in (0, 1):
                        for c in range(4):
                            last = pe.matmul(two[t % 2][:, n * 512:(n + 1) * 512],
                                             attnT[:, 4 * h + c, t * P:(t + 1) * P], w[:, c, n * 512:(n + 1) * 512],
                                             start=(h == 0 and c == 0), stop=(h == 1 and c == 3))
                    last.then_inc(wout_done if h else wout_half, 1)

            def turn_x1(t):
                pe.wait_ge(xn_ready, t + 1)
                if t == 0:
                    pe.wait_ge(gate_ready, 4)
                else:
                    pe.wait_ge(h2_ready, t)
                for c in range(KC):
                    last = pe.transpose(two[2][:, c * P:(c + 1) * P], xn[:, t, c * P:(c + 1) * P], ident[:, :])
                last.then_inc(xn_turned, 1)

            def route_logits(t):
                pe.wait_ge(h2_ready, t + 1)
                for c in range(KC):
                    last = pe.matmul(ps[:, 6, t * E:(t + 1) * E], h2T[:, c, t * P:(t + 1) * P],
                                     wr[:, c * E:(c + 1) * E], start=(c == 0), stop=(c == KC - 1))
                last.then_inc(router_done, 1)

            for t in range(TILES):
                project_out(t)
                if t:
                    turn_x1(t - 1)
                if t >= 2:
                    route_logits(t - 2)
            route_logits(TILES - 2)
            turn_x1(TILES - 1)
            route_logits(TILES - 1)

            pe.wait_ge(aff_ready, 1)
            for t in range(TILES):
                last = pe.transpose(two[0][0:E, t * P:(t + 1) * P], expl[:, t, :], ident[:, :])
            last.then_inc(aff_turned, 1)
            cast_gate(1, 5)
            pe.wait_ge(lists_ready, 1)
            for a in range(4):
                last = pe.transpose(ps[:, 7, a * E:(a + 1) * E], lists[:, a, :], ident[0:E, 0:E])
            last.then_inc(lists_turned, 1)

            G, U, GC, Y, YC, TX, TC, TA = (ps[:, b, :] for b in range(8))

            def turn_rows(n):
                pe.wait_ge(gathered_l, n * 16 + 16)
                pe.wait_ge(gathered_c, n * 16 + 16)
                for j in range(4):
                    pe.transpose(TX[:, j * P:(j + 1) * P], xg_l[:, j * P:(j + 1) * P], ident[:, :])
                for j in range(2):
                    last = pe.transpose(TC[:, j * P:(j + 1) * P], xg_c[:, j * P:(j + 1) * P], ident[:, :])
                last.then_inc(xe_turned, 1)

            def weight_in(s, e):
                pe.wait_ge(slot_in[s], e * 16 + 16 * (LOADS[s] + 1))

            def product_l(s, o, x):
                w = ring_slot(s).rearrange("p (c n) -> p c n", c=4)
                hf = s % 2
                for j in range(4):
                    for n in (0, 1):
                        last = pe.matmul(o[64 * n:64 * n + 64, :], x[:, j, hf, :], w[:, j, n * HALF:(n + 1) * HALF],
                                         start=(hf == 0 and j == 0), stop=(hf == 1 and j == 3))
                return last

            def product_c(s, o, x):
                w = ring_slot(s).rearrange("p (c n) -> p c n", c=4)
                hf = s % 2
                for j in range(4):
                    c = 4 * hf + j
                    for q in range(4):
                        last = pe.matmul(o[32 * q:32 * q + 32, :], x[:, c % 2, c // 2, :],
                                         w[:, j, q * QUART:(q + 1) * QUART], start=(c == 0), stop=(c == KC - 1))
                return last

            pe.wait_ge(rows_ready, 1)
            pe.wait_ge(gate_ready, 8)
            turn_rows(0)
            with pe.Fori(0, E) as e:
                pe.wait_ge(xe_ready, e + 1)
                for half, used in ((0, gate_a), (1, gate_b)):
                    weight_in(half, e)
                    product_c(half, GC[:, 0:QUART], xT_c)
                    product_l(half, G, xT_l).then_inc(used, 1)
                pe.wait_ge(y_ready, e + 1)
                weight_in(2, e)
                product_c(2, YC[:, QUART:], xT_c)
                product_l(2, U, xT_l).then_inc(up_a, 1)
                weight_in(3, e)
                product_c(3, YC[:, QUART:], xT_c).then_inc(up_c, 1)
                product_l(3, U, xT_l).then_inc(up_b, 1)
                turn_rows(e + 1)
                pe.wait_ge(act_c_ready, e + 1)
                for j in range(2):
                    last = pe.transpose(GC[:, QUART + j * P:QUART + (j + 1) * P], a_c[:, j * P:(j + 1) * P],
                                        ident[:, :])
                last.then_inc(act_c_turned, 1)
                pe.wait_ge(act_l_ready, e + 1)
                for j in range(4):
                    last = pe.transpose(TA[:, j * P:(j + 1) * P], a_l[:, j * P:(j + 1) * P], ident[:, :])
                last.then_inc(act_l_turned, 1)
                weight_in(4, e)
                pe.wait_ge(actT_c_ready, e + 1)
                product_c(4, YC[:, 0:QUART], aT_c)
                pe.wait_ge(actT_l_ready, e + 1)
                product_l(4, Y, aT_l).then_inc(down_a, 1)
                weight_in(5, e)
                product_c(5, YC[:, 0:QUART], aT_c)
                product_l(5, Y, aT_l).then_inc(down_b, 1)

        @block.scalar
        def _(act):
            n_loads = [0]

            def load(dst, src, **how):
                act.dma_start(dst, src, **how).then_inc(consts_in, 16)
                n_loads[0] += 1

            load(cache[:, 0:P], A["cache_a_k"][0, 0].rearrange("t h d -> t (h d)"))
            load(cache[:, P:2 * P], A["cache_a_v"][0, 0].rearrange("t h d -> t (h d)"))
            load(cache[:, 2 * P:3 * P], A["cache_b_k"][0, 0].rearrange("t h d -> t (h d)"))
            load(cache[:, 3 * P:4 * P], A["cache_b_v"][0, 0].rearrange("t h d -> t (h d)"))
            load(gqk[:, 0:DH], A["g_qa"].to_broadcast([P, DH]))
            load(gqk[:, DH:2 * DH], A["g_ka"].to_broadcast([P, DH]))
            load(rope[:, :, :, :].rearrange("p a t d -> p (a t) d"),
                 A["rope_tables"].rearrange("a (t p) d -> p (a t) d", p=P))
            load(sink[:, :], A["sink_b"].to_broadcast([P, HEADS]))
            load(masks, A["window_masks"].rearrange("a p j -> p a j"))
            load(wr[:, :].rearrange("p (c e) -> p c e", e=E), A["w_router"][0].rearrange("(c p) e -> p c e", p=P))
            for n, name in enumerate(("g_post_attn", "g_post_ffn")):
                rows = A[name].rearrange("a (q n) -> q a n", q=4)
                for q in range(4):
                    load(gpost[32 * q:32 * q + 32, n * QUART:(n + 1) * QUART], rows[q].to_broadcast([32, QUART]))
            assert n_loads[0] == N_CONSTS

            act.wait_ge(early_in, 16 * N_EARLY)
            act.wait_ge(silu_cleared, 1)
            act.activation(silu[:, :, 0:2], cvec[:, :].rearrange("p (c k) -> p k c", c=2), ACT.Silu).then_inc(silu_ready, 1)
            for t in range(TILES):
                act.wait_ge(x_loaded[t], 16)
                act.activation(xn[:, t, :], x_in[:, t, :], ACT.Square, accum_out=ss1[:, t:t + 1]).then_inc(x_squared, 1)
            for t in range(TILES):
                act.wait_ge(x_rstd, t + 1)
                act.activation(x_in[:, t, :], x_in[:, t, :], ACT.Identity, scale=rs1[:, t:t + 1]).then_inc(x_normed, 1)

            act.wait_ge(modcol_ready, 2)
            for c in range(KC):
                act.wait_ge(xt_done, c + 1)
                act.activation(hT[:, c, 0:P], ps[:, 5 + c % 2, 0:P], ACT.Identity, bias=cmod[:, 0, 0, c:c + 1],
                               scale=cmod[:, 1, 0, c:c + 1]).then_inc(htc_ready, 1)

            for i in range(3 * TILES):
                s, t = divmod(i, TILES)
                act.wait_ge(proj_done, i + 1)
                if s == 0 and t == 0:
                    dst = kv_ctx[:, :]
                else:
                    dst = nat[:, i % 2, :]
                    if i >= 2:
                        act.wait_ge(rot_ready, i - 1)
                if s < 2:
                    n = P if s == 0 else 512
                    if i:
                        act.wait_ge(head_mean, i)
                    act.activation(sq[:, 0:n], ps[:, i % 2, 0:n], ACT.Square).then_inc(sq_ready, 1)
                act.activation(dst, ps[:, i % 2, :], ACT.Copy).then_inc(nat_ready, 1)

            act.wait_ge(rot_ready, 1)
            for n, first in enumerate((0, P, 2 * P, 3 * P)):
                act.dma_start(out[2 + n][0, 0].rearrange("t h d -> t (h d)"), kv_ctx[:, first:first + P]).then_inc(stored, 16)

            n_units = len(HEAD_UNITS)

            def exponentials(u):
                g, h, t = HEAD_UNITS[u]
                n = key_count(g, t)
                b = u % 2
                act.wait_ge(negmax_ready, u + 1)
                if u >= 2:
                    act.wait_ge(probs_turned, u - 1)
                if u == 0:
                    act.wait_ge(qkT_ready, 3 * TILES + 1)
                if g:
                    act.activation(esink[:, b:b + 1], sink[:, h:h + 1], ACT.Exp, bias=negm[:, b:b + 1]).then_inc(sink_exp, 1)
                act.activation(probs[:, b, 0:n], two[b][:, 0:n], ACT.Exp, bias=negm[:, b:b + 1],
                               scale=DH ** -0.5, accum_out=den[:, b:b + 1]).then_inc(exp_done, 1)

            exponentials(0)
            for u in range(n_units):
                g, h, t = HEAD_UNITS[u]
                if u + 1 < n_units:
                    exponentials(u + 1)
                act.wait_ge(probs_turned, u + 1)
                k = u // 2
                if k >= 2:
                    act.wait_ge(pv_done, k - 1)
                n = key_count(g, t)
                act.activation(pT[:, k % 2, u % 2, 0:n], two[2][:, 0:n], ACT.Copy).then_inc(pT_ready, 1)

            act.wait_ge(pv_done, n_units // 2)
            for t in range(TILES):
                src = A["x_prompt"][0] if t == 0 else A["x_sample"][0, (t - 1) * P:t * P]
                act.dma_start(xr[:, t, :], src).then_inc(x_again, 16)

            def copy_gate(n):
                for r in range(4):
                    cond, half = divmod(r, 2)
                    act.wait_ge(gate_cast, 4 * n + r + 1)
                    act.activation(gate_rows[:, cond, half * HALF:(half + 1) * HALF], ps[:, 4 + r % 2, :],
                                   ACT.Copy).then_inc(gate_ready, 1)

            act.wait_ge(scores_done, n_units)
            copy_gate(0)

            for t in range(TILES):
                act.wait_ge(wout_done, t + 1)
                act.activation(xn[:, t, :], two[t % 2], ACT.Square, accum_out=sso[:, t:t + 1]).then_inc(o_squared, 1)
                act.wait_ge(x1_ready, t + 1)
                act.activation(xn[:, t, :], xr[:, t, :], ACT.Square, accum_out=ss2[:, t:t + 1]).then_inc(x1_squared, 1)
                act.wait_ge(x1_rstd, t + 1)
                act.activation(xn[:, t, :], xr[:, t, :], ACT.Identity, scale=rs2[:, t:t + 1]).then_inc(xn_ready, 1)
                act.wait_ge(xn_ready, t + 1)
                if t == 0:
                    act.dma_start(rows_c[0:4 * CTX].rearrange("(p q) n -> p (q n)", q=4), xn[:, 0, :]).then_inc(rows_stored, 16)
                else:
                    act.dma_start(rows_l[2 * (t - 1) * P:2 * t * P].rearrange("(p q) n -> p (q n)", q=2),
                                  xn[:, t, :]).then_inc(rows_stored, 16)
            act.wait_ge(logits_ready, 1)
            act.activation(expl, logit, ACT.Exp).then_inc(logits_exp, 1)
            copy_gate(1)

            with act.Fori(0, E) as e:
                act.wait_ge(gate_b, e + 1)
                act.activation(s_l, ps[:, 0, :], ACT.Silu).then_inc(silu_done, 1)
                act.activation(s_c, ps[:, 2, 0:QUART], ACT.Silu).then_inc(silu_done, 1)
                act.wait_ge(act_c_turned, e + 1)
                act.activation(aT_c.rearrange("p j q s -> p (j q s)"), ps[:, 2, QUART:], ACT.Copy).then_inc(actT_c_ready, 1)
                act.wait_ge(act_l_turned, e + 1)
                act.activation(aT_l.rearrange("p j h s -> p (j h s)"), ps[:, 7, :], ACT.Copy).then_inc(actT_l_ready, 1)

            for t in range(TILES):
                act.wait_ge(sum_in[t], 16)
                act.activation(squares[:, t, :], total[:, t, :], ACT.Square,
                               accum_out=ssf[:, t:t + 1]).then_inc(f_squared, 1)
            for t in range(TILES):
                act.wait_ge(f_ready, t + 1)
                dst = out[0][0] if t == 0 else out[1][0, (t - 1) * P:t * P]
                act.dma_start(dst, total[:, t, :]).then_inc(stored, 16)
            act.wait_ge(stored, 16 * (4 + TILES))

        @block.vector
        def _(dve):
            chain = [0]

            def link(ins):
                ins.then_inc(dve_step, 1)
                chain[0] += 1
                dve.wait_ge(dve_step, chain[0])

            dve.memset(mhalf[:, :], -0.5).then_inc(mhalf_set, 1)
            dve.memset(silu.rearrange("p c m -> p (c m)"), 0.0).then_inc(silu_cleared, 1)
            for t in range(TILES):
                dve.wait_ge(x_squared, t + 1)
                dve.tensor_scalar(ms1[:, t:t + 1], ss1[:, t:t + 1], 1.0 / D, EPS, ALU.mult, ALU.add).then_inc(x_mean, 1)

            dve.wait_ge(early_in, 16 * N_EARLY)
            cols = ps[:, 7, 0:2 * P].rearrange("p (j q r) -> p q j r", j=2, q=4)

            def columns(m):
                n = COLS[m]
                dve.wait_ge(modcol_done, n + 1)
                for cond in (0, 1):
                    dst = cmod[:, n, cond, :].rearrange("p (q j) -> p q j", j=2)
                    if n % 2 == 0:
                        last = dve.tensor_copy(dst, cols[:, :, :, cond])
                    else:
                        g = gpre[:, (n // 2) * KC:(n // 2 + 1) * KC].rearrange("p (q j) -> p q j", j=2)
                        last = dve.scalar_tensor_tensor(dst, cols[:, :, :, cond], 1.0, g, ALU.add, ALU.mult)
                last.then_inc(modcol_ready, 1)

            dve.wait_ge(ada_done, 1)
            dve.tensor_tensor(modq[:, 0, :], ps[:, 4, 0:QUART], modq[:, 0, :], ALU.add).then_inc(mod_ready, 1)
            columns(0)
            dve.wait_ge(ada_done, 2)
            dve.tensor_tensor(modq[:, 1, :], ps[:, 4, 0:QUART], modq[:, 1, :], ALU.add).then_inc(mod_ready, 1)
            columns(1)
            dve.wait_ge(modcol_ready, 2)
            for c in range(KC):
                dve.wait_ge(xt_done, c + 1)
                dve.tensor_scalar(hT[:, c, P:TOK], ps[:, 2 + c % 2, :], cmod[:, 1, 1, c:c + 1], cmod[:, 0, 1, c:c + 1],
                                  ALU.mult, ALU.add).then_inc(ht_ready, 1)

            dve.wait_ge(consts_in, 16 * N_CONSTS)
            link(dve.tensor_scalar(nsink[:, :], sink[:, :], -1.0, None, ALU.mult))
            gq = gqk[:, 0:DH]
            gq_swap = gq.rearrange("p (a b d) -> p a b d", a=2, b=2)
            for t in range(LT):
                dve.tensor_tensor(ropeq[:, 0, t, :], rope[:, 0, t, :], gq, ALU.mult)
                for b in (0, 1):
                    last = dve.tensor_tensor(ropeq[:, 1, t, :].rearrange("p (a b d) -> p a b d", a=2, b=2)[:, :, b, :],
                                             rope[:, 1, t, :].rearrange("p (a b d) -> p a b d", a=2, b=2)[:, :, b, :],
                                             gq_swap[:, :, 1 - b, :], ALU.mult)
            link(last)

            def rotate(dst, src, heads, tables, t, order):
                n = heads * DH
                direct = rot2[:, 0:n].rearrange("p (h d) -> p h d", d=DH)
                crossed = rot3[:, 0:n].rearrange("p (h d) -> p h d", d=DH)
                by_pair = "p (h a b d) -> p h a b d"
                cos = tables[:, 0, t, :].unsqueeze(1).to_broadcast([P, heads, DH])
                dve.tensor_tensor(direct, src.rearrange("p (h d) -> p h d", d=DH), cos, ALU.mult)
                for b in (0, 1):
                    sin = tables[:, 1, t, :].rearrange("p (a b d) -> p a b d", a=2, b=2)[:, :, b, :]
                    last = dve.tensor_tensor(rot3[:, 0:n].rearrange(by_pair, a=2, b=2, d=16)[:, :, :, b, :],
                                             src.rearrange(by_pair, a=2, b=2, d=16)[:, :, :, 1 - b, :],
                                             sin.unsqueeze(1).to_broadcast([P, heads, 2, 16]), ALU.mult)
                link(last)
                return dve.tensor_tensor(dst, order(direct), order(crossed), ALU.add)

            def paired(x3):
                return x3.rearrange("p (s j) d -> p j s d", s=2)

            def same(x3):
                return x3

            def qk_out(k):
                dve.wait_ge(qk_turned, k + 1)
                bank = ps[:, 2 + k % 2, :]
                s, t = divmod(k - 1, TILES)
                if k == 0 or s == 0:
                    at = 0 if k == 0 else (TOK if t == 0 else t * P)
                    b3 = bank[:, 0:2 * P].rearrange("p (g n) -> p g n", g=2)
                    if k == 0:
                        dve.wait_ge(kt_cleared, 1)
                    dve.tensor_copy(kT[0:64, :, 0, at:at + P], b3[0:64])
                    dve.tensor_copy(kT[64:128, :, 1, at:at + P], b3[64:128]).then_inc(qkT_ready, 1)
                else:
                    if k == TILES + 1:
                        dve.wait_ge(added_l, 16)
                        dve.wait_ge(added_c, 16)
                        dve.wait_ge(pad_cleared, 16)
                    dve.tensor_copy(qT[:, s - 1, :, t * P:(t + 1) * P],
                                    bank.rearrange("p (i n) -> p i n", i=PAIRS)).then_inc(qkT_ready, 1)

            for i in range(3 * TILES):
                s, t = divmod(i, TILES)
                src = kv_ctx[:, :] if i == 0 else nat[:, i % 2, :]
                heads = 2 if s == 0 else HEADS
                if s < 2:
                    dve.wait_ge(sq_ready, i + 1)
                    link(dve.tensor_reduce(ssh[:, 0:heads], sq[:, 0:heads * DH].rearrange("p (h d) -> p h d", d=DH),
                                           AX.X, ALU.add))
                    dve.tensor_scalar(msh[:, 0:heads], ssh[:, 0:heads], 1.0 / DH, EPS, ALU.mult, ALU.add)\
                        .then_inc(head_mean, 1)
                if i >= 1:
                    qk_out(i - 1)
                dve.wait_ge(nat_ready, i + 1)
                n3 = src[:, 0:heads * DH].rearrange("p (h d) -> p h d", d=DH)
                if s < 2:
                    dve.wait_ge(head_rstd, i + 1)
                    link(dve.tensor_tensor(n3, n3, rsh[:, 0:heads].unsqueeze(2).to_broadcast([P, heads, DH]), ALU.mult))
                if s == 0:
                    gained = dve.tensor_tensor(n3, n3, gqk[:, DH:2 * DH].unsqueeze(1).to_broadcast([P, heads, DH]),
                                               ALU.mult)
                    if t == 0:
                        gained.then_inc(rot_ready, 1)
                        continue
                    link(gained)
                if i >= 2:
                    dve.wait_ge(qk_turned, i)
                if i >= 1:
                    dve.wait_ge(rot_ready, i)
                if s == 0:
                    link(rotate(rot[:, i % 2, 0:P].rearrange("p (h d) -> p h d", d=DH), src[:, 0:P], 2, rope, t - 1, same))
                    link(dve.tensor_copy(vl[:, t - 1, 0:P], src[:, P:2 * P]))
                    link(rotate(rot[:, i % 2, P:2 * P].rearrange("p (h d) -> p h d", d=DH), src[:, 2 * P:3 * P], 2,
                                rope, t - 1, same))
                    dve.tensor_copy(vl[:, t - 1, P:2 * P], src[:, 3 * P:4 * P]).then_inc(rot_ready, 1)
                else:
                    dst = rot[:, i % 2, :].rearrange("p (j s d) -> p j s d", s=2, d=DH)
                    if t:
                        rotate(dst, src, HEADS, ropeq if s == 1 else rope, t - 1, paired).then_inc(rot_ready, 1)
                    elif s == 1:
                        dve.tensor_tensor(dst, paired(n3), gq.unsqueeze(1).unsqueeze(1).to_broadcast([P, 4, 2, DH]),
                                          ALU.mult).then_inc(rot_ready, 1)
                    else:
                        dve.tensor_copy(dst, paired(n3)).then_inc(rot_ready, 1)
            qk_out(3 * TILES - 1)
            dve.wait_ge(ada_done, 3)
            dve.tensor_tensor(modq[:, 2, :], ps[:, 4, 0:QUART], modq[:, 2, :], ALU.add).then_inc(mod_ready, 1)
            qk_out(3 * TILES)
            for m in (3, 4, 5):
                dve.wait_ge(ada_done, m + 1)
                dve.tensor_tensor(modq[:, m, :], ps[:, 4, 0:QUART], modq[:, m, :], ALU.add).then_inc(mod_ready, 1)
                if m in COLS:
                    columns(m)
            dve.wait_ge(mod_ready, N_MOD)
            dve.tensor_tensor(modq[:, 2, :], modq[:, 2, :], gpost[:, 0:QUART], ALU.mult).then_inc(gate_gained, 1)
            dve.tensor_tensor(modq[:, 5, :], modq[:, 5, :], gpost[:, QUART:], ALU.mult).then_inc(gate_gained, 1)

            n_units = len(HEAD_UNITS)
            n_sink = [0]

            def maxima(u):
                g, h, t = HEAD_UNITS[u]
                n, b = key_count(g, t), u % 2
                dve.wait_ge(scores_done, u + 1)
                if g and t:
                    lo, hi = max(0, t - 2), min(LT - 1, t)
                    before, after = lo < t - 1, hi > t - 1
                    if before and after:
                        v = two[b][:, 0:512].rearrange("p (k n) -> p k n", k=4)[:, 1:4:2, :]
                        link(dve.tensor_tensor(v, v, masks, ALU.add))
                    else:
                        at, m = (P, 0) if before else (n - P, 1)
                        link(dve.tensor_tensor(two[b][:, at:at + P], two[b][:, at:at + P], masks[:, m, :], ALU.add))
                link(dve.tensor_reduce(mx[:, b:b + 1], two[b][:, 0:n], AX.X, ALU.max))
                if g:
                    dve.tensor_scalar(negm[:, b:b + 1], mx[:, b:b + 1], -DH ** -0.5, nsink[:, h:h + 1], ALU.mult,
                                      ALU.min).then_inc(negmax_ready, 1)
                else:
                    dve.tensor_scalar(negm[:, b:b + 1], mx[:, b:b + 1], -DH ** -0.5, None, ALU.mult)\
                        .then_inc(negmax_ready, 1)

            def attn_out(k):
                g, h, t = HEAD_UNITS[2 * k]
                dve.wait_ge(pv_done, k + 1)
                dve.tensor_copy(attnT[:, 4 * g + h // 2, t * P:(t + 1) * P],
                                ps[:, 6 + k % 2, 0:P]).then_inc(attn_ready, 1)

            maxima(0)
            for u in range(n_units):
                g, h, t = HEAD_UNITS[u]
                n, b = key_count(g, t), u % 2
                if u + 1 < n_units:
                    maxima(u + 1)
                dve.wait_ge(exp_done, u + 1)
                if g:
                    n_sink[0] += 1
                    dve.wait_ge(sink_exp, n_sink[0])
                    link(dve.tensor_tensor(den[:, b:b + 1], den[:, b:b + 1], esink[:, b:b + 1], ALU.add))
                link(dve.reciprocal(rden[:, b:b + 1], den[:, b:b + 1]))
                dve.tensor_scalar(probs[:, b, 0:n], probs[:, b, 0:n], rden[:, b:b + 1], None, ALU.mult)\
                    .then_inc(probs_ready, 1)
                if u % 2 == 0 and u >= 4:
                    attn_out(u // 2 - 2)
            attn_out(n_units // 2 - 2)
            attn_out(n_units // 2 - 1)

            for t in range(TILES):
                dve.wait_ge(o_squared, t + 1)
                dve.tensor_scalar(mso[:, t:t + 1], sso[:, t:t + 1], 1.0 / D, EPS, ALU.mult, ALU.add).then_inc(o_mean, 1)
                dve.wait_ge(o_rstd, t + 1)
                if t == 0:
                    dve.wait_ge(gate_ready, 4)
                    dve.wait_ge(x_again, 16 * TILES)
                dve.scalar_tensor_tensor(xn[:, t, :], two[t % 2], rso[:, t:t + 1], gate_rows[:, min(t, 1), :],
                                         ALU.mult, ALU.mult).then_inc(o_scaled, 1)
                dve.wait_ge(o_scaled, t + 1)
                dve.tensor_tensor(xr[:, t, :], xr[:, t, :], xn[:, t, :], ALU.add).then_inc(x1_ready, 1)
                dve.wait_ge(x1_squared, t + 1)
                dve.tensor_scalar(ms2[:, t:t + 1], ss2[:, t:t + 1], 1.0 / D, EPS, ALU.mult, ALU.add).then_inc(x1_mean, 1)
                dve.wait_ge(xn_turned, t + 1)
                tt = slice(t * P, (t + 1) * P)
                v = two[2].rearrange("p (c n) -> p c n", c=KC)
                cond = min(t, 1)
                link(dve.tensor_tensor(v, v, cmod[:, 3, cond, :].unsqueeze(2).to_broadcast([P, KC, P]), ALU.mult))
                dve.tensor_tensor(h2T[:, :, tt], v, cmod[:, 2, cond, :].unsqueeze(2).to_broadcast([P, KC, P]),
                                  ALU.add).then_inc(h2_ready, 1)

            dve.wait_ge(router_done, TILES)
            lg = ps[:, 6, 0:TILES * E].rearrange("p (t e) -> p t e", t=TILES)
            link(dve.tensor_reduce(lmax, lg, AX.X, ALU.max))
            dve.tensor_tensor(logit, lg, lmax.unsqueeze(2).to_broadcast([P, TILES, E]), ALU.subtract)\
                .then_inc(logits_ready, 1)
            dve.wait_ge(logits_exp, 1)
            link(dve.tensor_reduce(lsum, expl, AX.X, ALU.add))
            link(dve.reciprocal(lrec, lsum))
            dve.tensor_tensor(expl, expl, lrec.unsqueeze(2).to_broadcast([P, TILES, E]), ALU.mult).then_inc(aff_ready, 1)
            dve.wait_ge(aff_turned, 1)
            link(dve.tensor_copy(aff, two[0][0:E, 0:TOK]))

            for vals, idx, cap, part in ((vals_l, idxu_l, CAP_L, aff[:, CTX:]), (vals_c, idxu_c, CAP_C, aff[:, 0:CTX])):
                for r in range(cap // 8):
                    k = slice(8 * r, 8 * r + 8)
                    link(dve.max(vals[:, k], part))
                    link(dve.max_index(idx[:, k], vals[:, k], part))
                    link(dve.match_replace(part, vals[:, k], part, -1.0))
            link(dve.tensor_copy(idxf_l, idxu_l))
            link(dve.tensor_copy(idxf_c, idxu_c))
            dve.wait_ge(pad_set, 3)
            for h in (0, 1):
                o = h * CAP_L
                dve.tensor_scalar(lists[:, 0, o:o + CAP_L], idxf_l, 2.0, float(h), ALU.mult, ALU.add)
                dve.tensor_copy(lists[:, 1, o:o + CAP_L], vals_l)
            for q in range(4):
                o = q * CPAD
                dve.tensor_scalar(lists[:, 2, o:o + CAP_C], idxf_c, 4.0, float(q), ALU.mult, ALU.add)
                last = dve.tensor_copy(lists[:, 3, o:o + CAP_C], vals_c)
            last.then_inc(lists_ready, 1)
            dve.wait_ge(lists_turned, 1)
            turned = ps[:, 7, 0:4 * E].rearrange("p (a e) -> p a e", a=4)
            dve.tensor_copy(row_l[:, 0:E], turned[:, 0, :])
            dve.tensor_copy(g_l, turned[:, 1, :]).then_inc(y_ready, 1)
            dve.tensor_copy(row_c[:, 0:E], turned[:, 2, :])
            dve.tensor_copy(g_c, turned[:, 3, :]).then_inc(rows_ready, 1)

            def modulate(n):
                dve.wait_ge(xe_turned, n + 1)
                tx = ps[:, 5, :].rearrange("p (j h s) -> p j h s", j=4, h=2)
                tc = ps[:, 6, 0:QUART].rearrange("p (j q s) -> p j q s", j=2, q=4)
                by_l = [cmod[:, m, 1, :].rearrange("p (h j) -> p j h", h=2).unsqueeze(3).to_broadcast([P, 4, 2, CAP_L])
                        for m in (2, 3)]
                by_c = [cmod[:, m, 0, :].rearrange("p (q j) -> p j q", q=4).unsqueeze(3).to_broadcast([P, 2, 4, CPAD])
                        for m in (2, 3)]
                dve.tensor_tensor(xT_l, tx, by_l[1], ALU.mult)
                dve.tensor_tensor(xT_c, tc, by_c[1], ALU.mult).then_inc(xe_scaled, 1)
                dve.wait_ge(xe_scaled, n + 1)
                dve.tensor_tensor(xT_l, xT_l, by_l[0], ALU.add)
                dve.tensor_tensor(xT_c, xT_c, by_c[0], ALU.add).then_inc(xe_ready, 1)

            modulate(0)
            with dve.Fori(0, E) as e:
                dve.wait_ge(up_c, e + 1)
                dve.wait_ge(silu_done, e * 2 + 2)
                dve.tensor_tensor(a_c, s_c, ps[:, 4, QUART:], ALU.mult).then_inc(act_c_ready, 1)
                dve.wait_ge(up_b, e + 1)
                dve.tensor_tensor(a_l, s_l, ps[:, 1, :], ALU.mult).then_inc(act_l_ready, 1)
                modulate(e + 1)
                dve.wait_ge(down_b, e + 1)
                dve.wait_ge(added_l, e * 16 + 16)
                dve.wait_ge(added_c, e * 16 + 16)
                dve.tensor_scalar(y_l, ps[:, 3, :], g_l[:, bass.ds(e, 1)], None, ALU.mult)
                dve.tensor_scalar(y_c, ps[:, 4, 0:QUART], g_c[:, bass.ds(e, 1)], None, ALU.mult).then_inc(y_ready, 1)

            def last_gated(t):
                dve.wait_ge(f_squared, t + 1)
                dve.tensor_scalar(msf[:, t:t + 1], ssf[:, t:t + 1], 1.0 / D, EPS, ALU.mult, ALU.add).then_inc(f_mean, 1)
                dve.tensor_tensor(total[:, t, :], total[:, t, :], gate_rows[:, min(t, 1), :], ALU.mult).then_inc(f_gated, 1)

            def last_sum(t):
                dve.wait_ge(f_rstd, t + 1)
                dve.wait_ge(f_gated, t + 1)
                dve.scalar_tensor_tensor(total[:, t, :], total[:, t, :], rsf[:, t:t + 1], xr[:, t, :],
                                         ALU.mult, ALU.add).then_inc(f_ready, 1)

            for t in range(TILES):
                last_gated(t)
                if t:
                    last_sum(t - 1)
            last_sum(TILES - 1)

        @block.gpsimd
        def _(pool):
            pool.memset(zeros, 0.0).then_inc(zeros_set, 1)
            pool.memset(kt[:, :], 0.0).then_inc(kt_cleared, 1)
            pool.wait_ge(zeros_set, 1)
            pool.dma_start(sum_l.rearrange("(p a) (b n) -> p (a b) n", p=P, n=QUART),
                           zeros.unsqueeze(1).to_broadcast([P, 16, QUART])).then_inc(added_l, 16)
            pool.dma_start(sum_c.rearrange("(p a) n -> p a n", p=64),
                           zeros[0:64].unsqueeze(1).to_broadcast([64, CTX_ROWS // 64, QUART])).then_inc(added_c, 16)
            pool.dma_start(rows_c[4 * CTX:CTX_ROWS], zeros[0:CTX_ROWS - 4 * CTX]).then_inc(pad_cleared, 16)
            pool.wait_ge(mhalf_set, 1)

            def root(dst, mean, n, ready, done, count):
                pool.wait_ge(ready, count)
                pool.tensor_tensor(dst, mean, mhalf[:, 0:n], ALU.pow).then_inc(done, 1)

            for t in range(TILES):
                root(rs1[:, t:t + 1], ms1[:, t:t + 1], 1, x_mean, x_rstd, t + 1)
            for i in range(2 * TILES):
                heads = 2 if i < TILES else HEADS
                root(rsh[:, 0:heads], msh[:, 0:heads], heads, head_mean, head_rstd, i + 1)
            for t in range(TILES):
                root(rso[:, t:t + 1], mso[:, t:t + 1], 1, o_mean, o_rstd, t + 1)
                root(rs2[:, t:t + 1], ms2[:, t:t + 1], 1, x1_mean, x1_rstd, t + 1)

            pool.wait_ge(scores_done, len(HEAD_UNITS))
            pool.iota(lists[:, 2, :].rearrange("e (q r) -> e q r", q=4)[:, :, CAP_C:], [[CPAD - CAP_C, 4], [1, CPAD - CAP_C]],
                      base=4 * CTX, channel_multiplier=0, allow_small_or_imprecise_dtypes=True).then_inc(pad_set, 1)
            pool.memset(lists[:, 3, :].rearrange("e (q r) -> e q r", q=4)[:, :, CAP_C:], 0.0).then_inc(pad_set, 1)
            pool.memset(kt[:, 1800:1840].bitcast(I32), 0).then_inc(pad_set, 1)

            def hold(pool):
                pool.tensor_tensor(held, mhalf[:, 0:1], mhalf[:, 1:2], ALU.add).then_inc(held_ops, 1)

            def gather(n):
                pool.tensor_copy(get_l, row_l[:, bass.ds(n, 1)])
                pool.tensor_copy(get_c, row_c[:, bass.ds(n, 1)]).then_inc(get_copied, 1)
                pool.wait_ge(get_copied, n + 1)
                hold(pool)
                pool.indirect_dma_start(xg_l, None, rows_l, bass.IndirectOffsetOnAxis(ap=get_l, axis=0))\
                    .then_inc(gathered_l, 16)
                pool.indirect_dma_start(xg_c, None, rows_c, bass.IndirectOffsetOnAxis(ap=get_c, axis=0))\
                    .then_inc(gathered_c, 16)

            pool.wait_ge(rows_ready, 1)
            pool.wait_ge(rows_stored, 16 * TILES)
            pool.wait_ge(pad_cleared, 16)
            gather(0)
            with pool.Fori(0, E) as e:
                pool.wait_ge(xe_turned, e + 1)
                gather(e + 1)
                pool.wait_ge(added_l, e * 16 + 16)
                pool.wait_ge(added_c, e * 16 + 16)
                pool.tensor_copy(put_l, row_l[:, bass.ds(e, 1)])
                pool.tensor_copy(put_c, row_c[:, bass.ds(e, 1)]).then_inc(put_copied, 1)
                pool.wait_ge(put_copied, e + 1)
                pool.wait_ge(y_ready, e + 2)
                hold(pool)
                pool.indirect_dma_start(sum_l, bass.IndirectOffsetOnAxis(ap=put_l, axis=0), y_l, None,
                                        compute_op=ALU.add).then_inc(added_l, 16)
                pool.indirect_dma_start(sum_c, bass.IndirectOffsetOnAxis(ap=put_c, axis=0), y_c, None,
                                        compute_op=ALU.add).then_inc(added_c, 16)
            pool.wait_ge(added_l, 16 * (E + 1))
            pool.wait_ge(added_c, 16 * (E + 1))
            for t in range(TILES):
                root(rsf[:, t:t + 1], msf[:, t:t + 1], 1, f_mean, f_rstd, t + 1)


_INS = ["x_prompt", "x_sample", "cache_a_k", "cache_a_v", "cache_b_k", "cache_b_v", "w_ada", "b_ada",
        "w_in", "g_qa", "g_ka", "sink_b", "w_out", "g_post_attn", "w_router", "w_gate",
        "w_up", "w_down", "g_post_ffn"]
_OUTS = [(1, CTX, D), (1, LAT, D)] + [(1, 1, CTX, 2, DH)] * 4
GRID_W = 64
ROPE_THETA = 10000.0


def shape_constants():
    half = DH // 4
    freqs = (np.float32(ROPE_THETA) ** (-np.arange(half, dtype=np.float32) / np.float32(half))).astype(np.float32)
    pos = np.arange(LAT)
    tables = np.zeros((2, LAT, DH), np.float32)
    for a, where in enumerate((pos // GRID_W, pos % GRID_W)):
        ang = where.astype(np.float32)[:, None] * freqs[None, :]
        cos, sin = np.cos(ang).astype(np.float32), np.sin(ang).astype(np.float32)
        o = 2 * half * a
        tables[0, :, o:o + half], tables[0, :, o + half:o + 2 * half] = cos, cos
        tables[1, :, o:o + half], tables[1, :, o + half:o + 2 * half] = -sin, sin
    q, k = np.arange(P)[:, None], np.arange(P)[None, :]
    masks = np.zeros((2, P, P), np.float32)
    masks[0][k < q] = NEG
    masks[1][k > q] = NEG
    return {"identity": np.eye(P, dtype=np.float32), "rope_tables": tables, "window_masks": masks}


def column_layouts(inputs):
    c = [np.asarray(inputs["c_ctx"]).reshape(P, KC), np.asarray(inputs["c"]).reshape(P, KC)]
    g = [np.asarray(inputs[n]).reshape(KC, P).T for n in ("g_pre_attn", "g_pre_ffn")]
    return {"c_columns": np.ascontiguousarray(np.concatenate(c, axis=1)),
            "g_pre_columns": np.ascontiguousarray(np.concatenate(g, axis=1))}


def kernel(**inputs):
    import concourse.bacc as bacc
    from concourse.bass_utils import run_bass_kernel_spmd

    nc = bacc.Bacc("TRN2", target_bir_lowering=False, num_devices=1)
    arrays, handles = {}, {}
    given = {name: np.ascontiguousarray(inputs[name]) for name in _INS}
    for name, a in {**given, **column_layouts(inputs), **shape_constants()}.items():
        arrays[f"in_{name}"] = a
        handles[name] = nc.dram_tensor(f"in_{name}", a.shape, mybir.dt.from_np(a.dtype), kind="ExternalInput").ap()
    outs = [nc.dram_tensor(f"out_{i}", s, F32, kind="ExternalOutput").ap() for i, s in enumerate(_OUTS)]
    build(nc, handles, outs)
    r = run_bass_kernel_spmd(nc, [arrays], core_ids=[0])
    return tuple(r.results[0][f"out_{i}"] for i in range(len(_OUTS)))
```

```python
from contextlib import ExitStack

import numpy as np

import concourse.bass as bass
from concourse import mybir

F32 = mybir.dt.float32
I32 = mybir.dt.int32
U32 = mybir.dt.uint32
ALU = mybir.AluOpType
ACT = mybir.ActivationFunctionType
AX = mybir.AxisListType

P = 128
D = 1024
KC = D // P
CTX = 128
LAT = 512
TILES = (CTX + LAT) // P
LT = LAT // P
TOK = CTX + LAT
DH = 64
HEADS = 8
PAIRS = HEADS // 2
E = 16
CAP_L = 2 * LAT // E
CAP_C = 2 * CTX // E
CPAD = 32
HALF = D // 2
QUART = D // 4
N_MOD = 6
EPS = 1e-6
SLOTS = 6
UNIT = 4096
NEG = -1e30
CTX_ROWS = 4 * CTX + 4 * (CPAD - CAP_C)

UNITS = ([("ada", m, h) for m in (0, 1) for h in (0, 1)] + [("win", s, 0) for s in range(3)]
         + [("ada", m, h) for m in (2, 3, 4, 5) for h in (0, 1)] + [("wout", 0, h) for h in (0, 1)])
UNIT_SLOT = [1, 2, 3, 4, 5, 0, 1, 2, 3, 4, 2, 3, 4, 2, 3, 4, 5]
ADA_AFTER = {2: 2, 5: 3, 8: 4, 11: 5}
MODS = (0, 1, 2, 3, 4, 5)
COLS = {0: 0, 1: 1, 3: 2, 4: 3}
OUT_ORDER = [1, 2, 3, 4, 0]
HEAD_UNITS = ([(0, h, t) for t in range(TILES) for h in range(HEADS)]
              + [(1, h, t) for t in OUT_ORDER for h in range(HEADS)])
A_UNITS = TILES * HEADS
OUT_STEPS = {2: (0, 3), 3: (3, 6), 4: (6, 9), 5: (9, 12), 6: (12, 14), 7: (14, 16)}


def slot_of(u):
    return UNIT_SLOT[u]


def unit_before(u, s):
    return max((v for v in range(u) if slot_of(v) == s), default=None)


def key_parts(g, t):
    if t == 0:
        return [(0, TOK, CTX)]
    if g == 0:
        return [(0, 0, 512), (512, 512, TOK - 512)]
    lo, hi = max(0, t - 2), min(LT - 1, t)
    return [(0, 0, CTX), (CTX, CTX + lo * P, (hi + 1 - lo) * P)]


def key_count(g, t):
    return sum(n for _, _, n in key_parts(g, t))


def value_blocks(g, t):
    if t == 0:
        return [4]
    if g == 0:
        return [-1, 0, 1, 2, 3]
    return [-1] + list(range(max(0, t - 2), min(LT - 1, t) + 1))


def build(nc, A, out):
    ctx = ExitStack()
    with ctx:
        def sb(name, n, dt=F32):
            return ctx.enter_context(nc.sbuf_tensor(name, [P, n], dt))

        def sem(name):
            return ctx.enter_context(nc.semaphore(name))

        def dram(name, shape):
            return nc.dram_tensor(name, shape, F32, kind="Internal").ap()

        ring = sb("ring", SLOTS * UNIT)
        reg1 = sb("reg1", KC * TOK)
        reg2_qt = sb("reg2_qt", KC * TOK + 2 * PAIRS * TOK)
        reg2, qt = reg2_qt[:, 0:KC * TOK], reg2_qt[:, KC * TOK:]
        reg3 = sb("reg3", KC * TOK)
        kt = sb("kt", 2 * 2 * (TOK + CTX))
        v_lat = sb("v_lat", LT * 256)
        kv_ctx = sb("kv_ctx", 512)
        cache = sb("cache", 4 * P)
        ident = sb("ident", P)
        mod = sb("mod", N_MOD * QUART)
        gpost = sb("gpost", 2 * QUART)
        gpre = sb("gpre", 2 * KC)
        colmod = sb("colmod", 4 * 2 * KC)
        wr = sb("wr", KC * E)
        cvec = sb("cvec", 2 * KC)
        gqk = sb("gqk", 2 * DH)
        sink = sb("sink", HEADS)
        nsink = sb("nsink", HEADS)
        small = sb("small", 160)
        mhalf = sb("mhalf", 16)
        held = small[:, 110:111]

        def ring_slot(s):
            if s >= SLOTS:
                return reg2_qt[:, (s - SLOTS) * UNIT:(s - SLOTS + 1) * UNIT]
            return ring[:, s * UNIT:(s + 1) * UNIT]

        x_in = reg1[:, :].rearrange("p (t d) -> p t d", t=TILES)
        hT = reg2.rearrange("p (c n) -> p c n", c=KC)
        attnT = reg1[:, :].rearrange("p (c n) -> p c n", c=KC)
        h2T = attnT
        xn = reg2.rearrange("p (t d) -> p t d", t=TILES)
        xr = reg3[:, :].rearrange("p (t d) -> p t d", t=TILES)
        total = xn
        nat = reg3[:, 0:1024].rearrange("p (b n) -> p b n", b=2)
        sq = reg3[:, 1024:1536]
        rot = reg3[:, 1536:2560].rearrange("p (b n) -> p b n", b=2)
        rot2 = reg3[:, 2560:3072]
        rope = reg3[:, 3072:3584].rearrange("p (a t d) -> p a t d", a=2, t=LT)
        ropeq = reg3[:, 3584:4096].rearrange("p (a t d) -> p a t d", a=2, t=LT)
        silu = reg3[:, 4352:4608].rearrange("p (c m) -> p c m", c=KC)
        rot3 = reg3[:, 4608:5120]
        probs = ring[:, 0:1280].rearrange("p (b n) -> p b n", b=2)
        pT = ring[:, 1280:3840].rearrange("p (b h n) -> p b h n", b=2, h=2)
        masks = ring[:, 3840:4096].rearrange("p (a j) -> p a j", a=2)
        qT = qt.rearrange("p (g i n) -> p g i n", g=2, i=PAIRS)
        kT = kt[:, :].rearrange("p (g v n) -> p g v n", g=2, v=2)
        vl = v_lat[:, :].rearrange("p (t n) -> p t n", t=LT)
        gate_rows = qt[:, 3072:3072 + 2 * D].rearrange("p (c n) -> p c n", c=2)
        cmod = colmod[:, :].rearrange("p (m c k) -> p m c k", m=4, c=2)
        modq = mod[:, :].rearrange("p (m n) -> p m n", m=N_MOD)
        ss1, ms1, rs1 = small[:, 0:5], small[:, 5:10], small[:, 10:15]
        sso, mso, rso = small[:, 15:20], small[:, 20:25], small[:, 25:30]
        ss2, ms2, rs2 = small[:, 30:35], small[:, 35:40], small[:, 40:45]
        ssh, msh, rsh = small[:, 45:53], small[:, 53:61], small[:, 61:69]
        mx, negm, den, rden, esink = (small[:, 69 + 2 * i:71 + 2 * i] for i in range(5))
        lmax, lsum, lrec = small[:, 80:85], small[:, 85:90], small[:, 90:95]
        ssf, msf, rsf = small[:, 95:100], small[:, 100:105], small[:, 105:110]
        logit = kt[:, 0:80].rearrange("p (t e) -> p t e", t=TILES)
        expl = kt[:, 80:160].rearrange("p (t e) -> p t e", t=TILES)
        aff = kt[0:E, 256:256 + TOK]
        vals_l, vals_c = kt[0:E, 1024:1024 + CAP_L], kt[0:E, 1088:1088 + CAP_C]
        idxu_l = kt[0:E, 1104:1104 + CAP_L].bitcast(U32)
        idxu_c = kt[0:E, 1168:1168 + CAP_C].bitcast(U32)
        idxf_l, idxf_c = kt[0:E, 1184:1184 + CAP_L], kt[0:E, 1248:1248 + CAP_C]
        lists = kt[0:E, 1280:1280 + 4 * P].rearrange("e (a r) -> e a r", a=4)
        row_l = kt[:, 1800:1800 + E + 2].bitcast(I32)
        row_c = kt[:, 1820:1820 + E + 2].bitcast(I32)
        g_l, g_c = kt[:, 1840:1840 + E], kt[:, 1856:1856 + E]
        get_l, get_c = kt[:, 1872:1873].bitcast(I32), kt[:, 1873:1874].bitcast(I32)
        put_l, put_c = kt[:, 1874:1875].bitcast(I32), kt[:, 1875:1876].bitcast(I32)
        xg_l, xg_c = reg1[:, 0:512], reg1[:, 512:768]
        xT_l = [v.rearrange("p (j h s) -> p j h s", j=4, h=2) for v in (reg1[:, 768:1280], kt[:, 2048:2560])]
        xT_c = [v.rearrange("p (j q s) -> p j q s", j=2, q=4) for v in (reg1[:, 1280:1536], kt[:, 2560:2816])]
        s_l, s_c = reg1[:, 1536:2048], reg1[:, 2048:2304]
        a_l, a_c = reg1[:, 2304:2816], reg1[:, 2816:3072]
        aT_l = reg1[:, 3072:3584].rearrange("p (j h s) -> p j h s", j=4, h=2)
        aT_c = reg1[:, 3584:3840].rearrange("p (j q s) -> p j q s", j=2, q=4)
        y_l, y_c = reg1[:, 3840:4352], reg1[:, 4352:4608]
        squares = x_in
        zeros = qt[:, 0:QUART]

        rows_l, rows_c = dram("rows_l", [2 * LAT, HALF]), dram("rows_c", [CTX_ROWS, QUART])
        sum_l, sum_c = dram("sum_l", [2 * LAT, HALF]), dram("sum_c", [CTX_ROWS, QUART])

        ps = ctx.enter_context(nc.psum_tensor("ps", [P, 8, 512], F32))
        flat = ps[:, :, :].rearrange("p b n -> p (b n)")
        out_lat, out_ctx = ps[:, 2:4, :], ps[:, 0:2, :]
        two = [flat[:, 0:1024], flat[:, 1024:2048], flat[:, 2048:3072]]

        def scores_at(u):
            return two[u % 2] if u < A_UNITS else ps[:, u % 2, :]

        cond_in, early_in, consts_in = sem("cond_in"), sem("early_in"), sem("consts_in")
        x_loaded = [sem(f"x_loaded{t}") for t in range(TILES)]
        slot_in = [sem(f"slot_in{s}") for s in range(SLOTS + 2)]
        zeros_set, pad_cleared = sem("zeros_set"), sem("pad_cleared")
        kt_cleared, mhalf_set = sem("kt_cleared"), sem("mhalf_set")
        silu_cleared, silu_ready = sem("silu_cleared"), sem("silu_ready")
        x_squared, x_mean, x_rstd, x_normed = sem("x_squared"), sem("x_mean"), sem("x_rstd"), sem("x_normed")
        ada_half, ada_done, mod_ready = sem("ada_half"), sem("ada_done"), sem("mod_ready")
        modcol_done, modcol_ready = sem("modcol_done"), sem("modcol_ready")
        xt_done, ht_ready, htc_ready = sem("xt_done"), sem("ht_ready"), sem("htc_ready")
        proj_done, nat_ready, sq_ready = sem("proj_done"), sem("nat_ready"), sem("sq_ready")
        head_mean, head_rstd, rot_ready = sem("head_mean"), sem("head_rstd"), sem("rot_ready")
        qk_turned, qkT_ready = sem("qk_turned"), sem("qkT_ready")
        scores_done, negmax_ready, exp_done = sem("scores_done"), sem("negmax_ready"), sem("exp_done")
        sink_exp, probs_ready = sem("sink_exp"), sem("probs_ready")
        probs_turned, pT_ready, pv_done, attn_ready = (sem("probs_turned"), sem("pT_ready"), sem("pv_done"),
                                                      sem("attn_ready"))
        gate_gained, gate_cast, gate_ready = sem("gate_gained"), sem("gate_cast"), sem("gate_ready")
        x_again, masks_in = sem("x_again"), sem("masks_in")
        wout_done = sem("wout_done")
        o_squared, o_mean, o_rstd, o_scaled = sem("o_squared"), sem("o_mean"), sem("o_rstd"), sem("o_scaled")
        x1_ready, x1_squared, x1_mean, x1_rstd = sem("x1_ready"), sem("x1_squared"), sem("x1_mean"), sem("x1_rstd")
        xn_ready, xn_turned, h2_ready, router_done = (sem("xn_ready"), sem("xn_turned"), sem("h2_ready"),
                                                      sem("router_done"))
        rows_stored = sem("rows_stored")
        logits_ready, logits_exp, aff_ready, aff_turned = (sem("logits_ready"), sem("logits_exp"),
                                                           sem("aff_ready"), sem("aff_turned"))
        lists_ready, lists_turned, rows_ready = sem("lists_ready"), sem("lists_turned"), sem("rows_ready")
        pad_set = sem("pad_set")
        get_copied, gathered_l, gathered_c = sem("get_copied"), sem("gathered_l"), sem("gathered_c")
        put_copied, added_l, added_c = sem("put_copied"), sem("added_l"), sem("added_c")
        xe_turned, xe_scaled, xe_ready = sem("xe_turned"), sem("xe_scaled"), sem("xe_ready")
        gate_a, gate_b, up_a, up_b, down_a, down_b = (sem(n) for n in (
            "gate_a", "gate_b", "up_a", "up_b", "down_a", "down_b"))
        up_c, silu_done = sem("up_c"), sem("silu_done")
        act_l_ready, act_l_turned = sem("act_l_ready"), sem("act_l_turned")
        act_c_ready, act_c_turned = sem("act_c_ready"), sem("act_c_turned")
        actT_l_ready, actT_c_ready, y_ready = sem("actT_l_ready"), sem("actT_c_ready"), sem("y_ready")
        sum_in = [sem(f"sum_in{t}") for t in range(TILES)]
        f_squared, f_mean, f_rstd = sem("f_squared"), sem("f_mean"), sem("f_rstd")
        f_gated, f_ready = sem("f_gated"), sem("f_ready")
        stored = sem("stored")
        dve_step, held_ops = sem("dve_step"), sem("held_ops")

        N_EARLY = 6
        N_CONSTS = 17
        LOADS = [sum((2 if UNITS[v][:2] == ("win", 0) else 1) for v in range(len(UNITS)) if slot_of(v) == s)
                 for s in range(SLOTS)]
        block = ctx.enter_context(nc.Block())

        @block.sync
        def _(sp):
            sp.dma_start(cvec[:, :], A["c_columns"]).then_inc(cond_in, 16)

            freed = []
            n_half = n_ada = 0
            for kind, m, h in UNITS:
                if kind == "ada" and h == 0:
                    n_half += 1
                    freed.append((ada_half, n_half))
                elif kind == "ada":
                    n_ada += 1
                    freed.append((ada_done, n_ada))
                elif kind == "win":
                    freed.append((proj_done, TILES * (m + 1)))
                else:
                    freed.append((wout_done, TILES))
            for u, (kind, m, h) in enumerate(UNITS):
                dst = ring_slot(slot_of(u))
                before = unit_before(u, slot_of(u))
                if before is not None:
                    sp.wait_ge(*freed[before])
                if u == 2:
                    for t in range(TILES):
                        src = A["x_prompt"][0] if t == 0 else A["x_sample"][0, (t - 1) * P:t * P]
                        sp.dma_start(x_in[:, t, :], src).then_inc(x_loaded[t], 16)
                if kind == "ada":
                    src = A["w_ada"][0].rearrange("(p c) n -> p c n", c=KC)[:, 4 * h:4 * h + 4, m * D:(m + 1) * D]
                    sp.dma_start(dst.rearrange("p (c n) -> p c n", c=4), src).then_inc(slot_in[slot_of(u)], 16)
                elif kind == "win":
                    w = A["w_in"][0].rearrange("(c p) n -> p c n", p=P)
                    d = dst.rearrange("p (c n) -> p c n", c=KC)
                    if m == 0:
                        sp.dma_start(d[:, :, 0:256], w[:, :, 512:768]).then_inc(slot_in[slot_of(u)], 16)
                        sp.dma_start(d[:, :, 256:512], w[:, :, 1280:1536]).then_inc(slot_in[slot_of(u)], 16)
                    else:
                        first = 0 if m == 1 else 768
                        sp.dma_start(d, w[:, :, first:first + 512]).then_inc(slot_in[slot_of(u)], 16)
                else:
                    src = A["w_out"][0].rearrange("(c p) n -> p c n", p=P)[:, 4 * h:4 * h + 4, :]
                    sp.dma_start(dst.rearrange("p (c n) -> p c n", c=4), src).then_inc(slot_in[slot_of(u)], 16)

            sp.wait_ge(qkT_ready, 3 * TILES + 1)
            sp.wait_ge(ada_done, N_MOD)
            sp.dma_start(masks, A["window_masks"].rearrange("a p j -> p a j")).then_inc(masks_in, 16)
            for t in range(TILES):
                src = A["x_prompt"][0] if t == 0 else A["x_sample"][0, (t - 1) * P:t * P]
                sp.dma_start(xr[:, t, :], src).then_inc(x_again, 16)

            def expert_weight(e, kind, half, s):
                w = (A["w_gate"], A["w_up"], A["w_down"])[kind]
                src = w[0].rearrange("e (c p) n -> e p c n", p=P)[e][:, 4 * half:4 * half + 4, :]
                sp.dma_start(ring_slot(s).rearrange("p (c n) -> p c n", c=4), src).then_inc(slot_in[s], 16)

            for s in (1, 2, 3, 0, 4, 5):
                sp.wait_ge(*freed[unit_before(len(UNITS), s)])
                if s == 0:
                    sp.wait_ge(pv_done, len(HEAD_UNITS) // 2)
                expert_weight(0, s // 2, s % 2, s)
            sp.wait_ge(scores_done, len(HEAD_UNITS))
            sp.wait_ge(rows_stored, 16 * TILES)
            sp.wait_ge(xn_turned, 2 * TILES)
            for half in (0, 1):
                expert_weight(1, 0, half, SLOTS + half)

            def refill(e, kind, odd=False):
                used = ((gate_a, gate_b), (up_a, up_b), (down_a, down_b))[kind]
                for half in (0, 1):
                    sp.wait_ge(used[half], e - 1 if kind == 0 else e)
                    expert_weight(e, kind, half, SLOTS + half if odd else 2 * kind + half)

            refill(2, 0)
            with sp.Fori(0, E // 2 - 2) as pair:
                for odd in (0, 1):
                    refill(pair * 2 + odd + 1, 1)
                    refill(pair * 2 + odd + 3, 0, odd=not odd)
                    refill(pair * 2 + odd + 1, 2)
            for e in range(E - 3, E):
                refill(e, 1)
                if e + 2 < E:
                    refill(e + 2, 0, odd=True)
                refill(e, 2)

            sp.wait_ge(added_l, 16 * (E + 1))
            sp.wait_ge(added_c, 16 * (E + 1))
            for t in range(TILES):
                src = (sum_c[0:4 * CTX].rearrange("(p q) n -> p (q n)", q=4) if t == 0 else
                       sum_l[2 * (t - 1) * P:2 * t * P].rearrange("(p q) n -> p (q n)", q=2))
                sp.dma_start(total[:, t, :], src).then_inc(sum_in[t], 16)

        @block.tensor
        def _(pe):
            def landed(u):
                loads = sum((2 if UNITS[v][:2] == ("win", 0) else 1) for v in range(u + 1) if slot_of(v) == slot_of(u))
                pe.wait_ge(slot_in[slot_of(u)], 16 * loads)

            def unit_at(u, c):
                return ring_slot(slot_of(u)).rearrange("p (c n) -> p c n", c=c)

            ada_units = [u for u, x in enumerate(UNITS) if x[0] == "ada"]
            win_units = [u for u, x in enumerate(UNITS) if x[0] == "win"]
            wout_units = [u for u, x in enumerate(UNITS) if x[0] == "wout"]

            def ada(m):
                if m:
                    pe.wait_ge(mod_ready, m)
                for h in (0, 1):
                    u = ada_units[2 * m + h]
                    landed(u)
                    w = unit_at(u, 4)
                    for c in range(4):
                        for q in range(4):
                            last = pe.matmul(ps[32 * q:32 * q + 32, 4, 0:QUART], silu[:, 4 * h + c, :],
                                             w[:, c, q * QUART:(q + 1) * QUART],
                                             start=(h == 0 and c == 0), stop=(h == 1 and c == 3))
                    last.then_inc(ada_done if h else ada_half, 1)

            def mod_columns(n, m):
                pe.wait_ge(mod_ready, m + 1)
                if n:
                    pe.wait_ge(modcol_ready, n)
                for j in range(2):
                    last = pe.transpose(ps[:, 7, j * P:(j + 1) * P], modq[:, m, j * P:(j + 1) * P], ident[:, :])
                last.then_inc(modcol_done, 1)

            pe.wait_ge(silu_ready, 1)
            ada(0)
            pe.wait_ge(early_in, 16 * N_EARLY)
            mod_columns(0, 0)
            def turn_x(c):
                if c >= 2:
                    pe.wait_ge(ht_ready, c - 1)
                    pe.wait_ge(htc_ready, c - 1)
                for t in range(TILES):
                    if c == 0:
                        pe.wait_ge(x_normed, t + 1)
                    o = ps[:, 5 + c % 2, 0:P] if t == 0 else ps[:, 2 + c % 2, (t - 1) * P:t * P]
                    last = pe.transpose(o, x_in[:, t, c * P:(c + 1) * P], ident[:, :])
                last.then_inc(xt_done, 1)
            turn_x(0)
            turn_x(1)
            ada(1)
            mod_columns(1, 1)
            def project(i):
                s, t = divmod(i, TILES)
                if i == 1:
                    pe.wait_ge(ht_ready, KC)
                if t == 0:
                    landed(win_units[s])
                if i >= 2:
                    pe.wait_ge(nat_ready, i - 1)
                w = unit_at(win_units[s], KC)
                for c in range(KC):
                    if i == 0:
                        if c + 2 < KC:
                            turn_x(c + 2)
                        pe.wait_ge(htc_ready, c + 1)
                    last = pe.matmul(ps[:, i % 2, :], hT[:, c, t * P:(t + 1) * P], w[:, c, :],
                                     start=(c == 0), stop=(c == KC - 1))
                last.then_inc(proj_done, 1)

            def turn_qk(k):
                if k >= 2:
                    pe.wait_ge(qkT_ready, k - 1)
                bank = ps[:, 2 + k % 2, :]
                if k == 0:
                    for g in (0, 1):
                        last = pe.transpose(bank[:, g * P:(g + 1) * P], cache[:, 2 * g * P:(2 * g + 1) * P], ident[:, :])
                else:
                    pe.wait_ge(rot_ready, k)
                    s, t = divmod(k - 1, TILES)
                    if s == 0:
                        for g in (0, 1):
                            src = kv_ctx[:, 256 * g:256 * g + P] if t == 0 else rot[:, (k - 1) % 2, g * P:(g + 1) * P]
                            last = pe.transpose(bank[:, g * P:(g + 1) * P], src, ident[:, :])
                    else:
                        for i in range(PAIRS):
                            last = pe.transpose(bank[:, i * P:(i + 1) * P], rot[:, (k - 1) % 2, i * P:(i + 1) * P],
                                                ident[:, :])
                last.then_inc(qk_turned, 1)

            for i in range(3 * TILES):
                project(i)
                if i == 1:
                    pe.wait_ge(consts_in, 16 * N_CONSTS)
                    turn_qk(0)
                if i >= 2:
                    turn_qk(i - 1)
                if i in ADA_AFTER:
                    ada(ADA_AFTER[i])
                if i - 2 in ADA_AFTER and ADA_AFTER[i - 2] in COLS:
                    mod_columns(COLS[ADA_AFTER[i - 2]], ADA_AFTER[i - 2])
            turn_qk(3 * TILES - 1)
            turn_qk(3 * TILES)

            def scores(u):
                g, h, t = HEAD_UNITS[u]
                if u == 0:
                    pe.wait_ge(qkT_ready, 3 * TILES + 1)
                if u >= 2:
                    pe.wait_ge(exp_done, u - 1)
                for at, k0, n in key_parts(g, t):
                    last = pe.matmul(scores_at(u)[:, at:at + n], qT[:, 1 - g, h % 4, t * P:(t + 1) * P],
                                     kT[:, g, h // 4, k0:k0 + n], start=True, stop=True)
                last.then_inc(scores_done, 1)

            def turn_probs(u):
                g, h, t = HEAD_UNITS[u]
                pe.wait_ge(probs_ready, u + 1)
                if u == 0:
                    pe.wait_ge(mod_ready, N_MOD)
                if u:
                    pe.wait_ge(pT_ready, u)
                for b in range(key_count(g, t) // P):
                    last = pe.transpose(two[2][:, b * P:(b + 1) * P], probs[:, u % 2, b * P:(b + 1) * P], ident[:, :])
                last.then_inc(probs_turned, 1)

            def values(k):
                g, h, t = HEAD_UNITS[2 * k]
                pe.wait_ge(pT_ready, 2 * k + 2)
                if k >= 2:
                    pe.wait_ge(attn_ready, k - 1)
                blocks = value_blocks(g, t)
                for n, b in enumerate(blocks):
                    for hh in (0, 1):
                        kv = (h + hh) // 4
                        if b == -1:
                            v = cache[:, (2 * g + 1) * P + kv * DH:(2 * g + 1) * P + (kv + 1) * DH]
                        elif b == 4:
                            v = kv_ctx[:, 256 * g + P + kv * DH:256 * g + P + (kv + 1) * DH]
                        else:
                            v = vl[:, b, g * P + kv * DH:g * P + (kv + 1) * DH]
                        last = pe.matmul(ps[64 * hh:64 * hh + 64, 6 + k % 2, 0:P], v,
                                         pT[:, k % 2, hh, n * P:(n + 1) * P], start=(n == 0),
                                         stop=(n == len(blocks) - 1))
                last.then_inc(pv_done, 1)

            n_units = len(HEAD_UNITS)

            def cast_gate(n, r):
                cond, half = divmod(r, 2)
                k = 4 * n + r
                if n == 0:
                    bank = 2 + r % 2
                    if r == 0:
                        pe.wait_ge(gate_gained, 1)
                        pe.wait_ge(exp_done, A_UNITS)
                else:
                    bank = 4 + r % 2
                    if r == 0:
                        pe.wait_ge(gate_gained, 2)
                        pe.wait_ge(h2_ready, 2 * TILES)
                if r >= 2:
                    pe.wait_ge(gate_ready, k - 1)
                for q in (0, 1):
                    row = 32 * (2 * half + q) + cond
                    last = pe.matmul(ps[:, bank, q * QUART:(q + 1) * QUART],
                                     ident[:, row:row + 1].to_broadcast([P, P]), modq[:, (2, 5)[n], :],
                                     start=True, stop=True)
                last.then_inc(gate_cast, 1)

            def project_out(o, first, last_one):
                t = OUT_ORDER[o]
                dst = out_ctx if t == 0 else out_lat
                for i in range(first, last_one):
                    n, c = divmod(i, KC)
                    if i == 0 and o == 0:
                        landed(wout_units[0])
                        landed(wout_units[1])
                        pe.wait_ge(gate_ready, 4)
                    elif i == 0 and t:
                        pe.wait_ge(o_scaled, o)
                    elif i == 0:
                        pe.wait_ge(exp_done, n_units)
                    if n == 0 and c >= 4:
                        pe.wait_ge(attn_ready, A_UNITS // 2 + PAIRS * o + c - 3)
                    last = pe.matmul(dst[:, n, :], attnT[:, c, t * P:(t + 1) * P],
                                     unit_at(wout_units[c // 4], 4)[:, c % 4, n * 512:(n + 1) * 512],
                                     start=(c == 0), stop=(c == KC - 1))
                    if i == 2 * KC - 1:
                        last.then_inc(wout_done, 1)

            def turn_x1(o, half):
                t, n = OUT_ORDER[o], 2 * o + half
                after = o >= TILES - 2
                pe.wait_ge(xn_ready, o + 1)
                if 0 < n < 2 * TILES - 3:
                    pe.wait_ge(h2_ready, n)
                elif n == 2 * TILES - 3:
                    pe.wait_ge(pT_ready, n_units)
                elif n:
                    pe.wait_ge(h2_ready, n - 1)
                bank = 4 if after and half else 5
                for c in range(4):
                    last = pe.transpose(ps[:, bank, c * P:(c + 1) * P],
                                        xn[:, t, (4 * half + c) * P:(4 * half + c + 1) * P], ident[:, :])
                last.then_inc(xn_turned, 1)

            def route_logits(o):
                t = OUT_ORDER[o]
                pe.wait_ge(h2_ready, 2 * o + 2)
                if o == 0:
                    pe.wait_ge(attn_ready, n_units // 2)
                for c in range(KC):
                    last = pe.matmul(ps[:, 6 if t else 7, t * E:(t + 1) * E], h2T[:, c, t * P:(t + 1) * P],
                                     wr[:, c * E:(c + 1) * E], start=(c == 0), stop=(c == KC - 1))
                last.then_inc(router_done, 1)

            scores(0)
            scores(1)
            for u in range(n_units):
                if u + 2 < n_units:
                    scores(u + 2)
                turn_probs(u)
                if u % 2 == 0 and u:
                    values(u // 2 - 1)
                o, j = divmod(u - A_UNITS, HEADS)
                if o == 0 and j < 4:
                    cast_gate(0, j)
                if o >= 1 and j in OUT_STEPS:
                    project_out(o - 1, *OUT_STEPS[j])
                if o >= 2 and j in (4, 6):
                    turn_x1(o - 2, (j - 4) // 2)
            values(n_units // 2 - 1)
            project_out(4, 0, KC)
            for o in range(3):
                route_logits(o)
            turn_x1(3, 0)
            project_out(4, KC, KC + 4)
            turn_x1(3, 1)
            project_out(4, KC + 4, 2 * KC)
            route_logits(3)

            pe.wait_ge(aff_ready, 1)
            for t in range(1, TILES):
                last = pe.transpose(ps[0:E, 2, (t - 1) * P:t * P], expl[:, t, :], ident[:, :])
            last.then_inc(aff_turned, 1)
            turn_x1(4, 0)
            turn_x1(4, 1)
            route_logits(4)
            pe.wait_ge(aff_ready, 2)
            pe.transpose(ps[0:E, 3, 0:P], expl[:, 0, :], ident[:, :]).then_inc(aff_turned, 1)
            for r in range(4):
                cast_gate(1, r)
            pe.wait_ge(lists_ready, 1)
            for a in range(4):
                last = pe.transpose(ps[:, 7, a * E:(a + 1) * E], lists[:, a, :], ident[0:E, 0:E])
            last.then_inc(lists_turned, 1)

            G, U, GC, Y, YC, TX, TC, TA = (ps[:, b, :] for b in range(8))

            def turn_rows(n):
                pe.wait_ge(gathered_l, n * 16 + 16)
                pe.wait_ge(gathered_c, n * 16 + 16)
                for j in range(4):
                    pe.transpose(TX[:, j * P:(j + 1) * P], xg_l[:, j * P:(j + 1) * P], ident[:, :])
                for j in range(2):
                    last = pe.transpose(TC[:, j * P:(j + 1) * P], xg_c[:, j * P:(j + 1) * P], ident[:, :])
                last.then_inc(xe_turned, 1)

            def weight_in(s, e):
                pe.wait_ge(slot_in[s], e * 16 + 16 * (LOADS[s] + 1))

            def gate_in(half, pair, odd):
                if odd:
                    pe.wait_ge(slot_in[SLOTS + half], pair * 16 + 16)
                else:
                    pe.wait_ge(slot_in[half], pair * 16 + 16 * (LOADS[half] + 1))

            def product_l(s, o, x):
                w = ring_slot(s).rearrange("p (c n) -> p c n", c=4)
                hf = s % 2
                for j in range(4):
                    for n in (0, 1):
                        last = pe.matmul(o[64 * n:64 * n + 64, :], x[:, j, hf, :], w[:, j, n * HALF:(n + 1) * HALF],
                                         start=(hf == 0 and j == 0), stop=(hf == 1 and j == 3))
                return last

            def product_c(s, o, x):
                w = ring_slot(s).rearrange("p (c n) -> p c n", c=4)
                hf = s % 2
                for j in range(4):
                    c = 4 * hf + j
                    for q in range(4):
                        last = pe.matmul(o[32 * q:32 * q + 32, :], x[:, c % 2, c // 2, :],
                                         w[:, j, q * QUART:(q + 1) * QUART], start=(c == 0), stop=(c == KC - 1))
                return last

            pe.wait_ge(rows_ready, 1)
            pe.wait_ge(gate_ready, 8)
            turn_rows(0)

            def gate_product(pair, odd, half):
                gate_in(half, pair, odd)
                s = SLOTS * odd + half
                product_c(s, GC[:, 0:QUART], xT_c[odd])
                product_l(s, G, xT_l[odd]).then_inc((gate_a, gate_b)[half], 1)

            def expert(e, odd, following):
                weight_in(2, e)
                pe.wait_ge(silu_done, e * 2 + 2)
                product_c(2, GC[:, QUART:], xT_c[odd])
                product_l(2, U, xT_l[odd]).then_inc(up_a, 1)
                turn_rows(e + 1)
                weight_in(3, e)
                product_c(3, GC[:, QUART:], xT_c[odd]).then_inc(up_c, 1)
                product_l(3, U, xT_l[odd]).then_inc(up_b, 1)
                pe.wait_ge(act_c_ready, e + 1)
                if following:
                    pe.wait_ge(xe_ready, e + 2)
                    gate_product(*following, 0)
                for j in range(2):
                    last = pe.transpose(TC[:, QUART + j * P:QUART + (j + 1) * P], a_c[:, j * P:(j + 1) * P],
                                        ident[:, :])
                last.then_inc(act_c_turned, 1)
                pe.wait_ge(act_l_ready, e + 1)
                for j in range(4):
                    last = pe.transpose(TA[:, j * P:(j + 1) * P], a_l[:, j * P:(j + 1) * P], ident[:, :])
                last.then_inc(act_l_turned, 1)
                if following:
                    gate_product(*following, 1)
                pe.wait_ge(y_ready, e + 1)
                weight_in(4, e)
                pe.wait_ge(actT_c_ready, e + 1)
                product_c(4, YC[:, 0:QUART], aT_c)
                pe.wait_ge(actT_l_ready, e + 1)
                product_l(4, Y, aT_l).then_inc(down_a, 1)
                weight_in(5, e)
                product_c(5, YC[:, 0:QUART], aT_c)
                product_l(5, Y, aT_l).then_inc(down_b, 1)

            pe.wait_ge(xe_ready, 1)
            gate_product(0, 0, 0)
            gate_product(0, 0, 1)
            with pe.Fori(0, E // 2 - 1) as pair:
                expert(pair * 2, 0, (pair, 1))
                expert(pair * 2 + 1, 1, (pair + 1, 0))
            expert(E - 2, 0, (E // 2 - 1, 1))
            expert(E - 1, 1, None)

        @block.scalar
        def _(act):
            n_loads = [0]

            def load(dst, src, **how):
                act.dma_start(dst, src, **how).then_inc(consts_in, 16)
                n_loads[0] += 1

            act.dma_start(ident[:, :], A["identity"]).then_inc(early_in, 16)
            act.dma_start(gpre[:, :], A["g_pre_columns"]).then_inc(early_in, 16)
            b_rows = A["b_ada"][0].rearrange("(m q n) -> q m n", m=N_MOD, q=4)
            for q in range(4):
                act.dma_start(modq[32 * q:32 * q + 32, :, :], b_rows[q:q + 1].to_broadcast([32, N_MOD, QUART]))\
                    .then_inc(early_in, 16)
            load(cache[:, 0:P], A["cache_a_k"][0, 0].rearrange("t h d -> t (h d)"))
            load(cache[:, P:2 * P], A["cache_a_v"][0, 0].rearrange("t h d -> t (h d)"))
            load(cache[:, 2 * P:3 * P], A["cache_b_k"][0, 0].rearrange("t h d -> t (h d)"))
            load(cache[:, 3 * P:4 * P], A["cache_b_v"][0, 0].rearrange("t h d -> t (h d)"))
            load(gqk[:, 0:DH], A["g_qa"].to_broadcast([P, DH]))
            load(gqk[:, DH:2 * DH], A["g_ka"].to_broadcast([P, DH]))
            load(rope[:, :, :, :].rearrange("p a t d -> p (a t) d"),
                 A["rope_tables"].rearrange("a (t p) d -> p (a t) d", p=P))
            load(sink[:, :], A["sink_b"].to_broadcast([P, HEADS]))
            load(wr[:, :].rearrange("p (c e) -> p c e", e=E), A["w_router"][0].rearrange("(c p) e -> p c e", p=P))
            for n, name in enumerate(("g_post_attn", "g_post_ffn")):
                rows = A[name].rearrange("a (q n) -> q a n", q=4)
                for q in range(4):
                    load(gpost[32 * q:32 * q + 32, n * QUART:(n + 1) * QUART], rows[q].to_broadcast([32, QUART]))
            assert n_loads[0] == N_CONSTS

            act.wait_ge(cond_in, 16)
            act.wait_ge(silu_cleared, 1)
            act.activation(silu[:, :, 0:2], cvec[:, :].rearrange("p (c k) -> p k c", c=2), ACT.Silu).then_inc(silu_ready, 1)
            for t in range(TILES):
                act.wait_ge(x_loaded[t], 16)
                act.activation(xn[:, t, :], x_in[:, t, :], ACT.Square, accum_out=ss1[:, t:t + 1]).then_inc(x_squared, 1)
            for t in range(TILES):
                act.wait_ge(x_rstd, t + 1)
                act.activation(x_in[:, t, :], x_in[:, t, :], ACT.Identity, scale=rs1[:, t:t + 1]).then_inc(x_normed, 1)

            act.wait_ge(modcol_ready, 2)
            for c in range(KC):
                act.wait_ge(xt_done, c + 1)
                act.activation(hT[:, c, 0:P], ps[:, 5 + c % 2, 0:P], ACT.Identity, bias=cmod[:, 0, 0, c:c + 1],
                               scale=cmod[:, 1, 0, c:c + 1]).then_inc(htc_ready, 1)

            for i in range(3 * TILES):
                s, t = divmod(i, TILES)
                act.wait_ge(proj_done, i + 1)
                if s == 0 and t == 0:
                    dst = kv_ctx[:, :]
                else:
                    dst = nat[:, i % 2, :]
                    if i >= 2:
                        act.wait_ge(rot_ready, i - 1)
                if s < 2:
                    n = P if s == 0 else 512
                    if i:
                        act.wait_ge(head_mean, i)
                    act.activation(sq[:, 0:n], ps[:, i % 2, 0:n], ACT.Square).then_inc(sq_ready, 1)
                act.activation(dst, ps[:, i % 2, :], ACT.Copy).then_inc(nat_ready, 1)

            act.wait_ge(rot_ready, 1)
            for n, first in enumerate((0, P, 2 * P, 3 * P)):
                act.dma_start(out[2 + n][0, 0].rearrange("t h d -> t (h d)"), kv_ctx[:, first:first + P]).then_inc(stored, 16)

            n_units = len(HEAD_UNITS)

            def exponentials(u):
                g, h, t = HEAD_UNITS[u]
                n = key_count(g, t)
                b = u % 2
                act.wait_ge(negmax_ready, u + 1)
                if u >= 2:
                    act.wait_ge(probs_turned, u - 1)
                if g:
                    act.activation(esink[:, b:b + 1], sink[:, h:h + 1], ACT.Exp, bias=negm[:, b:b + 1]).then_inc(sink_exp, 1)
                act.activation(probs[:, b, 0:n], scores_at(u)[:, 0:n], ACT.Exp, bias=negm[:, b:b + 1],
                               scale=DH ** -0.5, accum_out=den[:, b:b + 1]).then_inc(exp_done, 1)

            def copy_gate(n, r):
                cond, half = divmod(r, 2)
                act.wait_ge(gate_cast, 4 * n + r + 1)
                bank = (4 + r % 2) if n else (2 + r % 2)
                act.activation(gate_rows[:, cond, half * HALF:(half + 1) * HALF], ps[:, bank, :],
                               ACT.Copy).then_inc(gate_ready, 1)

            def square_out(o):
                t = OUT_ORDER[o]
                act.wait_ge(wout_done, o + 1)
                act.activation(xn[:, t, :].rearrange("p (a n) -> p a n", a=2), out_lat if t else out_ctx, ACT.Square,
                               accum_out=sso[:, t:t + 1]).then_inc(o_squared, 1)

            def square_x1(o):
                t = OUT_ORDER[o]
                act.wait_ge(x1_ready, o + 1)
                act.activation(xn[:, t, :], xr[:, t, :], ACT.Square, accum_out=ss2[:, t:t + 1]).then_inc(x1_squared, 1)

            def normalise_x1(o):
                t = OUT_ORDER[o]
                act.wait_ge(x1_rstd, o + 1)
                act.activation(xn[:, t, :], xr[:, t, :], ACT.Identity, scale=rs2[:, t:t + 1]).then_inc(xn_ready, 1)

            def store_rows(o):
                t = OUT_ORDER[o]
                act.wait_ge(xn_ready, o + 1)
                if t == 0:
                    act.dma_start(rows_c[0:4 * CTX].rearrange("(p q) n -> p (q n)", q=4), xn[:, 0, :]).then_inc(rows_stored, 16)
                else:
                    act.dma_start(rows_l[2 * (t - 1) * P:2 * t * P].rearrange("(p q) n -> p (q n)", q=2),
                                  xn[:, t, :]).then_inc(rows_stored, 16)

            exponentials(0)
            for u in range(n_units):
                g, h, t = HEAD_UNITS[u]
                if u + 1 < n_units:
                    exponentials(u + 1)
                o, j = divmod(u - A_UNITS, HEADS)
                if o >= 2 and j in (0, 2, 3, 4):
                    {0: square_out, 2: square_x1, 3: normalise_x1, 4: store_rows}[j](o - 2)
                act.wait_ge(probs_turned, u + 1)
                k = u // 2
                if k >= 2:
                    act.wait_ge(pv_done, k - 1)
                n = key_count(g, t)
                act.activation(pT[:, k % 2, u % 2, 0:n], two[2][:, 0:n], ACT.Copy).then_inc(pT_ready, 1)
                if o == 0 and j < 4:
                    copy_gate(0, j)
            for step in (square_out, square_x1, normalise_x1, store_rows):
                step(3)
            square_out(4)
            act.wait_ge(logits_ready, 1)
            act.activation(expl[:, 1:, :], logit[:, 1:, :], ACT.Exp).then_inc(logits_exp, 1)
            square_x1(4)
            normalise_x1(4)
            store_rows(4)
            for half in (0, 1):
                act.wait_ge(xn_turned, 2 * TILES - 1 + half)
                for c in range(4):
                    k = 4 * half + c
                    last = act.activation(h2T[:, k, 0:P], ps[:, 5 - half, c * P:(c + 1) * P], ACT.Identity,
                                          bias=cmod[:, 2, 0, k:k + 1], scale=cmod[:, 3, 0, k:k + 1])
                last.then_inc(h2_ready, 1)
            act.wait_ge(logits_ready, 2)
            act.activation(expl[:, 0, :], logit[:, 0, :], ACT.Exp).then_inc(logits_exp, 1)
            for r in range(4):
                copy_gate(1, r)

            def silu_gate(e):
                act.wait_ge(gate_b, e + 1)
                act.activation(s_c, ps[:, 2, 0:QUART], ACT.Silu).then_inc(silu_done, 1)
                act.activation(s_l, ps[:, 0, :], ACT.Silu).then_inc(silu_done, 1)

            def copy_turned(e):
                act.wait_ge(act_c_turned, e + 1)
                act.activation(aT_c.rearrange("p j q s -> p (j q s)"), ps[:, 6, QUART:], ACT.Copy).then_inc(actT_c_ready, 1)
                act.wait_ge(act_l_turned, e + 1)
                act.activation(aT_l.rearrange("p j h s -> p (j h s)"), ps[:, 7, :], ACT.Copy).then_inc(actT_l_ready, 1)

            silu_gate(0)
            with act.Fori(0, E - 1) as e:
                copy_turned(e)
                silu_gate(e + 1)
            copy_turned(E - 1)

            for t in range(TILES):
                act.wait_ge(sum_in[t], 16)
                act.activation(squares[:, t, :], total[:, t, :], ACT.Square,
                               accum_out=ssf[:, t:t + 1]).then_inc(f_squared, 1)
            for t in range(TILES):
                act.wait_ge(f_ready, t + 1)
                dst = out[0][0] if t == 0 else out[1][0, (t - 1) * P:t * P]
                act.dma_start(dst, total[:, t, :]).then_inc(stored, 16)
            act.wait_ge(stored, 16 * (4 + TILES))

        @block.vector
        def _(dve):
            chain = [0]

            def link(ins):
                ins.then_inc(dve_step, 1)
                chain[0] += 1
                dve.wait_ge(dve_step, chain[0])

            dve.memset(mhalf[:, :], -0.5).then_inc(mhalf_set, 1)
            dve.memset(silu.rearrange("p c m -> p (c m)"), 0.0).then_inc(silu_cleared, 1)
            for t in range(TILES):
                dve.wait_ge(x_squared, t + 1)
                dve.tensor_scalar(ms1[:, t:t + 1], ss1[:, t:t + 1], 1.0 / D, EPS, ALU.mult, ALU.add).then_inc(x_mean, 1)

            dve.wait_ge(early_in, 16 * N_EARLY)
            cols = ps[:, 7, 0:2 * P].rearrange("p (j q r) -> p q j r", j=2, q=4)

            def columns(m):
                n = COLS[m]
                dve.wait_ge(modcol_done, n + 1)
                for cond in (0, 1):
                    dst = cmod[:, n, cond, :].rearrange("p (q j) -> p q j", j=2)
                    if n % 2 == 0:
                        last = dve.tensor_copy(dst, cols[:, :, :, cond])
                    else:
                        g = gpre[:, (n // 2) * KC:(n // 2 + 1) * KC].rearrange("p (q j) -> p q j", j=2)
                        last = dve.scalar_tensor_tensor(dst, cols[:, :, :, cond], 1.0, g, ALU.add, ALU.mult)
                last.then_inc(modcol_ready, 1)

            dve.wait_ge(ada_done, 1)
            dve.tensor_tensor(modq[:, 0, :], ps[:, 4, 0:QUART], modq[:, 0, :], ALU.add).then_inc(mod_ready, 1)
            columns(0)
            dve.wait_ge(ada_done, 2)
            dve.tensor_tensor(modq[:, 1, :], ps[:, 4, 0:QUART], modq[:, 1, :], ALU.add).then_inc(mod_ready, 1)
            columns(1)
            dve.wait_ge(modcol_ready, 2)
            for c in range(KC):
                dve.wait_ge(xt_done, c + 1)
                dve.tensor_scalar(hT[:, c, P:TOK], ps[:, 2 + c % 2, :], cmod[:, 1, 1, c:c + 1], cmod[:, 0, 1, c:c + 1],
                                  ALU.mult, ALU.add).then_inc(ht_ready, 1)

            dve.wait_ge(consts_in, 16 * N_CONSTS)
            link(dve.tensor_scalar(nsink[:, :], sink[:, :], -1.0, None, ALU.mult))
            gq = gqk[:, 0:DH]
            gq_swap = gq.rearrange("p (a b d) -> p a b d", a=2, b=2)
            for t in range(LT):
                dve.tensor_tensor(ropeq[:, 0, t, :], rope[:, 0, t, :], gq, ALU.mult)
                for b in (0, 1):
                    last = dve.tensor_tensor(ropeq[:, 1, t, :].rearrange("p (a b d) -> p a b d", a=2, b=2)[:, :, b, :],
                                             rope[:, 1, t, :].rearrange("p (a b d) -> p a b d", a=2, b=2)[:, :, b, :],
                                             gq_swap[:, :, 1 - b, :], ALU.mult)
            link(last)

            def rotate(dst, src, heads, tables, t, order):
                n = heads * DH
                direct = rot2[:, 0:n].rearrange("p (h d) -> p h d", d=DH)
                crossed = rot3[:, 0:n].rearrange("p (h d) -> p h d", d=DH)
                by_pair = "p (h a b d) -> p h a b d"
                cos = tables[:, 0, t, :].unsqueeze(1).to_broadcast([P, heads, DH])
                dve.tensor_tensor(direct, src.rearrange("p (h d) -> p h d", d=DH), cos, ALU.mult)
                for b in (0, 1):
                    sin = tables[:, 1, t, :].rearrange("p (a b d) -> p a b d", a=2, b=2)[:, :, b, :]
                    last = dve.tensor_tensor(rot3[:, 0:n].rearrange(by_pair, a=2, b=2, d=16)[:, :, :, b, :],
                                             src.rearrange(by_pair, a=2, b=2, d=16)[:, :, :, 1 - b, :],
                                             sin.unsqueeze(1).to_broadcast([P, heads, 2, 16]), ALU.mult)
                link(last)
                return dve.tensor_tensor(dst, order(direct), order(crossed), ALU.add)

            def paired(x3):
                return x3.rearrange("p (s j) d -> p j s d", s=2)

            def same(x3):
                return x3

            def qk_out(k):
                dve.wait_ge(qk_turned, k + 1)
                bank = ps[:, 2 + k % 2, :]
                s, t = divmod(k - 1, TILES)
                if k == 0 or s == 0:
                    at = 0 if k == 0 else (TOK if t == 0 else t * P)
                    b3 = bank[:, 0:2 * P].rearrange("p (g n) -> p g n", g=2)
                    if k == 0:
                        dve.wait_ge(kt_cleared, 1)
                    dve.tensor_copy(kT[0:64, :, 0, at:at + P], b3[0:64])
                    dve.tensor_copy(kT[64:128, :, 1, at:at + P], b3[64:128]).then_inc(qkT_ready, 1)
                else:
                    if k == TILES + 1:
                        dve.wait_ge(added_l, 16)
                        dve.wait_ge(added_c, 16)
                        dve.wait_ge(pad_cleared, 16)
                    dve.tensor_copy(qT[:, 2 - s, :, t * P:(t + 1) * P],
                                    bank.rearrange("p (i n) -> p i n", i=PAIRS)).then_inc(qkT_ready, 1)

            for i in range(3 * TILES):
                s, t = divmod(i, TILES)
                if i - 1 in ADA_AFTER:
                    m = ADA_AFTER[i - 1]
                    dve.wait_ge(ada_done, m + 1)
                    dve.tensor_tensor(modq[:, m, :], ps[:, 4, 0:QUART], modq[:, m, :], ALU.add).then_inc(mod_ready, 1)
                if i - 3 in ADA_AFTER and ADA_AFTER[i - 3] in COLS:
                    columns(ADA_AFTER[i - 3])
                src = kv_ctx[:, :] if i == 0 else nat[:, i % 2, :]
                heads = 2 if s == 0 else HEADS
                if s < 2:
                    dve.wait_ge(sq_ready, i + 1)
                    link(dve.tensor_reduce(ssh[:, 0:heads], sq[:, 0:heads * DH].rearrange("p (h d) -> p h d", d=DH),
                                           AX.X, ALU.add))
                    dve.tensor_scalar(msh[:, 0:heads], ssh[:, 0:heads], 1.0 / DH, EPS, ALU.mult, ALU.add)\
                        .then_inc(head_mean, 1)
                if i >= 1:
                    qk_out(i - 1)
                dve.wait_ge(nat_ready, i + 1)
                n3 = src[:, 0:heads * DH].rearrange("p (h d) -> p h d", d=DH)
                if s < 2:
                    dve.wait_ge(head_rstd, i + 1)
                    link(dve.tensor_tensor(n3, n3, rsh[:, 0:heads].unsqueeze(2).to_broadcast([P, heads, DH]), ALU.mult))
                if s == 0:
                    gained = dve.tensor_tensor(n3, n3, gqk[:, DH:2 * DH].unsqueeze(1).to_broadcast([P, heads, DH]),
                                               ALU.mult)
                    if t == 0:
                        gained.then_inc(rot_ready, 1)
                        continue
                    link(gained)
                if i >= 2:
                    dve.wait_ge(qk_turned, i)
                if i >= 1:
                    dve.wait_ge(rot_ready, i)
                if s == 0:
                    link(rotate(rot[:, i % 2, 0:P].rearrange("p (h d) -> p h d", d=DH), src[:, 0:P], 2, rope, t - 1, same))
                    link(dve.tensor_copy(vl[:, t - 1, 0:P], src[:, P:2 * P]))
                    link(rotate(rot[:, i % 2, P:2 * P].rearrange("p (h d) -> p h d", d=DH), src[:, 2 * P:3 * P], 2,
                                rope, t - 1, same))
                    dve.tensor_copy(vl[:, t - 1, P:2 * P], src[:, 3 * P:4 * P]).then_inc(rot_ready, 1)
                else:
                    dst = rot[:, i % 2, :].rearrange("p (j s d) -> p j s d", s=2, d=DH)
                    if t:
                        rotate(dst, src, HEADS, ropeq if s == 1 else rope, t - 1, paired).then_inc(rot_ready, 1)
                    elif s == 1:
                        dve.tensor_tensor(dst, paired(n3), gq.unsqueeze(1).unsqueeze(1).to_broadcast([P, 4, 2, DH]),
                                          ALU.mult).then_inc(rot_ready, 1)
                    else:
                        dve.tensor_copy(dst, paired(n3)).then_inc(rot_ready, 1)
            qk_out(3 * TILES - 1)
            qk_out(3 * TILES)
            dve.wait_ge(mod_ready, N_MOD)
            dve.tensor_tensor(modq[:, 2, :], modq[:, 2, :], gpost[:, 0:QUART], ALU.mult).then_inc(gate_gained, 1)
            dve.tensor_tensor(modq[:, 5, :], modq[:, 5, :], gpost[:, QUART:], ALU.mult).then_inc(gate_gained, 1)

            n_units = len(HEAD_UNITS)
            n_sink = [0]

            def maxima(u):
                g, h, t = HEAD_UNITS[u]
                n, b = key_count(g, t), u % 2
                dve.wait_ge(scores_done, u + 1)
                if g and u == A_UNITS:
                    dve.wait_ge(masks_in, 16)
                if g and t:
                    lo, hi = max(0, t - 2), min(LT - 1, t)
                    before, after = lo < t - 1, hi > t - 1
                    if before and after:
                        v = scores_at(u)[:, 0:512].rearrange("p (k n) -> p k n", k=4)[:, 1:4:2, :]
                        link(dve.tensor_tensor(v, v, masks, ALU.add))
                    else:
                        at, m = (P, 0) if before else (n - P, 1)
                        link(dve.tensor_tensor(scores_at(u)[:, at:at + P], scores_at(u)[:, at:at + P], masks[:, m, :], ALU.add))
                link(dve.tensor_reduce(mx[:, b:b + 1], scores_at(u)[:, 0:n], AX.X, ALU.max))
                if g:
                    dve.tensor_scalar(negm[:, b:b + 1], mx[:, b:b + 1], -DH ** -0.5, nsink[:, h:h + 1], ALU.mult,
                                      ALU.min).then_inc(negmax_ready, 1)
                else:
                    dve.tensor_scalar(negm[:, b:b + 1], mx[:, b:b + 1], -DH ** -0.5, None, ALU.mult)\
                        .then_inc(negmax_ready, 1)

            def attn_out(k):
                g, h, t = HEAD_UNITS[2 * k]
                dve.wait_ge(pv_done, k + 1)
                dve.tensor_copy(attnT[:, 4 * g + h // 2, t * P:(t + 1) * P],
                                ps[:, 6 + k % 2, 0:P]).then_inc(attn_ready, 1)

            def out_mean(o):
                t = OUT_ORDER[o]
                dve.wait_ge(o_squared, o + 1)
                dve.tensor_scalar(mso[:, t:t + 1], sso[:, t:t + 1], 1.0 / D, EPS, ALU.mult, ALU.add).then_inc(o_mean, 1)

            def gate_out(o):
                t = OUT_ORDER[o]
                dve.wait_ge(o_rstd, o + 1)
                if o == 0:
                    dve.wait_ge(gate_ready, 4)
                dve.scalar_tensor_tensor(xn[:, t, :].rearrange("p (a n) -> p a n", a=2), out_lat if t else out_ctx,
                                         rso[:, t:t + 1],
                                         gate_rows[:, min(t, 1), :].rearrange("p (a n) -> p a n", a=2),
                                         ALU.mult, ALU.mult).then_inc(o_scaled, 1)

            def add_out(o):
                t = OUT_ORDER[o]
                if o == 0:
                    dve.wait_ge(x_again, 16 * TILES)
                dve.wait_ge(o_scaled, o + 1)
                dve.tensor_tensor(xr[:, t, :], xr[:, t, :], xn[:, t, :], ALU.add).then_inc(x1_ready, 1)

            def x1_mean_of(o):
                t = OUT_ORDER[o]
                dve.wait_ge(x1_squared, o + 1)
                dve.tensor_scalar(ms2[:, t:t + 1], ss2[:, t:t + 1], 1.0 / D, EPS, ALU.mult, ALU.add).then_inc(x1_mean, 1)

            def modulate_x1(o, half):
                t = OUT_ORDER[o]
                cond, tt = min(t, 1), slice(t * P, (t + 1) * P)
                dve.wait_ge(xn_turned, 2 * o + half + 1)
                bank = 4 if o >= TILES - 2 and half else 5
                v = ps[:, bank, :].rearrange("p (c n) -> p c n", c=4)
                scale, shift = (cmod[:, m, cond, 4 * half:4 * half + 4].unsqueeze(2).to_broadcast([P, 4, P]) for m in (3, 2))
                link(dve.tensor_tensor(v, v, scale, ALU.mult))
                dve.tensor_tensor(h2T[:, 4 * half:4 * half + 4, tt], v, shift, ALU.add).then_inc(h2_ready, 1)

            maxima(0)
            for u in range(n_units):
                g, h, t = HEAD_UNITS[u]
                n, b = key_count(g, t), u % 2
                if u + 1 < n_units:
                    maxima(u + 1)
                o, j = divmod(u - A_UNITS, HEADS)
                if o >= 2 and j == 1:
                    gate_out(o - 2)
                dve.wait_ge(exp_done, u + 1)
                if g:
                    n_sink[0] += 1
                    dve.wait_ge(sink_exp, n_sink[0])
                    link(dve.tensor_tensor(den[:, b:b + 1], den[:, b:b + 1], esink[:, b:b + 1], ALU.add))
                link(dve.reciprocal(rden[:, b:b + 1], den[:, b:b + 1]))
                dve.tensor_scalar(probs[:, b, 0:n], probs[:, b, 0:n], rden[:, b:b + 1], None, ALU.mult)\
                    .then_inc(probs_ready, 1)
                if u % 2 == 0 and u >= 4:
                    attn_out(u // 2 - 2)
                if o >= 2 and j == 0:
                    out_mean(o - 2)
                if o >= 2 and j == 1:
                    add_out(o - 2)
                if o >= 2 and j == 2:
                    x1_mean_of(o - 2)
                if o >= 2 and j in (5, 7):
                    modulate_x1(o - 2, (j - 5) // 2)
            attn_out(n_units // 2 - 2)
            attn_out(n_units // 2 - 1)
            out_mean(3)
            gate_out(3)
            add_out(3)
            x1_mean_of(3)
            modulate_x1(3, 0)
            modulate_x1(3, 1)

            def softmax(n, tiles, bank):
                k = tiles.stop - tiles.start
                lg = ps[:, bank, tiles.start * E:tiles.stop * E].rearrange("p (t e) -> p t e", t=k)
                wide = lambda v: v[:, tiles].unsqueeze(2).to_broadcast([P, k, E])
                link(dve.tensor_reduce(lmax[:, tiles], lg, AX.X, ALU.max))
                dve.tensor_tensor(logit[:, tiles, :], lg, wide(lmax), ALU.subtract).then_inc(logits_ready, 1)
                dve.wait_ge(logits_exp, n)
                link(dve.tensor_reduce(lsum[:, tiles], expl[:, tiles, :], AX.X, ALU.add))
                link(dve.reciprocal(lrec[:, tiles], lsum[:, tiles]))
                dve.tensor_tensor(expl[:, tiles, :], expl[:, tiles, :], wide(lrec), ALU.mult).then_inc(aff_ready, 1)

            def top_eight(vals, idx, part, r, cap):
                k = slice(8 * r, 8 * r + 8)
                link(dve.max(vals[:, k], part))
                link(dve.max_index(idx[:, k], vals[:, k], part))
                if 8 * r + 8 < cap:
                    link(dve.match_replace(part, vals[:, k], part, -1.0))

            dve.wait_ge(router_done, TILES - 1)
            softmax(1, slice(1, TILES), 6)
            dve.wait_ge(aff_turned, 1)
            link(dve.tensor_copy(aff[:, CTX:], ps[0:E, 2, :]))
            def context_softmax():
                dve.wait_ge(router_done, TILES)
                softmax(2, slice(0, 1), 7)

            among = {0: (lambda: gate_out(4), lambda: add_out(4)), 1: (lambda: x1_mean_of(4),), 5: (context_softmax,)}
            out_mean(4)
            for r in range(CAP_L // 8):
                top_eight(vals_l, idxu_l, aff[:, CTX:], r, CAP_L)
                for step in among.get(r, ()):
                    step()
            dve.wait_ge(aff_turned, 2)
            link(dve.tensor_copy(aff[:, 0:CTX], ps[0:E, 3, 0:CTX]))
            for r in range(CAP_C // 8):
                top_eight(vals_c, idxu_c, aff[:, 0:CTX], r, CAP_C)
            link(dve.tensor_copy(idxf_l, idxu_l))
            link(dve.tensor_copy(idxf_c, idxu_c))
            dve.wait_ge(pad_set, 3)
            for h in (0, 1):
                o = h * CAP_L
                dve.tensor_scalar(lists[:, 0, o:o + CAP_L], idxf_l, 2.0, float(h), ALU.mult, ALU.add)
                dve.tensor_copy(lists[:, 1, o:o + CAP_L], vals_l)
            for q in range(4):
                o = q * CPAD
                dve.tensor_scalar(lists[:, 2, o:o + CAP_C], idxf_c, 4.0, float(q), ALU.mult, ALU.add)
                last = dve.tensor_copy(lists[:, 3, o:o + CAP_C], vals_c)
            last.then_inc(lists_ready, 1)
            dve.wait_ge(lists_turned, 1)
            turned = ps[:, 7, 0:4 * E].rearrange("p (a e) -> p a e", a=4)
            dve.tensor_copy(row_l[:, 0:E], turned[:, 0, :])
            dve.tensor_copy(g_l, turned[:, 1, :]).then_inc(y_ready, 1)
            dve.tensor_copy(row_c[:, 0:E], turned[:, 2, :])
            dve.tensor_copy(g_c, turned[:, 3, :]).then_inc(rows_ready, 1)

            def modulate(n, odd):
                dve.wait_ge(xe_turned, n + 1)
                tx = ps[:, 5, :].rearrange("p (j h s) -> p j h s", j=4, h=2)
                tc = ps[:, 6, 0:QUART].rearrange("p (j q s) -> p j q s", j=2, q=4)
                by_l = [cmod[:, m, 1, :].rearrange("p (h j) -> p j h", h=2).unsqueeze(3).to_broadcast([P, 4, 2, CAP_L])
                        for m in (2, 3)]
                by_c = [cmod[:, m, 0, :].rearrange("p (q j) -> p j q", q=4).unsqueeze(3).to_broadcast([P, 2, 4, CPAD])
                        for m in (2, 3)]
                dve.tensor_tensor(xT_l[odd], tx, by_l[1], ALU.mult)
                dve.tensor_tensor(xT_c[odd], tc, by_c[1], ALU.mult).then_inc(xe_scaled, 1)
                dve.wait_ge(xe_scaled, n + 1)
                dve.tensor_tensor(xT_l[odd], xT_l[odd], by_l[0], ALU.add)
                dve.tensor_tensor(xT_c[odd], xT_c[odd], by_c[0], ALU.add).then_inc(xe_ready, 1)

            def activations(e):
                dve.wait_ge(up_c, e + 1)
                dve.wait_ge(silu_done, e * 2 + 2)
                dve.tensor_tensor(a_c, s_c, ps[:, 2, QUART:], ALU.mult).then_inc(act_c_ready, 1)
                dve.wait_ge(up_b, e + 1)
                dve.tensor_tensor(a_l, s_l, ps[:, 1, :], ALU.mult).then_inc(act_l_ready, 1)

            def weigh(e):
                dve.wait_ge(down_b, e + 1)
                dve.wait_ge(added_l, e * 16 + 16)
                dve.wait_ge(added_c, e * 16 + 16)
                dve.tensor_scalar(y_l, ps[:, 3, :], g_l[:, bass.ds(e, 1)], None, ALU.mult)
                dve.tensor_scalar(y_c, ps[:, 4, 0:QUART], g_c[:, bass.ds(e, 1)], None, ALU.mult).then_inc(y_ready, 1)

            modulate(0, 0)
            with dve.Fori(0, E // 2) as pair:
                for odd in (0, 1):
                    modulate(pair * 2 + odd + 1, 1 - odd)
                    activations(pair * 2 + odd)
                    weigh(pair * 2 + odd)

            def last_gated(t):
                dve.wait_ge(f_squared, t + 1)
                dve.tensor_scalar(msf[:, t:t + 1], ssf[:, t:t + 1], 1.0 / D, EPS, ALU.mult, ALU.add).then_inc(f_mean, 1)
                dve.tensor_tensor(total[:, t, :], total[:, t, :], gate_rows[:, min(t, 1), :], ALU.mult).then_inc(f_gated, 1)

            def last_sum(t):
                dve.wait_ge(f_rstd, t + 1)
                dve.wait_ge(f_gated, t + 1)
                dve.scalar_tensor_tensor(total[:, t, :], total[:, t, :], rsf[:, t:t + 1], xr[:, t, :],
                                         ALU.mult, ALU.add).then_inc(f_ready, 1)

            for t in range(TILES):
                last_gated(t)
                if t:
                    last_sum(t - 1)
            last_sum(TILES - 1)

        @block.gpsimd
        def _(pool):
            pool.memset(zeros, 0.0).then_inc(zeros_set, 1)
            pool.memset(kt[:, :], 0.0).then_inc(kt_cleared, 1)
            pool.wait_ge(mhalf_set, 1)

            def root(dst, mean, n, ready, done, count):
                pool.wait_ge(ready, count)
                pool.tensor_tensor(dst, mean, mhalf[:, 0:n], ALU.pow).then_inc(done, 1)

            for t in range(TILES):
                root(rs1[:, t:t + 1], ms1[:, t:t + 1], 1, x_mean, x_rstd, t + 1)
            pool.wait_ge(proj_done, 1)
            pool.wait_ge(zeros_set, 1)
            pool.dma_start(sum_l.rearrange("(p a) (b n) -> p (a b) n", p=P, n=QUART),
                           zeros.unsqueeze(1).to_broadcast([P, 16, QUART])).then_inc(added_l, 16)
            pool.dma_start(sum_c.rearrange("(p a) n -> p a n", p=64),
                           zeros[0:64].unsqueeze(1).to_broadcast([64, CTX_ROWS // 64, QUART])).then_inc(added_c, 16)
            pool.dma_start(rows_c[4 * CTX:CTX_ROWS], zeros[0:CTX_ROWS - 4 * CTX]).then_inc(pad_cleared, 16)
            for i in range(2 * TILES):
                heads = 2 if i < TILES else HEADS
                root(rsh[:, 0:heads], msh[:, 0:heads], heads, head_mean, head_rstd, i + 1)
            for o, t in enumerate(OUT_ORDER):
                root(rso[:, t:t + 1], mso[:, t:t + 1], 1, o_mean, o_rstd, o + 1)
                root(rs2[:, t:t + 1], ms2[:, t:t + 1], 1, x1_mean, x1_rstd, o + 1)

            pool.wait_ge(scores_done, len(HEAD_UNITS))
            pool.iota(lists[:, 2, :].rearrange("e (q r) -> e q r", q=4)[:, :, CAP_C:], [[CPAD - CAP_C, 4], [1, CPAD - CAP_C]],
                      base=4 * CTX, channel_multiplier=0, allow_small_or_imprecise_dtypes=True).then_inc(pad_set, 1)
            pool.memset(lists[:, 3, :].rearrange("e (q r) -> e q r", q=4)[:, :, CAP_C:], 0.0).then_inc(pad_set, 1)
            pool.memset(kt[:, 1800:1840].bitcast(I32), 0).then_inc(pad_set, 1)

            def hold(pool):
                pool.tensor_tensor(held, mhalf[:, 0:1], mhalf[:, 1:2], ALU.add).then_inc(held_ops, 1)

            def gather(n):
                pool.tensor_copy(get_l, row_l[:, bass.ds(n, 1)])
                pool.tensor_copy(get_c, row_c[:, bass.ds(n, 1)]).then_inc(get_copied, 1)
                pool.wait_ge(get_copied, n + 1)
                hold(pool)
                pool.indirect_dma_start(xg_l, None, rows_l, bass.IndirectOffsetOnAxis(ap=get_l, axis=0))\
                    .then_inc(gathered_l, 16)
                pool.indirect_dma_start(xg_c, None, rows_c, bass.IndirectOffsetOnAxis(ap=get_c, axis=0))\
                    .then_inc(gathered_c, 16)

            pool.wait_ge(rows_ready, 1)
            pool.wait_ge(rows_stored, 16 * TILES)
            pool.wait_ge(pad_cleared, 16)
            gather(0)
            pool.wait_ge(xe_turned, 1)
            gather(1)
            with pool.Fori(0, E) as e:
                pool.wait_ge(xe_turned, e + 2)
                gather(e + 2)
                pool.wait_ge(added_l, e * 16 + 16)
                pool.wait_ge(added_c, e * 16 + 16)
                pool.tensor_copy(put_l, row_l[:, bass.ds(e, 1)])
                pool.tensor_copy(put_c, row_c[:, bass.ds(e, 1)]).then_inc(put_copied, 1)
                pool.wait_ge(put_copied, e + 1)
                pool.wait_ge(y_ready, e + 2)
                hold(pool)
                pool.indirect_dma_start(sum_l, bass.IndirectOffsetOnAxis(ap=put_l, axis=0), y_l, None,
                                        compute_op=ALU.add).then_inc(added_l, 16)
                pool.indirect_dma_start(sum_c, bass.IndirectOffsetOnAxis(ap=put_c, axis=0), y_c, None,
                                        compute_op=ALU.add).then_inc(added_c, 16)
            pool.wait_ge(added_l, 16 * (E + 1))
            pool.wait_ge(added_c, 16 * (E + 1))
            for t in range(TILES):
                root(rsf[:, t:t + 1], msf[:, t:t + 1], 1, f_mean, f_rstd, t + 1)


_INS = ["x_prompt", "x_sample", "cache_a_k", "cache_a_v", "cache_b_k", "cache_b_v", "w_ada", "b_ada",
        "w_in", "g_qa", "g_ka", "sink_b", "w_out", "g_post_attn", "w_router", "w_gate",
        "w_up", "w_down", "g_post_ffn"]
_OUTS = [(1, CTX, D), (1, LAT, D)] + [(1, 1, CTX, 2, DH)] * 4
GRID_W = 64
ROPE_THETA = 10000.0


def shape_constants():
    half = DH // 4
    freqs = (np.float32(ROPE_THETA) ** (-np.arange(half, dtype=np.float32) / np.float32(half))).astype(np.float32)
    pos = np.arange(LAT)
    tables = np.zeros((2, LAT, DH), np.float32)
    for a, where in enumerate((pos // GRID_W, pos % GRID_W)):
        ang = where.astype(np.float32)[:, None] * freqs[None, :]
        cos, sin = np.cos(ang).astype(np.float32), np.sin(ang).astype(np.float32)
        o = 2 * half * a
        tables[0, :, o:o + half], tables[0, :, o + half:o + 2 * half] = cos, cos
        tables[1, :, o:o + half], tables[1, :, o + half:o + 2 * half] = -sin, sin
    q, k = np.arange(P)[:, None], np.arange(P)[None, :]
    masks = np.zeros((2, P, P), np.float32)
    masks[0][k < q] = NEG
    masks[1][k > q] = NEG
    return {"identity": np.eye(P, dtype=np.float32), "rope_tables": tables, "window_masks": masks}


def column_layouts(inputs):
    c = [np.asarray(inputs["c_ctx"]).reshape(P, KC), np.asarray(inputs["c"]).reshape(P, KC)]
    g = [np.asarray(inputs[n]).reshape(KC, P).T for n in ("g_pre_attn", "g_pre_ffn")]
    return {"c_columns": np.ascontiguousarray(np.concatenate(c, axis=1)),
            "g_pre_columns": np.ascontiguousarray(np.concatenate(g, axis=1))}


def kernel(**inputs):
    import concourse.bacc as bacc
    from concourse.bass_utils import run_bass_kernel_spmd

    nc = bacc.Bacc("TRN2", target_bir_lowering=False, num_devices=1)
    arrays, handles = {}, {}
    given = {name: np.ascontiguousarray(inputs[name]) for name in _INS}
    for name, a in {**given, **column_layouts(inputs), **shape_constants()}.items():
        arrays[f"in_{name}"] = a
        handles[name] = nc.dram_tensor(f"in_{name}", a.shape, mybir.dt.from_np(a.dtype), kind="ExternalInput").ap()
    outs = [nc.dram_tensor(f"out_{i}", s, F32, kind="ExternalOutput").ap() for i, s in enumerate(_OUTS)]
    build(nc, handles, outs)
    r = run_bass_kernel_spmd(nc, [arrays], core_ids=[0])
    return tuple(r.results[0][f"out_{i}"] for i in range(len(_OUTS)))
```

```python
from contextlib import ExitStack

import numpy as np

import concourse.bass as bass
from concourse import mybir

F32 = mybir.dt.float32
F32R = mybir.dt.float32r
I32 = mybir.dt.int32
U32 = mybir.dt.uint32
ALU = mybir.AluOpType
ACT = mybir.ActivationFunctionType
AX = mybir.AxisListType

P = 128
D = 1024
KC = D // P
CTX = 128
LAT = 512
TILES = (CTX + LAT) // P
LT = LAT // P
TOK = CTX + LAT
DH = 64
HEADS = 8
PAIRS = HEADS // 2
E = 16
CAP_L = 2 * LAT // E
CAP_C = 2 * CTX // E
CPAD = 32
HALF = D // 2
QUART = D // 4
N_MOD = 6
EPS = 1e-6
SLOTS = 6
UNIT = 4096
NEG = -1e30
CTX_ROWS = 4 * CTX + 4 * (CPAD - CAP_C)

UNITS = ([("ada", m, h) for m in (0, 1) for h in (0, 1)] + [("win", 0, 0), ("win", 1, 0)]
         + [("ada", m, h) for m in (2, 3) for h in (0, 1)] + [("ada", 4, 0), ("win", 2, 0)]
         + [("ada", 4, 1), ("ada", 5, 0), ("ada", 5, 1)] + [("wout", 0, h) for h in (0, 1)])
UNIT_SLOT = [1, 2, 3, 4, 5, 0, 2, 3, 4, 2, 3, 5, 4, 2, 3, 4, 5]
ADA_AFTER = {2: 2, 5: 3, 8: 4, 11: 5}
COLS = {0: 0, 1: 1, 3: 2, 4: 3}
OUT_ORDER = [1, 2, 3, 4, 0]
HEAD_UNITS = ([(0, h, t) for t in range(TILES) for h in range(HEADS)]
              + [(1, h, t) for t in OUT_ORDER for h in range(HEADS)])
A_UNITS = TILES * HEADS
POOL_GATED = (0, 2)


def slot_of(u):
    return UNIT_SLOT[u]


def unit_before(u, s):
    return max((v for v in range(u) if slot_of(v) == s), default=None)


def key_parts(g, t):
    if t == 0:
        return [(0, TOK, CTX)]
    if g == 0:
        return [(0, 0, 512), (512, 512, TOK - 512)]
    lo, hi = max(0, t - 2), min(LT - 1, t)
    return [(0, 0, CTX), (CTX, CTX + lo * P, (hi + 1 - lo) * P)]


def key_count(g, t):
    return sum(n for _, _, n in key_parts(g, t))


def value_blocks(g, t):
    if t == 0:
        return [4]
    if g == 0:
        return [-1, 0, 1, 2, 3]
    return [-1] + list(range(max(0, t - 2), min(LT - 1, t) + 1))


def build(nc, A, out):
    ctx = ExitStack()
    with ctx:
        def sb(name, n, dt=F32):
            return ctx.enter_context(nc.sbuf_tensor(name, [P, n], dt))

        def sb_over(name, n, offset):
            return nc.alloc_sbuf_tensor_at(name, [P, n], F32R, offset=offset)

        def next_offset():
            return -(-nc.sbuf_base // 32) * 32

        def sem(name):
            return ctx.enter_context(nc.semaphore(name))

        def dram(name, shape):
            return nc.dram_tensor(name, shape, F32, kind="Internal").ap()

        ring_offset = next_offset()
        ring = sb("ring", SLOTS * UNIT)
        reg1 = sb("reg1", KC * TOK)
        qt_offset = next_offset() + 4 * KC * TOK
        reg2_qt = sb("reg2_qt", KC * TOK + 2 * PAIRS * TOK)
        reg2, qt = reg2_qt[:, 0:KC * TOK], reg2_qt[:, KC * TOK:]
        reg3 = sb("reg3", KC * TOK)
        kt_offset = next_offset()
        kt = sb("kt", 2 * 2 * (TOK + CTX))
        v_lat = sb("v_lat", LT * 256)
        kv_ctx = sb("kv_ctx", 512)
        cache = sb("cache", 4 * P)
        ident = sb("ident", P)
        mod = sb("mod", N_MOD * QUART)
        gpost = sb("gpost", 2 * QUART)
        gpre = sb("gpre", 2 * KC)
        colmod = sb("colmod", 4 * 2 * KC)
        wr = sb("wr", KC * E)
        cvec = sb("cvec", 2 * KC)
        gqk = sb("gqk", 2 * DH)
        sink = sb("sink", HEADS)
        nsink = sb("nsink", HEADS)
        small = sb("small", 160)
        mhalf = sb("mhalf", 16)
        held = small[:, 110:111]

        def ring_slot(s):
            if s >= SLOTS:
                return reg2_qt[:, (s - SLOTS) * UNIT:(s - SLOTS + 1) * UNIT]
            return ring[:, s * UNIT:(s + 1) * UNIT]

        x_in = reg1[:, :].rearrange("p (t d) -> p t d", t=TILES)
        hT = reg2.rearrange("p (c n) -> p c n", c=KC)
        attnT = reg1[:, :].rearrange("p (c n) -> p c n", c=KC)
        h2T = attnT
        xn = reg2.rearrange("p (t d) -> p t d", t=TILES)
        xr = reg3[:, :].rearrange("p (t d) -> p t d", t=TILES)
        total = xn
        nat = reg3[:, 0:1024].rearrange("p (b n) -> p b n", b=2)
        sq = reg3[:, 1024:1536]
        rot = reg3[:, 1536:2560].rearrange("p (b n) -> p b n", b=2)
        rot2 = reg3[:, 2560:3072]
        rope = reg3[:, 3072:3584].rearrange("p (a t d) -> p a t d", a=2, t=LT)
        ropeq = reg3[:, 3584:4096].rearrange("p (a t d) -> p a t d", a=2, t=LT)
        silu = reg3[:, 4352:4608].rearrange("p (c m) -> p c m", c=KC)
        rot3 = reg3[:, 4608:5120]
        split = reg1[:, 0:2048].rearrange("p (b n) -> p b n", b=2)
        buffers = ring[:, 2 * UNIT:4 * UNIT]
        probs = buffers[:, 0:1920].rearrange("p (b n) -> p b n", b=3)
        pT = buffers[:, 1920:4480].rearrange("p (b h n) -> p b h n", b=2, h=2)
        masks = buffers[:, 4480:4736].rearrange("p (a j) -> p a j", a=2)
        q_a, k_a = sb_over("q_a", HEADS * TOK, qt_offset), sb_over("k_a", 4 * (TOK + CTX), kt_offset)
        q_b = sb_over("q_b", HEADS * TOK, ring_offset)
        k_b = sb_over("k_b", 4 * (TOK + CTX), ring_offset + 4 * HEADS * TOK)
        qT = [v[:, :].rearrange("p (h n) -> p h n", h=HEADS) for v in (q_a, q_b)]
        kT = [v[:, :].rearrange("p (b n) -> p b n", b=4) for v in (k_a, k_b)]
        vl = v_lat[:, :].rearrange("p (t n) -> p t n", t=LT)
        gate_rows = qt[:, 3072:3072 + 2 * D].rearrange("p (c n) -> p c n", c=2)
        cmod = colmod[:, :].rearrange("p (m c k) -> p m c k", m=4, c=2)
        modq = mod[:, :].rearrange("p (m n) -> p m n", m=N_MOD)
        ss1, ms1, rs1 = small[:, 0:5], small[:, 5:10], small[:, 10:15]
        sso, mso, rso = small[:, 15:20], small[:, 20:25], small[:, 25:30]
        ss2, ms2, rs2 = small[:, 30:35], small[:, 35:40], small[:, 40:45]
        ssh, msh, rsh = small[:, 45:53], small[:, 53:61], small[:, 61:69]
        mx, negm, den, rden, esink = (small[:, 69 + 2 * i:71 + 2 * i] for i in range(5))
        lmax, lsum, lrec = small[:, 80:85], small[:, 85:90], small[:, 90:95]
        ssf, msf, rsf = small[:, 95:100], small[:, 100:105], small[:, 105:110]
        logit = kt[:, 0:80].rearrange("p (t e) -> p t e", t=TILES)
        expl = kt[:, 80:160].rearrange("p (t e) -> p t e", t=TILES)
        affs = [kt[0:E, 256:256 + TOK], kt[0:E, 2048:2048 + TOK]]
        vals_l, vals_c = kt[0:E, 1024:1024 + CAP_L], kt[0:E, 1088:1088 + CAP_C]
        idxu_l = kt[0:E, 1104:1104 + CAP_L].bitcast(U32)
        idxu_c = kt[0:E, 1168:1168 + CAP_C].bitcast(U32)
        idxf_l, idxf_c = kt[0:E, 1184:1184 + CAP_L], kt[0:E, 1248:1248 + CAP_C]
        lists = kt[0:E, 1280:1280 + 4 * P].rearrange("e (a r) -> e a r", a=4)
        row_l = kt[:, 1800:1800 + E + 2].bitcast(I32)
        row_c = kt[:, 1820:1820 + E + 2].bitcast(I32)
        g_l, g_c = kt[:, 1840:1840 + E], kt[:, 1856:1856 + E]
        get_l, get_c = kt[:, 1872:1873].bitcast(I32), kt[:, 1873:1874].bitcast(I32)
        put_l, put_c = kt[:, 1874:1875].bitcast(I32), kt[:, 1875:1876].bitcast(I32)
        xg_l, xg_c = reg1[:, 0:512], reg1[:, 512:768]
        xT_l = [v.rearrange("p (j h s) -> p j h s", j=4, h=2) for v in (reg1[:, 768:1280], kt[:, 2048:2560])]
        xT_c = [v.rearrange("p (j q s) -> p j q s", j=2, q=4) for v in (reg1[:, 1280:1536], kt[:, 2560:2816])]
        s_l, s_c = reg1[:, 1536:2048], reg1[:, 2048:2304]
        a_l, a_c = reg1[:, 2304:2816], reg1[:, 2816:3072]
        aT_l = reg1[:, 3072:3584].rearrange("p (j h s) -> p j h s", j=4, h=2)
        aT_c = reg1[:, 3584:3840].rearrange("p (j q s) -> p j q s", j=2, q=4)
        y_l, y_c = reg1[:, 3840:4352], reg1[:, 4352:4608]
        squares = x_in
        zeros = qt[:, 0:QUART]

        rows_l, rows_c = dram("rows_l", [2 * LAT, HALF]), dram("rows_c", [CTX_ROWS, QUART])
        sum_l, sum_c = dram("sum_l", [2 * LAT, HALF]), dram("sum_c", [CTX_ROWS, QUART])

        ps = ctx.enter_context(nc.psum_tensor("ps", [P, 8, 512], F32))
        flat = ps[:, :, :].rearrange("p b n -> p (b n)")

        def out_at(o):
            return ps[:, 5:7, :] if o % 2 else ps[:, 2:4, :]

        two = [flat[:, 0:1024], flat[:, 1024:2048], flat[:, 2048:3072]]

        def scores_at(u):
            return two[u % 2] if u < A_UNITS else ps[:, u % 2, :]

        def part_sources(k):
            b = k % 2
            s, t = divmod(k - 1, TILES)
            if k == 0 or s == 0:
                for g in (0, 1):
                    if k == 0:
                        src = cache[:, 2 * g * P:(2 * g + 1) * P]
                    elif t == 0:
                        src = kv_ctx[:, 256 * g:256 * g + P]
                    else:
                        src = rot[:, (k - 1) % 2, g * P:(g + 1) * P]
                    dst = split[:, b, 512 * g:512 * g + 512].rearrange("p (v r u d) -> p r v u d", v=2, r=2, u=2)
                    yield src.rearrange("p (v d) -> p v d", v=2).unsqueeze(2).to_broadcast([P, 2, 2, DH]), dst
            else:
                yield (rot[:, (k - 1) % 2, :].rearrange("p (h d) -> p h d", d=DH),
                       split[:, b, :].rearrange("p (h r d) -> p r h d", h=HEADS, r=2))

        cond_in, early_in, consts_in = sem("cond_in"), sem("early_in"), sem("consts_in")
        x_loaded = [sem(f"x_loaded{t}") for t in range(TILES)]
        slot_in = [sem(f"slot_in{s}") for s in range(SLOTS + 2)]
        zeros_set, pad_cleared = sem("zeros_set"), sem("pad_cleared")
        mhalf_set = sem("mhalf_set")
        high_ready, split_ready = sem("high_ready"), sem("split_ready")
        silu_cleared, silu_ready = sem("silu_cleared"), sem("silu_ready")
        x_squared, x_mean, x_rstd, x_normed = sem("x_squared"), sem("x_mean"), sem("x_rstd"), sem("x_normed")
        ada_half, ada_done, mod_ready = sem("ada_half"), sem("ada_done"), sem("mod_ready")
        modcol_done, modcol_ready = sem("modcol_done"), sem("modcol_ready")
        xt_done, ht_ready, htc_ready = sem("xt_done"), sem("ht_ready"), sem("htc_ready")
        proj_done, nat_ready, sq_ready = sem("proj_done"), sem("nat_ready"), sem("sq_ready")
        head_mean, head_rstd, rot_ready = sem("head_mean"), sem("head_rstd"), sem("rot_ready")
        qk_turned, qkT_ready, qkT_act = sem("qk_turned"), sem("qkT_ready"), sem("qkT_act")
        scores_done, negmax_ready, exp_done = sem("scores_done"), sem("negmax_ready"), sem("exp_done")
        sink_exp, probs_ready = sem("sink_exp"), sem("probs_ready")
        probs_turned, pT_ready, pv_done, attn_ready = (sem("probs_turned"), sem("pT_ready"), sem("pv_done"),
                                                      sem("attn_ready"))
        gate_gained, gate_cast, gate_ready = sem("gate_gained"), sem("gate_cast"), sem("gate_ready")
        x_again, masks_in = sem("x_again"), sem("masks_in")
        wout_done = sem("wout_done")
        o_squared, o_mean, o_rstd, o_scaled = sem("o_squared"), sem("o_mean"), sem("o_rstd"), sem("o_scaled")
        x1_ready, x1_squared, x1_mean, x1_rstd = sem("x1_ready"), sem("x1_squared"), sem("x1_mean"), sem("x1_rstd")
        xn_ready, xn_turned, h2_ready, router_done = (sem("xn_ready"), sem("xn_turned"), sem("h2_ready"),
                                                      sem("router_done"))
        rows_stored = sem("rows_stored")
        logits_ready, logits_exp, aff_ready, aff_turned = (sem("logits_ready"), sem("logits_exp"),
                                                           sem("aff_ready"), sem("aff_turned"))
        lists_ready, lists_turned, rows_ready = sem("lists_ready"), sem("lists_turned"), sem("rows_ready")
        pad_set = sem("pad_set")
        get_copied, gathered_l, gathered_c = sem("get_copied"), sem("gathered_l"), sem("gathered_c")
        put_copied, added_l, added_c = sem("put_copied"), sem("added_l"), sem("added_c")
        xe_turned, xe_scaled, xe_ready = sem("xe_turned"), sem("xe_scaled"), sem("xe_ready")
        gate_a, gate_b, up_a, up_b, down_a, down_b = (sem(n) for n in (
            "gate_a", "gate_b", "up_a", "up_b", "down_a", "down_b"))
        up_c, silu_done = sem("up_c"), sem("silu_done")
        act_l_ready, act_l_turned = sem("act_l_ready"), sem("act_l_turned")
        act_c_ready, act_c_turned = sem("act_c_ready"), sem("act_c_turned")
        actT_l_ready, actT_c_ready, y_ready = sem("actT_l_ready"), sem("actT_c_ready"), sem("y_ready")
        sum_in = [sem(f"sum_in{t}") for t in range(TILES)]
        f_squared, f_mean, f_rstd = sem("f_squared"), sem("f_mean"), sem("f_rstd")
        f_gated, f_gated_pool, f_ready = sem("f_gated"), sem("f_gated_pool"), sem("f_ready")
        stored = sem("stored")
        dve_step, held_ops = sem("dve_step"), sem("held_ops")

        N_EARLY = 6
        N_CONSTS = 17
        LOADS = [sum((2 if UNITS[v][:2] == ("win", 0) else 1) for v in range(len(UNITS)) if slot_of(v) == s)
                 for s in range(SLOTS)]
        block = ctx.enter_context(nc.Block())

        @block.sync
        def _(sp):
            sp.dma_start(cvec[:, :], A["c_columns"]).then_inc(cond_in, 16)

            freed = []
            n_half = n_ada = 0
            for kind, m, h in UNITS:
                if kind == "ada" and h == 0:
                    n_half += 1
                    freed.append((ada_half, n_half))
                elif kind == "ada":
                    n_ada += 1
                    freed.append((ada_done, n_ada))
                elif kind == "win":
                    freed.append((proj_done, TILES * (m + 1)))
                else:
                    freed.append((wout_done, TILES))
            for u, (kind, m, h) in enumerate(UNITS):
                dst = ring_slot(slot_of(u))
                before = unit_before(u, slot_of(u))
                if before is not None:
                    sp.wait_ge(*freed[before])
                if u == 2:
                    for t in range(TILES):
                        src = A["x_prompt"][0] if t == 0 else A["x_sample"][0, (t - 1) * P:t * P]
                        sp.dma_start(x_in[:, t, :], src).then_inc(x_loaded[t], 16)
                if kind == "ada":
                    src = A["w_ada"][0].rearrange("(p c) n -> p c n", c=KC)[:, 4 * h:4 * h + 4, m * D:(m + 1) * D]
                    sp.dma_start(dst.rearrange("p (c n) -> p c n", c=4), src).then_inc(slot_in[slot_of(u)], 16)
                elif kind == "win":
                    w = A["w_in"][0].rearrange("(c p) n -> p c n", p=P)
                    d = dst.rearrange("p (c n) -> p c n", c=KC)
                    if m == 0:
                        sp.dma_start(d[:, :, 0:256], w[:, :, 512:768]).then_inc(slot_in[slot_of(u)], 16)
                        sp.dma_start(d[:, :, 256:512], w[:, :, 1280:1536]).then_inc(slot_in[slot_of(u)], 16)
                    else:
                        first = 0 if m == 1 else 768
                        sp.dma_start(d, w[:, :, first:first + 512]).then_inc(slot_in[slot_of(u)], 16)
                else:
                    src = A["w_out"][0].rearrange("(c p) n -> p c n", p=P)[:, 4 * h:4 * h + 4, :]
                    sp.dma_start(dst.rearrange("p (c n) -> p c n", c=4), src).then_inc(slot_in[slot_of(u)], 16)

            sp.wait_ge(qkT_ready, 3 * TILES + 1)
            sp.wait_ge(ada_done, N_MOD)
            sp.dma_start(masks, A["window_masks"].rearrange("a p j -> p a j")).then_inc(masks_in, 16)
            for t in range(TILES):
                src = A["x_prompt"][0] if t == 0 else A["x_sample"][0, (t - 1) * P:t * P]
                sp.dma_start(xr[:, t, :], src).then_inc(x_again, 16)

            def expert_weight(e, kind, half, s):
                w = (A["w_gate"], A["w_up"], A["w_down"])[kind]
                src = w[0].rearrange("e (c p) n -> e p c n", p=P)[e][:, 4 * half:4 * half + 4, :]
                sp.dma_start(ring_slot(s).rearrange("p (c n) -> p c n", c=4), src).then_inc(slot_in[s], 16)

            for s in range(SLOTS):
                sp.wait_ge(*freed[unit_before(len(UNITS), s)])
                if s == 0:
                    sp.wait_ge(pv_done, len(HEAD_UNITS) // 2)
                expert_weight(0, s // 2, s % 2, s)
            sp.wait_ge(scores_done, len(HEAD_UNITS))
            sp.wait_ge(rows_stored, 16 * TILES)
            sp.wait_ge(xn_turned, 2 * TILES)
            for half in (0, 1):
                expert_weight(1, 0, half, SLOTS + half)

            def refill(e, kind, odd=False):
                used = ((gate_a, gate_b), (up_a, up_b), (down_a, down_b))[kind]
                for half in (0, 1):
                    sp.wait_ge(used[half], e - 1 if kind == 0 else e)
                    expert_weight(e, kind, half, SLOTS + half if odd else 2 * kind + half)

            refill(2, 0)
            with sp.Fori(0, E // 2 - 2) as pair:
                for odd in (0, 1):
                    refill(pair * 2 + odd + 1, 1)
                    refill(pair * 2 + odd + 3, 0, odd=not odd)
                    refill(pair * 2 + odd + 1, 2)
            for e in range(E - 3, E):
                refill(e, 1)
                if e + 2 < E:
                    refill(e + 2, 0, odd=True)
                refill(e, 2)

            sp.wait_ge(added_l, 16 * (E + 1))
            sp.wait_ge(added_c, 16 * (E + 1))
            for t in range(TILES):
                src = (sum_c[0:4 * CTX].rearrange("(p q) n -> p (q n)", q=4) if t == 0 else
                       sum_l[2 * (t - 1) * P:2 * t * P].rearrange("(p q) n -> p (q n)", q=2))
                sp.dma_start(total[:, t, :], src).then_inc(sum_in[t], 16)

        @block.tensor
        def _(pe):
            def landed(u):
                loads = sum((2 if UNITS[v][:2] == ("win", 0) else 1) for v in range(u + 1) if slot_of(v) == slot_of(u))
                pe.wait_ge(slot_in[slot_of(u)], 16 * loads)

            def unit_at(u, c):
                return ring_slot(slot_of(u)).rearrange("p (c n) -> p c n", c=c)

            ada_units = [u for u, x in enumerate(UNITS) if x[0] == "ada"]
            win_units = [u for u, x in enumerate(UNITS) if x[0] == "win"]
            wout_units = [u for u, x in enumerate(UNITS) if x[0] == "wout"]

            def ada(m):
                if m:
                    pe.wait_ge(mod_ready, m)
                for h in (0, 1):
                    u = ada_units[2 * m + h]
                    landed(u)
                    w = unit_at(u, 4)
                    for c in range(4):
                        for q in range(4):
                            last = pe.matmul(ps[32 * q:32 * q + 32, 4, 0:QUART], silu[:, 4 * h + c, :],
                                             w[:, c, q * QUART:(q + 1) * QUART],
                                             start=(h == 0 and c == 0), stop=(h == 1 and c == 3))
                    last.then_inc(ada_done if h else ada_half, 1)

            def mod_columns(n, m):
                pe.wait_ge(mod_ready, m + 1)
                if n:
                    pe.wait_ge(modcol_ready, n)
                for j in range(2):
                    last = pe.transpose(ps[:, 7, j * P:(j + 1) * P], modq[:, m, j * P:(j + 1) * P], ident[:, :])
                last.then_inc(modcol_done, 1)

            pe.wait_ge(silu_ready, 1)
            ada(0)
            pe.wait_ge(early_in, 16 * N_EARLY)
            mod_columns(0, 0)
            def turn_x(c):
                if c >= 2:
                    pe.wait_ge(ht_ready, c - 1)
                    pe.wait_ge(htc_ready, c - 1)
                for t in range(TILES):
                    if c == 0:
                        pe.wait_ge(x_normed, t + 1)
                    o = ps[:, 5 + c % 2, 0:P] if t == 0 else ps[:, 2 + c % 2, (t - 1) * P:t * P]
                    last = pe.transpose(o, x_in[:, t, c * P:(c + 1) * P], ident[:, :])
                last.then_inc(xt_done, 1)
            turn_x(0)
            turn_x(1)
            ada(1)
            mod_columns(1, 1)
            def project(i):
                s, t = divmod(i, TILES)
                if i == 1:
                    pe.wait_ge(ht_ready, KC)
                if t == 0:
                    landed(win_units[s])
                if i >= 2:
                    pe.wait_ge(nat_ready, i - 1)
                w = unit_at(win_units[s], KC)
                for c in range(KC):
                    if i == 0:
                        if c + 2 < KC:
                            turn_x(c + 2)
                        pe.wait_ge(htc_ready, c + 1)
                    last = pe.matmul(ps[:, i % 2, :], hT[:, c, t * P:(t + 1) * P], w[:, c, :],
                                     start=(c == 0), stop=(c == KC - 1))
                last.then_inc(proj_done, 1)

            def turned_banks(k):
                return (2, 3) if k % 2 == 0 else (5, 6)

            def turn_qk(k):
                pe.wait_ge(split_ready, k + 1)
                if k < 2:
                    pe.wait_ge(htc_ready, KC)
                else:
                    pe.wait_ge(qkT_ready, k - 1)
                    pe.wait_ge(qkT_act, k - 1)
                for b in range(8):
                    last = pe.transpose(ps[:, turned_banks(k)[b // 4], (b % 4) * P:(b % 4 + 1) * P],
                                        split[:, k % 2, b * P:(b + 1) * P], ident[:, :])
                last.then_inc(qk_turned, 1)

            for i in range(3 * TILES):
                project(i)
                if i == 1:
                    turn_qk(0)
                if i >= 2:
                    turn_qk(i - 1)
                if i in ADA_AFTER:
                    ada(ADA_AFTER[i])
                if i - 2 in ADA_AFTER and ADA_AFTER[i - 2] in COLS:
                    mod_columns(COLS[ADA_AFTER[i - 2]], ADA_AFTER[i - 2])
            turn_qk(3 * TILES - 1)

            def scores(u):
                g, h, t = HEAD_UNITS[u]
                if u in (0, A_UNITS):
                    pe.wait_ge(qkT_ready, (2 + g) * TILES + 1)
                    pe.wait_ge(qkT_act, (2 + g) * TILES + 1)
                if u == 0:
                    pe.wait_ge(nat_ready, 3 * TILES)
                if u == 1:
                    pe.wait_ge(qkT_ready, 3 * TILES)
                    pe.wait_ge(qkT_act, 3 * TILES)
                if u >= 2:
                    pe.wait_ge(exp_done, u - 1)
                for at, k0, n in key_parts(g, t):
                    for part in (0, 1):
                        last = pe.matmul(scores_at(u)[:, at:at + n], qT[g][:, h, t * P:(t + 1) * P],
                                         kT[g][:, 2 * (h // 4) + part, k0:k0 + n], start=(part == 0), stop=(part == 1))
                last.then_inc(scores_done, 1)

            def turn_probs(u):
                g, h, t = HEAD_UNITS[u]
                pe.wait_ge(probs_ready, u + 1)
                if u == 0:
                    pe.wait_ge(mod_ready, N_MOD)
                if u:
                    pe.wait_ge(pT_ready, u)
                for b in range(key_count(g, t) // P):
                    last = pe.transpose(two[2][:, b * P:(b + 1) * P], probs[:, u % 3, b * P:(b + 1) * P], ident[:, :])
                last.then_inc(probs_turned, 1)

            def values(k):
                g, h, t = HEAD_UNITS[2 * k]
                pe.wait_ge(pT_ready, 2 * k + 2)
                bank = 6 + k % 2 if k < A_UNITS // 2 else 7
                if k == 0:
                    pe.wait_ge(qkT_ready, 3 * TILES + 1)
                    pe.wait_ge(qkT_act, 3 * TILES + 1)
                if k >= 2:
                    pe.wait_ge(attn_ready, k - 1 if k < A_UNITS // 2 else k)
                blocks = value_blocks(g, t)
                for n, b in enumerate(blocks):
                    for hh in (0, 1):
                        kv = (h + hh) // 4
                        if b == -1:
                            v = cache[:, (2 * g + 1) * P + kv * DH:(2 * g + 1) * P + (kv + 1) * DH]
                        elif b == 4:
                            v = kv_ctx[:, 256 * g + P + kv * DH:256 * g + P + (kv + 1) * DH]
                        else:
                            v = vl[:, b, g * P + kv * DH:g * P + (kv + 1) * DH]
                        last = pe.matmul(ps[64 * hh:64 * hh + 64, bank, 0:P], v,
                                         pT[:, k % 2, hh, n * P:(n + 1) * P], start=(n == 0),
                                         stop=(n == len(blocks) - 1))
                last.then_inc(pv_done, 1)

            n_units = len(HEAD_UNITS)

            def cast_gate(n, r):
                cond, half = divmod(r, 2)
                k = 4 * n + r
                if n == 0:
                    bank = 2 + r % 2
                    if r == 0:
                        pe.wait_ge(gate_gained, 1)
                        pe.wait_ge(exp_done, A_UNITS)
                else:
                    bank = 4 + r % 2
                    if r == 0:
                        pe.wait_ge(gate_gained, 2)
                        pe.wait_ge(aff_ready, 1)
                        pe.wait_ge(h2_ready, 2 * TILES)
                if r >= 2:
                    pe.wait_ge(gate_ready, k - 1)
                for q in (0, 1):
                    row = 32 * (2 * half + q) + cond
                    last = pe.matmul(ps[:, bank, q * QUART:(q + 1) * QUART],
                                     ident[:, row:row + 1].to_broadcast([P, P]), modq[:, (2, 5)[n], :],
                                     start=True, stop=True)
                last.then_inc(gate_cast, 1)

            def project_out(o, first, last_one):
                t = OUT_ORDER[o]
                for i in range(first, last_one):
                    n, c = divmod(i, KC)
                    if i == 0 and o == 0:
                        landed(wout_units[0])
                        landed(wout_units[1])
                        pe.wait_ge(gate_ready, 4)
                    elif i == 0 and o == 1:
                        pe.wait_ge(pT_ready, A_UNITS)
                        pe.wait_ge(attn_ready, A_UNITS // 2)
                    elif i == 0:
                        pe.wait_ge(h2_ready, 2 * o - 2)
                    if n == 0 and c >= 4:
                        pe.wait_ge(attn_ready, A_UNITS // 2 + PAIRS * o + c - 3)
                    last = pe.matmul(out_at(o)[:, n, :], attnT[:, c, t * P:(t + 1) * P],
                                     unit_at(wout_units[c // 4], 4)[:, c % 4, n * 512:(n + 1) * 512],
                                     start=(c == 0), stop=(c == KC - 1))
                    if i == 2 * KC - 1:
                        last.then_inc(wout_done, 1)

            def turn_x1(o, half):
                t = OUT_ORDER[o]
                pe.wait_ge(xn_ready, o + 1)
                for c in range(4):
                    last = pe.transpose(out_at(o)[:, half, c * P:(c + 1) * P],
                                        xn[:, t, (4 * half + c) * P:(4 * half + c + 1) * P], ident[:, :])
                last.then_inc(xn_turned, 1)

            def route_logits(o):
                t = OUT_ORDER[o]
                pe.wait_ge(h2_ready, 2 * o + 2)
                if o == 0:
                    pe.wait_ge(pT_ready, n_units)
                    pe.wait_ge(attn_ready, n_units // 2)
                for c in range(KC):
                    last = pe.matmul(ps[:, 4 if t else 7, t * E:(t + 1) * E], h2T[:, c, t * P:(t + 1) * P],
                                     wr[:, c * E:(c + 1) * E], start=(c == 0), stop=(c == KC - 1))
                last.then_inc(router_done, 1)

            scores(0)
            scores(1)
            turn_qk(3 * TILES)
            for u in range(n_units):
                if u:
                    turn_probs(u - 1)
                if u + 2 < n_units:
                    scores(u + 2)
                if u % 2 and u >= 3:
                    values((u - 3) // 2)
                o, j = divmod(u - A_UNITS, HEADS)
                if o == 0 and j < 4:
                    cast_gate(0, j)
                if o >= 1:
                    project_out(o - 1, 2 * j, 2 * j + 2)
                if o >= 2 and j == 4:
                    turn_x1(o - 2, 0)
                    turn_x1(o - 2, 1)
            turn_probs(n_units - 1)
            values(n_units // 2 - 1)
            project_out(4, 0, KC)
            for o in range(3):
                route_logits(o)
            turn_x1(3, 0)
            project_out(4, KC, KC + 4)
            turn_x1(3, 1)
            project_out(4, KC + 4, 2 * KC)
            route_logits(3)

            pe.wait_ge(aff_ready, 1)
            for t in range(1, TILES):
                last = pe.transpose(ps[0:E, 0, (t - 1) * P:t * P], expl[:, t, :], ident[:, :])
            last.then_inc(aff_turned, 1)
            turn_x1(4, 0)
            turn_x1(4, 1)
            route_logits(4)
            pe.wait_ge(aff_ready, 2)
            pe.transpose(ps[0:E, 1, 0:P], expl[:, 0, :], ident[:, :]).then_inc(aff_turned, 1)
            for r in range(4):
                cast_gate(1, r)
            pe.wait_ge(lists_ready, 1)
            for a in range(4):
                last = pe.transpose(ps[:, 7, a * E:(a + 1) * E], lists[:, a, :], ident[0:E, 0:E])
            last.then_inc(lists_turned, 1)

            G, U, GC, Y, YC, TX, TC, TA = (ps[:, b, :] for b in range(8))

            def turn_rows(n):
                pe.wait_ge(gathered_l, n * 16 + 16)
                pe.wait_ge(gathered_c, n * 16 + 16)
                for j in range(4):
                    pe.transpose(TX[:, j * P:(j + 1) * P], xg_l[:, j * P:(j + 1) * P], ident[:, :])
                for j in range(2):
                    last = pe.transpose(TC[:, j * P:(j + 1) * P], xg_c[:, j * P:(j + 1) * P], ident[:, :])
                last.then_inc(xe_turned, 1)

            def weight_in(s, e):
                pe.wait_ge(slot_in[s], e * 16 + 16 * (LOADS[s] + 1))

            def gate_in(half, pair, odd):
                if odd:
                    pe.wait_ge(slot_in[SLOTS + half], pair * 16 + 16)
                else:
                    pe.wait_ge(slot_in[half], pair * 16 + 16 * (LOADS[half] + 1))

            def product_l(s, o, x):
                w = ring_slot(s).rearrange("p (c n) -> p c n", c=4)
                hf = s % 2
                for j in range(4):
                    for n in (0, 1):
                        last = pe.matmul(o[64 * n:64 * n + 64, :], x[:, j, hf, :], w[:, j, n * HALF:(n + 1) * HALF],
                                         start=(hf == 0 and j == 0), stop=(hf == 1 and j == 3))
                return last

            def product_c(s, o, x):
                w = ring_slot(s).rearrange("p (c n) -> p c n", c=4)
                hf = s % 2
                for j in range(4):
                    c = 4 * hf + j
                    for q in range(4):
                        last = pe.matmul(o[32 * q:32 * q + 32, :], x[:, c % 2, c // 2, :],
                                         w[:, j, q * QUART:(q + 1) * QUART], start=(c == 0), stop=(c == KC - 1))
                return last

            pe.wait_ge(rows_ready, 1)
            pe.wait_ge(gate_ready, 8)
            turn_rows(0)

            def gate_product(pair, odd, half):
                gate_in(half, pair, odd)
                s = SLOTS * odd + half
                product_c(s, GC[:, 0:QUART], xT_c[odd])
                product_l(s, G, xT_l[odd]).then_inc((gate_a, gate_b)[half], 1)

            def expert(e, odd, following):
                weight_in(2, e)
                pe.wait_ge(silu_done, e * 2 + 2)
                product_c(2, GC[:, QUART:], xT_c[odd])
                product_l(2, U, xT_l[odd]).then_inc(up_a, 1)
                turn_rows(e + 1)
                weight_in(3, e)
                product_c(3, GC[:, QUART:], xT_c[odd]).then_inc(up_c, 1)
                product_l(3, U, xT_l[odd]).then_inc(up_b, 1)
                pe.wait_ge(act_c_ready, e + 1)
                if following:
                    pe.wait_ge(xe_ready, e + 2)
                    gate_product(*following, 0)
                for j in range(2):
                    last = pe.transpose(TC[:, QUART + j * P:QUART + (j + 1) * P], a_c[:, j * P:(j + 1) * P],
                                        ident[:, :])
                last.then_inc(act_c_turned, 1)
                pe.wait_ge(act_l_ready, e + 1)
                for j in range(4):
                    last = pe.transpose(TA[:, j * P:(j + 1) * P], a_l[:, j * P:(j + 1) * P], ident[:, :])
                last.then_inc(act_l_turned, 1)
                if following:
                    gate_product(*following, 1)
                pe.wait_ge(y_ready, e + 1)
                weight_in(4, e)
                pe.wait_ge(actT_c_ready, e + 1)
                product_c(4, YC[:, 0:QUART], aT_c)
                pe.wait_ge(actT_l_ready, e + 1)
                product_l(4, Y, aT_l).then_inc(down_a, 1)
                weight_in(5, e)
                product_c(5, YC[:, 0:QUART], aT_c)
                product_l(5, Y, aT_l).then_inc(down_b, 1)

            pe.wait_ge(xe_ready, 1)
            gate_product(0, 0, 0)
            gate_product(0, 0, 1)
            with pe.Fori(0, E // 2 - 1) as pair:
                expert(pair * 2, 0, (pair, 1))
                expert(pair * 2 + 1, 1, (pair + 1, 0))
            expert(E - 2, 0, (E // 2 - 1, 1))
            expert(E - 1, 1, None)

        @block.scalar
        def _(act):
            n_loads = [0]

            def load(dst, src, **how):
                act.dma_start(dst, src, **how).then_inc(consts_in, 16)
                n_loads[0] += 1

            act.dma_start(ident[:, :], A["identity"]).then_inc(early_in, 16)
            act.dma_start(gpre[:, :], A["g_pre_columns"]).then_inc(early_in, 16)
            b_rows = A["b_ada"][0].rearrange("(m q n) -> q m n", m=N_MOD, q=4)
            for q in range(4):
                act.dma_start(modq[32 * q:32 * q + 32, :, :], b_rows[q:q + 1].to_broadcast([32, N_MOD, QUART]))\
                    .then_inc(early_in, 16)
            load(cache[:, 0:P], A["cache_a_k"][0, 0].rearrange("t h d -> t (h d)"))
            load(cache[:, P:2 * P], A["cache_a_v"][0, 0].rearrange("t h d -> t (h d)"))
            load(cache[:, 2 * P:3 * P], A["cache_b_k"][0, 0].rearrange("t h d -> t (h d)"))
            load(cache[:, 3 * P:4 * P], A["cache_b_v"][0, 0].rearrange("t h d -> t (h d)"))
            load(gqk[:, 0:DH], A["g_qa"].to_broadcast([P, DH]))
            load(gqk[:, DH:2 * DH], A["g_ka"].to_broadcast([P, DH]))
            load(rope[:, :, :, :].rearrange("p a t d -> p (a t) d"),
                 A["rope_tables"].rearrange("a (t p) d -> p (a t) d", p=P))
            load(sink[:, :], A["sink_b"].to_broadcast([P, HEADS]))
            load(wr[:, :].rearrange("p (c e) -> p c e", e=E), A["w_router"][0].rearrange("(c p) e -> p c e", p=P))
            for n, name in enumerate(("g_post_attn", "g_post_ffn")):
                rows = A[name].rearrange("a (q n) -> q a n", q=4)
                for q in range(4):
                    load(gpost[32 * q:32 * q + 32, n * QUART:(n + 1) * QUART], rows[q].to_broadcast([32, QUART]))
            assert n_loads[0] == N_CONSTS

            act.wait_ge(cond_in, 16)
            act.wait_ge(silu_cleared, 1)
            act.activation(silu[:, :, 0:2], cvec[:, :].rearrange("p (c k) -> p k c", c=2), ACT.Silu).then_inc(silu_ready, 1)
            for t in range(TILES):
                act.wait_ge(x_loaded[t], 16)
                act.activation(xn[:, t, :], x_in[:, t, :], ACT.Square, accum_out=ss1[:, t:t + 1]).then_inc(x_squared, 1)
            for t in range(TILES):
                act.wait_ge(x_rstd, t + 1)
                act.activation(x_in[:, t, :], x_in[:, t, :], ACT.Identity, scale=rs1[:, t:t + 1]).then_inc(x_normed, 1)

            act.wait_ge(modcol_ready, 2)
            for c in range(KC):
                act.wait_ge(xt_done, c + 1)
                act.activation(hT[:, c, 0:P], ps[:, 5 + c % 2, 0:P], ACT.Identity, bias=cmod[:, 0, 0, c:c + 1],
                               scale=cmod[:, 1, 0, c:c + 1]).then_inc(htc_ready, 1)

            def high_part(k):
                if k == 0:
                    act.wait_ge(consts_in, 16 * N_CONSTS)
                else:
                    act.wait_ge(rot_ready, k)
                if k >= 2:
                    act.wait_ge(qk_turned, k - 1)
                for src, dst in part_sources(k):
                    last = act.activation(dst[:, 0].bitcast(F32R), src, ACT.Copy)
                last.then_inc(high_ready, 1)

            def first_half_out(k):
                act.wait_ge(qk_turned, k + 1)
                bank = ps[:, (5 if k % 2 else 2), :].rearrange("p (b n) -> p b n", b=4)
                s, t = divmod(k - 1, TILES)
                if k == 0 or s == 0:
                    at = 0 if k == 0 else (TOK if t == 0 else t * P)
                    dst = kT[0][:, :, at:at + P]
                else:
                    if k == TILES + 1:
                        act.wait_ge(added_l, 16)
                        act.wait_ge(added_c, 16)
                        act.wait_ge(pad_cleared, 16)
                    dst = qT[s - 1][:, 0:4, t * P:(t + 1) * P]
                act.activation(dst, bank, ACT.Copy).then_inc(qkT_act, 1)

            for i in range(3 * TILES):
                s, t = divmod(i, TILES)
                act.wait_ge(proj_done, i + 1)
                if s == 0 and t == 0:
                    dst = kv_ctx[:, :]
                else:
                    dst = nat[:, i % 2, :]
                    if i >= 2:
                        act.wait_ge(rot_ready, i - 1)
                if s < 2:
                    n = P if s == 0 else 512
                    if i:
                        act.wait_ge(head_mean, i)
                    act.activation(sq[:, 0:n], ps[:, i % 2, 0:n], ACT.Square).then_inc(sq_ready, 1)
                act.activation(dst, ps[:, i % 2, :], ACT.Copy).then_inc(nat_ready, 1)
                high_part(i)
                if i >= 1:
                    first_half_out(i - 1)
            first_half_out(3 * TILES - 1)
            high_part(3 * TILES)

            act.wait_ge(rot_ready, 1)
            for n, first in enumerate((0, P, 2 * P, 3 * P)):
                act.dma_start(out[2 + n][0, 0].rearrange("t h d -> t (h d)"), kv_ctx[:, first:first + P]).then_inc(stored, 16)

            n_units = len(HEAD_UNITS)

            def exponentials(u):
                g, h, t = HEAD_UNITS[u]
                n = key_count(g, t)
                b = u % 2
                act.wait_ge(negmax_ready, u + 1)
                if u >= 3:
                    act.wait_ge(probs_turned, u - 2)
                if g:
                    act.activation(esink[:, b:b + 1], sink[:, h:h + 1], ACT.Exp, bias=negm[:, b:b + 1]).then_inc(sink_exp, 1)
                act.activation(probs[:, u % 3, 0:n], scores_at(u)[:, 0:n], ACT.Exp, bias=negm[:, b:b + 1],
                               scale=DH ** -0.5, accum_out=den[:, b:b + 1]).then_inc(exp_done, 1)

            def copy_gate(n, r):
                cond, half = divmod(r, 2)
                act.wait_ge(gate_cast, 4 * n + r + 1)
                bank = (4 + r % 2) if n else (2 + r % 2)
                act.activation(gate_rows[:, cond, half * HALF:(half + 1) * HALF], ps[:, bank, :],
                               ACT.Copy).then_inc(gate_ready, 1)

            def square_out(o):
                t = OUT_ORDER[o]
                act.wait_ge(wout_done, o + 1)
                act.activation(xn[:, t, :].rearrange("p (a n) -> p a n", a=2), out_at(o), ACT.Square,
                               accum_out=sso[:, t:t + 1]).then_inc(o_squared, 1)

            def square_x1(o):
                t = OUT_ORDER[o]
                act.wait_ge(x1_ready, o + 1)
                act.activation(xn[:, t, :], xr[:, t, :], ACT.Square, accum_out=ss2[:, t:t + 1]).then_inc(x1_squared, 1)

            def normalise_x1(o):
                t = OUT_ORDER[o]
                act.wait_ge(x1_rstd, o + 1)
                act.activation(xn[:, t, :], xr[:, t, :], ACT.Identity, scale=rs2[:, t:t + 1]).then_inc(xn_ready, 1)

            def store_rows(o):
                t = OUT_ORDER[o]
                act.wait_ge(xn_ready, o + 1)
                if t == 0:
                    act.dma_start(rows_c[0:4 * CTX].rearrange("(p q) n -> p (q n)", q=4), xn[:, 0, :]).then_inc(rows_stored, 16)
                else:
                    act.dma_start(rows_l[2 * (t - 1) * P:2 * t * P].rearrange("(p q) n -> p (q n)", q=2),
                                  xn[:, t, :]).then_inc(rows_stored, 16)

            def copy_pT(u):
                g, h, t = HEAD_UNITS[u]
                act.wait_ge(probs_turned, u + 1)
                k = u // 2
                if k >= 2:
                    act.wait_ge(pv_done, k - 1)
                n = key_count(g, t)
                act.activation(pT[:, k % 2, u % 2, 0:n], two[2][:, 0:n], ACT.Copy).then_inc(pT_ready, 1)

            exponentials(0)
            for u in range(n_units):
                if u:
                    copy_pT(u - 1)
                if u + 1 < n_units:
                    exponentials(u + 1)
                if u == 0:
                    first_half_out(3 * TILES)
                o, j = divmod(u - A_UNITS, HEADS)
                if o >= 2 and j in (0, 2, 3, 4):
                    {0: square_out, 2: square_x1, 3: normalise_x1, 4: store_rows}[j](o - 2)
                if o == 0 and j < 4:
                    copy_gate(0, j)
            copy_pT(n_units - 1)
            for step in (square_out, square_x1, normalise_x1, store_rows):
                step(3)
            square_out(4)
            act.wait_ge(logits_ready, 1)
            act.activation(expl[:, 1:, :], logit[:, 1:, :], ACT.Exp).then_inc(logits_exp, 1)
            square_x1(4)
            normalise_x1(4)
            store_rows(4)
            for half in (0, 1):
                act.wait_ge(xn_turned, 2 * TILES - 1 + half)
                for c in range(4):
                    k = 4 * half + c
                    last = act.activation(h2T[:, k, 0:P], out_at(4)[:, half, c * P:(c + 1) * P], ACT.Identity,
                                          bias=cmod[:, 2, 0, k:k + 1], scale=cmod[:, 3, 0, k:k + 1])
                last.then_inc(h2_ready, 1)
            act.wait_ge(logits_ready, 2)
            act.activation(expl[:, 0, :], logit[:, 0, :], ACT.Exp).then_inc(logits_exp, 1)
            for r in range(4):
                copy_gate(1, r)

            def silu_gate(e):
                act.wait_ge(gate_b, e + 1)
                act.activation(s_c, ps[:, 2, 0:QUART], ACT.Silu).then_inc(silu_done, 1)
                act.activation(s_l, ps[:, 0, :], ACT.Silu).then_inc(silu_done, 1)

            def copy_turned(e):
                act.wait_ge(act_c_turned, e + 1)
                act.activation(aT_c.rearrange("p j q s -> p (j q s)"), ps[:, 6, QUART:], ACT.Copy).then_inc(actT_c_ready, 1)
                act.wait_ge(act_l_turned, e + 1)
                act.activation(aT_l.rearrange("p j h s -> p (j h s)"), ps[:, 7, :], ACT.Copy).then_inc(actT_l_ready, 1)

            silu_gate(0)
            with act.Fori(0, E - 1) as e:
                copy_turned(e)
                silu_gate(e + 1)
            copy_turned(E - 1)

            for t in range(TILES):
                act.wait_ge(sum_in[t], 16)
                act.activation(squares[:, t, :], total[:, t, :], ACT.Square,
                               accum_out=ssf[:, t:t + 1]).then_inc(f_squared, 1)
            for t in range(TILES):
                act.wait_ge(f_ready, t + 1)
                dst = out[0][0] if t == 0 else out[1][0, (t - 1) * P:t * P]
                act.dma_start(dst, total[:, t, :]).then_inc(stored, 16)
            act.wait_ge(stored, 16 * (4 + TILES))

        @block.vector
        def _(dve):
            chain = [0]

            def link(ins):
                ins.then_inc(dve_step, 1)
                chain[0] += 1
                dve.wait_ge(dve_step, chain[0])

            dve.memset(mhalf[:, :], -0.5).then_inc(mhalf_set, 1)
            dve.memset(silu.rearrange("p c m -> p (c m)"), 0.0).then_inc(silu_cleared, 1)
            for t in range(TILES):
                dve.wait_ge(x_squared, t + 1)
                dve.tensor_scalar(ms1[:, t:t + 1], ss1[:, t:t + 1], 1.0 / D, EPS, ALU.mult, ALU.add).then_inc(x_mean, 1)

            dve.wait_ge(early_in, 16 * N_EARLY)
            cols = ps[:, 7, 0:2 * P].rearrange("p (j q r) -> p q j r", j=2, q=4)

            def columns(m):
                n = COLS[m]
                dve.wait_ge(modcol_done, n + 1)
                for cond in (0, 1):
                    dst = cmod[:, n, cond, :].rearrange("p (q j) -> p q j", j=2)
                    if n % 2 == 0:
                        last = dve.tensor_copy(dst, cols[:, :, :, cond])
                    else:
                        g = gpre[:, (n // 2) * KC:(n // 2 + 1) * KC].rearrange("p (q j) -> p q j", j=2)
                        last = dve.scalar_tensor_tensor(dst, cols[:, :, :, cond], 1.0, g, ALU.add, ALU.mult)
                last.then_inc(modcol_ready, 1)

            dve.wait_ge(ada_done, 1)
            dve.tensor_tensor(modq[:, 0, :], ps[:, 4, 0:QUART], modq[:, 0, :], ALU.add).then_inc(mod_ready, 1)
            columns(0)
            dve.wait_ge(ada_done, 2)
            dve.tensor_tensor(modq[:, 1, :], ps[:, 4, 0:QUART], modq[:, 1, :], ALU.add).then_inc(mod_ready, 1)
            columns(1)
            dve.wait_ge(modcol_ready, 2)
            for c in range(KC):
                dve.wait_ge(xt_done, c + 1)
                dve.tensor_scalar(hT[:, c, P:TOK], ps[:, 2 + c % 2, :], cmod[:, 1, 1, c:c + 1], cmod[:, 0, 1, c:c + 1],
                                  ALU.mult, ALU.add).then_inc(ht_ready, 1)

            dve.wait_ge(consts_in, 16 * N_CONSTS)
            link(dve.tensor_scalar(nsink[:, :], sink[:, :], -1.0, None, ALU.mult))
            gq = gqk[:, 0:DH]
            gq_swap = gq.rearrange("p (a b d) -> p a b d", a=2, b=2)
            for t in range(LT):
                dve.tensor_tensor(ropeq[:, 0, t, :], rope[:, 0, t, :], gq, ALU.mult)
                for b in (0, 1):
                    last = dve.tensor_tensor(ropeq[:, 1, t, :].rearrange("p (a b d) -> p a b d", a=2, b=2)[:, :, b, :],
                                             rope[:, 1, t, :].rearrange("p (a b d) -> p a b d", a=2, b=2)[:, :, b, :],
                                             gq_swap[:, :, 1 - b, :], ALU.mult)
            link(last)

            def rotate(dst, src, heads, tables, t):
                n = heads * DH
                direct = rot2[:, 0:n].rearrange("p (h d) -> p h d", d=DH)
                crossed = rot3[:, 0:n].rearrange("p (h d) -> p h d", d=DH)
                by_pair = "p (h a b d) -> p h a b d"
                cos = tables[:, 0, t, :].unsqueeze(1).to_broadcast([P, heads, DH])
                dve.tensor_tensor(direct, src.rearrange("p (h d) -> p h d", d=DH), cos, ALU.mult)
                for b in (0, 1):
                    sin = tables[:, 1, t, :].rearrange("p (a b d) -> p a b d", a=2, b=2)[:, :, b, :]
                    last = dve.tensor_tensor(rot3[:, 0:n].rearrange(by_pair, a=2, b=2, d=16)[:, :, :, b, :],
                                             src.rearrange(by_pair, a=2, b=2, d=16)[:, :, :, 1 - b, :],
                                             sin.unsqueeze(1).to_broadcast([P, heads, 2, 16]), ALU.mult)
                link(last)
                return dve.tensor_tensor(dst, direct, crossed, ALU.add)

            def low_part(k):
                dve.wait_ge(high_ready, k + 1)
                for src, dst in part_sources(k):
                    last = dve.tensor_tensor(dst[:, 1].bitcast(F32R), src, dst[:, 0], ALU.subtract)
                last.then_inc(split_ready, 1)

            def qk_out(k):
                dve.wait_ge(qk_turned, k + 1)
                bank = ps[:, (6 if k % 2 else 3), :].rearrange("p (b n) -> p b n", b=4)
                s, t = divmod(k - 1, TILES)
                if k == 0 or s == 0:
                    at = 0 if k == 0 else (TOK if t == 0 else t * P)
                    dst = kT[1][:, :, at:at + P]
                else:
                    if k == TILES + 1:
                        dve.wait_ge(added_l, 16)
                        dve.wait_ge(added_c, 16)
                        dve.wait_ge(pad_cleared, 16)
                    dst = qT[s - 1][:, 4:8, t * P:(t + 1) * P]
                dve.tensor_copy(dst, bank).then_inc(qkT_ready, 1)

            for i in range(3 * TILES):
                s, t = divmod(i, TILES)
                if i - 1 in ADA_AFTER:
                    m = ADA_AFTER[i - 1]
                    dve.wait_ge(ada_done, m + 1)
                    dve.tensor_tensor(modq[:, m, :], ps[:, 4, 0:QUART], modq[:, m, :], ALU.add).then_inc(mod_ready, 1)
                if i - 3 in ADA_AFTER and ADA_AFTER[i - 3] in COLS:
                    columns(ADA_AFTER[i - 3])
                src = kv_ctx[:, :] if i == 0 else nat[:, i % 2, :]
                heads = 2 if s == 0 else HEADS
                if s < 2:
                    dve.wait_ge(sq_ready, i + 1)
                    link(dve.tensor_reduce(ssh[:, 0:heads], sq[:, 0:heads * DH].rearrange("p (h d) -> p h d", d=DH),
                                           AX.X, ALU.add))
                    dve.tensor_scalar(msh[:, 0:heads], ssh[:, 0:heads], 1.0 / DH, EPS, ALU.mult, ALU.add)\
                        .then_inc(head_mean, 1)
                low_part(i)
                if i >= 1:
                    qk_out(i - 1)
                dve.wait_ge(nat_ready, i + 1)
                n3 = src[:, 0:heads * DH].rearrange("p (h d) -> p h d", d=DH)
                if s < 2:
                    dve.wait_ge(head_rstd, i + 1)
                    link(dve.tensor_tensor(n3, n3, rsh[:, 0:heads].unsqueeze(2).to_broadcast([P, heads, DH]), ALU.mult))
                if s == 0:
                    gained = dve.tensor_tensor(n3, n3, gqk[:, DH:2 * DH].unsqueeze(1).to_broadcast([P, heads, DH]),
                                               ALU.mult)
                    if t == 0:
                        gained.then_inc(rot_ready, 1)
                        continue
                    link(gained)
                if i >= 2:
                    dve.wait_ge(qk_turned, i)
                if i >= 1:
                    dve.wait_ge(rot_ready, i)
                if s == 0:
                    link(rotate(rot[:, i % 2, 0:P].rearrange("p (h d) -> p h d", d=DH), src[:, 0:P], 2, rope, t - 1))
                    link(dve.tensor_copy(vl[:, t - 1, 0:P], src[:, P:2 * P]))
                    link(rotate(rot[:, i % 2, P:2 * P].rearrange("p (h d) -> p h d", d=DH), src[:, 2 * P:3 * P], 2,
                                rope, t - 1))
                    dve.tensor_copy(vl[:, t - 1, P:2 * P], src[:, 3 * P:4 * P]).then_inc(rot_ready, 1)
                else:
                    dst = rot[:, i % 2, :].rearrange("p (h d) -> p h d", d=DH)
                    if t:
                        rotate(dst, src, HEADS, ropeq if s == 1 else rope, t - 1).then_inc(rot_ready, 1)
                    elif s == 1:
                        dve.tensor_tensor(dst, n3, gq.unsqueeze(1).to_broadcast([P, HEADS, DH]),
                                          ALU.mult).then_inc(rot_ready, 1)
                    else:
                        dve.tensor_copy(dst, n3).then_inc(rot_ready, 1)
            qk_out(3 * TILES - 1)

            n_units = len(HEAD_UNITS)
            n_sink = [0]

            def maxima(u):
                g, h, t = HEAD_UNITS[u]
                n, b = key_count(g, t), u % 2
                dve.wait_ge(scores_done, u + 1)
                if g and u == A_UNITS:
                    dve.wait_ge(masks_in, 16)
                if g and t:
                    lo, hi = max(0, t - 2), min(LT - 1, t)
                    before, after = lo < t - 1, hi > t - 1
                    if before and after:
                        v = scores_at(u)[:, 0:512].rearrange("p (k n) -> p k n", k=4)[:, 1:4:2, :]
                        link(dve.tensor_tensor(v, v, masks, ALU.add))
                    else:
                        at, m = (P, 0) if before else (n - P, 1)
                        link(dve.tensor_tensor(scores_at(u)[:, at:at + P], scores_at(u)[:, at:at + P], masks[:, m, :], ALU.add))
                link(dve.tensor_reduce(mx[:, b:b + 1], scores_at(u)[:, 0:n], AX.X, ALU.max))
                if g:
                    dve.tensor_scalar(negm[:, b:b + 1], mx[:, b:b + 1], -DH ** -0.5, nsink[:, h:h + 1], ALU.mult,
                                      ALU.min).then_inc(negmax_ready, 1)
                else:
                    dve.tensor_scalar(negm[:, b:b + 1], mx[:, b:b + 1], -DH ** -0.5, None, ALU.mult)\
                        .then_inc(negmax_ready, 1)

            def attn_out(k):
                g, h, t = HEAD_UNITS[2 * k]
                dve.wait_ge(pv_done, k + 1)
                dve.tensor_copy(attnT[:, 4 * g + h // 2, t * P:(t + 1) * P],
                                ps[:, 6 + k % 2 if k < A_UNITS // 2 else 7, 0:P]).then_inc(attn_ready, 1)

            def out_mean(o):
                t = OUT_ORDER[o]
                dve.wait_ge(o_squared, o + 1)
                dve.tensor_scalar(mso[:, t:t + 1], sso[:, t:t + 1], 1.0 / D, EPS, ALU.mult, ALU.add).then_inc(o_mean, 1)

            def gate_out(o):
                t = OUT_ORDER[o]
                dve.wait_ge(o_rstd, o + 1)
                if o == 0:
                    dve.wait_ge(gate_ready, 4)
                dve.scalar_tensor_tensor(xn[:, t, :].rearrange("p (a n) -> p a n", a=2), out_at(o),
                                         rso[:, t:t + 1],
                                         gate_rows[:, min(t, 1), :].rearrange("p (a n) -> p a n", a=2),
                                         ALU.mult, ALU.mult).then_inc(o_scaled, 1)

            def add_out(o):
                t = OUT_ORDER[o]
                if o == 0:
                    dve.wait_ge(x_again, 16 * TILES)
                dve.wait_ge(o_scaled, o + 1)
                dve.tensor_tensor(xr[:, t, :], xr[:, t, :], xn[:, t, :], ALU.add).then_inc(x1_ready, 1)

            def x1_mean_of(o):
                t = OUT_ORDER[o]
                dve.wait_ge(x1_squared, o + 1)
                dve.tensor_scalar(ms2[:, t:t + 1], ss2[:, t:t + 1], 1.0 / D, EPS, ALU.mult, ALU.add).then_inc(x1_mean, 1)

            def modulate_x1(o, half):
                t = OUT_ORDER[o]
                cond, tt = min(t, 1), slice(t * P, (t + 1) * P)
                dve.wait_ge(xn_turned, 2 * o + half + 1)
                v = out_at(o)[:, half, :].rearrange("p (c n) -> p c n", c=4)
                scale, shift = (cmod[:, m, cond, 4 * half:4 * half + 4].unsqueeze(2).to_broadcast([P, 4, P]) for m in (3, 2))
                link(dve.tensor_tensor(v, v, scale, ALU.mult))
                dve.tensor_tensor(h2T[:, 4 * half:4 * half + 4, tt], v, shift, ALU.add).then_inc(h2_ready, 1)

            maxima(0)
            low_part(3 * TILES)
            for u in range(n_units):
                g, h, t = HEAD_UNITS[u]
                n, b = key_count(g, t), u % 2
                if u + 1 < n_units:
                    maxima(u + 1)
                o, j = divmod(u - A_UNITS, HEADS)
                if o >= 2 and j == 1:
                    gate_out(o - 2)
                dve.wait_ge(exp_done, u + 1)
                if g:
                    n_sink[0] += 1
                    dve.wait_ge(sink_exp, n_sink[0])
                    link(dve.tensor_tensor(den[:, b:b + 1], den[:, b:b + 1], esink[:, b:b + 1], ALU.add))
                link(dve.reciprocal(rden[:, b:b + 1], den[:, b:b + 1]))
                dve.tensor_scalar(probs[:, u % 3, 0:n], probs[:, u % 3, 0:n], rden[:, b:b + 1], None, ALU.mult)\
                    .then_inc(probs_ready, 1)
                if u == 0:
                    qk_out(3 * TILES)
                if u == 4:
                    dve.wait_ge(mod_ready, N_MOD)
                    dve.tensor_tensor(modq[:, 2, :], modq[:, 2, :], gpost[:, 0:QUART], ALU.mult).then_inc(gate_gained, 1)
                    dve.tensor_tensor(modq[:, 5, :], modq[:, 5, :], gpost[:, QUART:], ALU.mult).then_inc(gate_gained, 1)
                if u % 2 == 0 and u >= 4:
                    attn_out((u - 4) // 2)
                if o >= 2 and j == 0:
                    out_mean(o - 2)
                if o >= 2 and j == 1:
                    add_out(o - 2)
                if o >= 2 and j == 2:
                    x1_mean_of(o - 2)
                if o >= 2 and j in (5, 7):
                    modulate_x1(o - 2, (j - 5) // 2)
            attn_out(n_units // 2 - 2)
            attn_out(n_units // 2 - 1)
            out_mean(3)
            gate_out(3)
            add_out(3)
            x1_mean_of(3)
            modulate_x1(3, 0)
            modulate_x1(3, 1)

            def softmax(n, tiles, bank):
                k = tiles.stop - tiles.start
                lg = ps[:, bank, tiles.start * E:tiles.stop * E].rearrange("p (t e) -> p t e", t=k)
                wide = lambda v: v[:, tiles].unsqueeze(2).to_broadcast([P, k, E])
                link(dve.tensor_reduce(lmax[:, tiles], lg, AX.X, ALU.max))
                dve.tensor_tensor(logit[:, tiles, :], lg, wide(lmax), ALU.subtract).then_inc(logits_ready, 1)
                dve.wait_ge(logits_exp, n)
                link(dve.tensor_reduce(lsum[:, tiles], expl[:, tiles, :], AX.X, ALU.add))
                link(dve.reciprocal(lrec[:, tiles], lsum[:, tiles]))
                dve.tensor_tensor(expl[:, tiles, :], expl[:, tiles, :], wide(lrec), ALU.mult).then_inc(aff_ready, 1)

            def top_eight(vals, idx, tokens, r, cap):
                k = slice(8 * r, 8 * r + 8)
                here, left = affs[r % 2][:, tokens], affs[1 - r % 2][:, tokens]
                link(dve.max(vals[:, k], here))
                found = dve.max_index(idx[:, k], vals[:, k], here)
                if 8 * r + 8 < cap:
                    link(dve.match_replace(left, vals[:, k], here, -1.0))
                else:
                    link(found)

            dve.wait_ge(router_done, TILES - 1)
            softmax(1, slice(1, TILES), 4)
            dve.wait_ge(aff_turned, 1)
            link(dve.tensor_copy(affs[0][:, CTX:], ps[0:E, 0, :]))
            def context_softmax():
                dve.wait_ge(router_done, TILES)
                softmax(2, slice(0, 1), 7)

            among = {0: (lambda: gate_out(4), lambda: add_out(4)), 1: (lambda: x1_mean_of(4),), 5: (context_softmax,)}
            out_mean(4)
            for r in range(CAP_L // 8):
                top_eight(vals_l, idxu_l, slice(CTX, TOK), r, CAP_L)
                for step in among.get(r, ()):
                    step()
            dve.wait_ge(aff_turned, 2)
            link(dve.tensor_copy(affs[0][:, 0:CTX], ps[0:E, 1, 0:CTX]))
            for r in range(CAP_C // 8):
                top_eight(vals_c, idxu_c, slice(0, CTX), r, CAP_C)
            link(dve.tensor_copy(idxf_l, idxu_l))
            link(dve.tensor_copy(idxf_c, idxu_c))
            dve.wait_ge(pad_set, 3)
            for h in (0, 1):
                o = h * CAP_L
                dve.tensor_scalar(lists[:, 0, o:o + CAP_L], idxf_l, 2.0, float(h), ALU.mult, ALU.add)
                dve.tensor_copy(lists[:, 1, o:o + CAP_L], vals_l)
            for q in range(4):
                o = q * CPAD
                dve.tensor_scalar(lists[:, 2, o:o + CAP_C], idxf_c, 4.0, float(q), ALU.mult, ALU.add)
                last = dve.tensor_copy(lists[:, 3, o:o + CAP_C], vals_c)
            last.then_inc(lists_ready, 1)
            dve.wait_ge(lists_turned, 1)
            turned = ps[:, 7, 0:4 * E].rearrange("p (a e) -> p a e", a=4)
            dve.tensor_copy(row_l[:, 0:E], turned[:, 0, :])
            dve.tensor_copy(g_l, turned[:, 1, :]).then_inc(y_ready, 1)
            dve.tensor_copy(row_c[:, 0:E], turned[:, 2, :])
            dve.tensor_copy(g_c, turned[:, 3, :]).then_inc(rows_ready, 1)

            def modulate(n, odd):
                dve.wait_ge(xe_turned, n + 1)
                tx = ps[:, 5, :].rearrange("p (j h s) -> p j h s", j=4, h=2)
                tc = ps[:, 6, 0:QUART].rearrange("p (j q s) -> p j q s", j=2, q=4)
                by_l = [cmod[:, m, 1, :].rearrange("p (h j) -> p j h", h=2).unsqueeze(3).to_broadcast([P, 4, 2, CAP_L])
                        for m in (2, 3)]
                by_c = [cmod[:, m, 0, :].rearrange("p (q j) -> p j q", q=4).unsqueeze(3).to_broadcast([P, 2, 4, CPAD])
                        for m in (2, 3)]
                dve.tensor_tensor(xT_l[odd], tx, by_l[1], ALU.mult)
                dve.tensor_tensor(xT_c[odd], tc, by_c[1], ALU.mult).then_inc(xe_scaled, 1)
                dve.wait_ge(xe_scaled, n + 1)
                dve.tensor_tensor(xT_l[odd], xT_l[odd], by_l[0], ALU.add)
                dve.tensor_tensor(xT_c[odd], xT_c[odd], by_c[0], ALU.add).then_inc(xe_ready, 1)

            def activations(e):
                dve.wait_ge(up_c, e + 1)
                dve.wait_ge(silu_done, e * 2 + 2)
                dve.tensor_tensor(a_c, s_c, ps[:, 2, QUART:], ALU.mult).then_inc(act_c_ready, 1)
                dve.wait_ge(up_b, e + 1)
                dve.tensor_tensor(a_l, s_l, ps[:, 1, :], ALU.mult).then_inc(act_l_ready, 1)

            def weigh(e):
                dve.wait_ge(down_b, e + 1)
                dve.wait_ge(added_l, e * 16 + 16)
                dve.wait_ge(added_c, e * 16 + 16)
                dve.tensor_scalar(y_l, ps[:, 3, :], g_l[:, bass.ds(e, 1)], None, ALU.mult)
                dve.tensor_scalar(y_c, ps[:, 4, 0:QUART], g_c[:, bass.ds(e, 1)], None, ALU.mult).then_inc(y_ready, 1)

            modulate(0, 0)
            with dve.Fori(0, E // 2) as pair:
                for odd in (0, 1):
                    modulate(pair * 2 + odd + 1, 1 - odd)
                    activations(pair * 2 + odd)
                    weigh(pair * 2 + odd)

            def last_gated(t):
                dve.wait_ge(f_squared, t + 1)
                dve.tensor_scalar(msf[:, t:t + 1], ssf[:, t:t + 1], 1.0 / D, EPS, ALU.mult, ALU.add).then_inc(f_mean, 1)
                if t not in POOL_GATED:
                    dve.tensor_tensor(total[:, t, :], total[:, t, :], gate_rows[:, min(t, 1), :], ALU.mult).then_inc(f_gated, 1)

            def last_sum(t):
                dve.wait_ge(f_rstd, t + 1)
                if t in POOL_GATED:
                    dve.wait_ge(f_gated_pool, POOL_GATED.index(t) + 1)
                else:
                    dve.wait_ge(f_gated, sum(v not in POOL_GATED for v in range(t + 1)))
                dve.scalar_tensor_tensor(total[:, t, :], total[:, t, :], rsf[:, t:t + 1], xr[:, t, :],
                                         ALU.mult, ALU.add).then_inc(f_ready, 1)

            for t in range(TILES):
                last_gated(t)
                if t >= 2:
                    last_sum(t - 2)
            last_sum(TILES - 2)
            last_sum(TILES - 1)

        @block.gpsimd
        def _(pool):
            pool.memset(zeros, 0.0).then_inc(zeros_set, 1)
            pool.wait_ge(mhalf_set, 1)

            def root(dst, mean, n, ready, done, count):
                pool.wait_ge(ready, count)
                pool.tensor_tensor(dst, mean, mhalf[:, 0:n], ALU.pow).then_inc(done, 1)

            for t in range(TILES):
                root(rs1[:, t:t + 1], ms1[:, t:t + 1], 1, x_mean, x_rstd, t + 1)
            pool.wait_ge(proj_done, 1)
            pool.wait_ge(zeros_set, 1)
            pool.dma_start(sum_l.rearrange("(p a) (b n) -> p (a b) n", p=P, n=QUART),
                           zeros.unsqueeze(1).to_broadcast([P, 16, QUART])).then_inc(added_l, 16)
            pool.dma_start(sum_c.rearrange("(p a) n -> p a n", p=64),
                           zeros[0:64].unsqueeze(1).to_broadcast([64, CTX_ROWS // 64, QUART])).then_inc(added_c, 16)
            pool.dma_start(rows_c[4 * CTX:CTX_ROWS], zeros[0:CTX_ROWS - 4 * CTX]).then_inc(pad_cleared, 16)
            for i in range(2 * TILES):
                heads = 2 if i < TILES else HEADS
                root(rsh[:, 0:heads], msh[:, 0:heads], heads, head_mean, head_rstd, i + 1)
            for o, t in enumerate(OUT_ORDER):
                root(rso[:, t:t + 1], mso[:, t:t + 1], 1, o_mean, o_rstd, o + 1)
                root(rs2[:, t:t + 1], ms2[:, t:t + 1], 1, x1_mean, x1_rstd, o + 1)

            pool.wait_ge(scores_done, len(HEAD_UNITS))
            pool.iota(lists[:, 2, :].rearrange("e (q r) -> e q r", q=4)[:, :, CAP_C:], [[CPAD - CAP_C, 4], [1, CPAD - CAP_C]],
                      base=4 * CTX, channel_multiplier=0, allow_small_or_imprecise_dtypes=True).then_inc(pad_set, 1)
            pool.memset(lists[:, 3, :].rearrange("e (q r) -> e q r", q=4)[:, :, CAP_C:], 0.0).then_inc(pad_set, 1)
            pool.memset(kt[:, 1800:1840].bitcast(I32), 0).then_inc(pad_set, 1)

            def hold(pool):
                pool.tensor_tensor(held, mhalf[:, 0:1], mhalf[:, 1:2], ALU.add).then_inc(held_ops, 1)

            def gather(n):
                pool.tensor_copy(get_l, row_l[:, bass.ds(n, 1)])
                pool.tensor_copy(get_c, row_c[:, bass.ds(n, 1)]).then_inc(get_copied, 1)
                pool.wait_ge(get_copied, n + 1)
                hold(pool)
                pool.indirect_dma_start(xg_l, None, rows_l, bass.IndirectOffsetOnAxis(ap=get_l, axis=0))\
                    .then_inc(gathered_l, 16)
                pool.indirect_dma_start(xg_c, None, rows_c, bass.IndirectOffsetOnAxis(ap=get_c, axis=0))\
                    .then_inc(gathered_c, 16)

            pool.wait_ge(rows_ready, 1)
            pool.wait_ge(rows_stored, 16 * TILES)
            pool.wait_ge(pad_cleared, 16)
            gather(0)
            pool.wait_ge(xe_turned, 1)
            gather(1)
            with pool.Fori(0, E) as e:
                pool.wait_ge(xe_turned, e + 2)
                gather(e + 2)
                pool.wait_ge(added_l, e * 16 + 16)
                pool.wait_ge(added_c, e * 16 + 16)
                pool.tensor_copy(put_l, row_l[:, bass.ds(e, 1)])
                pool.tensor_copy(put_c, row_c[:, bass.ds(e, 1)]).then_inc(put_copied, 1)
                pool.wait_ge(put_copied, e + 1)
                pool.wait_ge(y_ready, e + 2)
                hold(pool)
                pool.indirect_dma_start(sum_l, bass.IndirectOffsetOnAxis(ap=put_l, axis=0), y_l, None,
                                        compute_op=ALU.add).then_inc(added_l, 16)
                pool.indirect_dma_start(sum_c, bass.IndirectOffsetOnAxis(ap=put_c, axis=0), y_c, None,
                                        compute_op=ALU.add).then_inc(added_c, 16)
            pool.wait_ge(added_l, 16 * (E + 1))
            pool.wait_ge(added_c, 16 * (E + 1))
            for t in range(TILES):
                root(rsf[:, t:t + 1], msf[:, t:t + 1], 1, f_mean, f_rstd, t + 1)
                if t in POOL_GATED:
                    pool.wait_ge(f_squared, t + 1)
                    pool.tensor_tensor(total[:, t, :], total[:, t, :], gate_rows[:, min(t, 1), :], ALU.mult)\
                        .then_inc(f_gated_pool, 1)


_INS = ["x_prompt", "x_sample", "cache_a_k", "cache_a_v", "cache_b_k", "cache_b_v", "w_ada", "b_ada",
        "w_in", "g_qa", "g_ka", "sink_b", "w_out", "g_post_attn", "w_router", "w_gate",
        "w_up", "w_down", "g_post_ffn"]
_OUTS = [(1, CTX, D), (1, LAT, D)] + [(1, 1, CTX, 2, DH)] * 4
GRID_W = 64
ROPE_THETA = 10000.0


def shape_constants():
    half = DH // 4
    freqs = (np.float32(ROPE_THETA) ** (-np.arange(half, dtype=np.float32) / np.float32(half))).astype(np.float32)
    pos = np.arange(LAT)
    tables = np.zeros((2, LAT, DH), np.float32)
    for a, where in enumerate((pos // GRID_W, pos % GRID_W)):
        ang = where.astype(np.float32)[:, None] * freqs[None, :]
        cos, sin = np.cos(ang).astype(np.float32), np.sin(ang).astype(np.float32)
        o = 2 * half * a
        tables[0, :, o:o + half], tables[0, :, o + half:o + 2 * half] = cos, cos
        tables[1, :, o:o + half], tables[1, :, o + half:o + 2 * half] = -sin, sin
    q, k = np.arange(P)[:, None], np.arange(P)[None, :]
    masks = np.zeros((2, P, P), np.float32)
    masks[0][k < q] = NEG
    masks[1][k > q] = NEG
    return {"identity": np.eye(P, dtype=np.float32), "rope_tables": tables, "window_masks": masks}


def column_layouts(inputs):
    c = [np.asarray(inputs["c_ctx"]).reshape(P, KC), np.asarray(inputs["c"]).reshape(P, KC)]
    g = [np.asarray(inputs[n]).reshape(KC, P).T for n in ("g_pre_attn", "g_pre_ffn")]
    return {"c_columns": np.ascontiguousarray(np.concatenate(c, axis=1)),
            "g_pre_columns": np.ascontiguousarray(np.concatenate(g, axis=1))}


def kernel(**inputs):
    import concourse.bacc as bacc
    from concourse.bass_utils import run_bass_kernel_spmd

    nc = bacc.Bacc("TRN2", target_bir_lowering=False, num_devices=1)
    arrays, handles = {}, {}
    given = {name: np.ascontiguousarray(inputs[name]) for name in _INS}
    for name, a in {**given, **column_layouts(inputs), **shape_constants()}.items():
        arrays[f"in_{name}"] = a
        handles[name] = nc.dram_tensor(f"in_{name}", a.shape, mybir.dt.from_np(a.dtype), kind="ExternalInput").ap()
    outs = [nc.dram_tensor(f"out_{i}", s, F32, kind="ExternalOutput").ap() for i, s in enumerate(_OUTS)]
    build(nc, handles, outs)
    r = run_bass_kernel_spmd(nc, [arrays], core_ids=[0])
    return tuple(r.results[0][f"out_{i}"] for i in range(len(_OUTS)))
```
